# Optimizing a Trainium2 kernel written in Bass

```python
import jax
import jax.numpy as jnp
from jax import lax
import numpy as np
import math
import jax, jax.numpy as jnp

D_MODEL = 2048
BATCH = 1
SEQ = 256
DEPTH = 1

GRID_W = 64
CTX_LEN = 256
EPS = 1e-6
CONV_DIM = D_MODEL // 2
CONV_WIDTH = 31
SGU_DIM = D_MODEL // 2
SGU_CHUNK = 128
SGU_GROUPS = SGU_DIM // 128
NA_HEAD_DIM = 64
NA_HEADS = (D_MODEL // 2) // NA_HEAD_DIM
NA_DIM = NA_HEADS * NA_HEAD_DIM
NA_KH = 8
NA_KW = 16
N_BRANCH = 3
D_FF = 4 * D_MODEL
Q_OFF = 2 * CONV_DIM + 2 * SGU_DIM
K_OFF = Q_OFF + NA_DIM
V_OFF = K_OFF + NA_DIM
G_OFF = V_OFF + NA_DIM
IN_DIM = G_OFF + N_BRANCH * D_MODEL
NEG_INF = -1e30


def rms_norm(x, g):
    xf = x.astype(jnp.float32)
    y = xf * lax.rsqrt(jnp.mean(xf * xf, axis=-1, keepdims=True) + EPS)
    return (y * g.astype(jnp.float32)).astype(x.dtype)

def layer_norm(x, g, b):
    xf = x.astype(jnp.float32)
    xc = xf - jnp.mean(xf, axis=-1, keepdims=True)
    var = jnp.mean(xc * xc, axis=-1, keepdims=True)
    return (xc * lax.rsqrt(var + EPS) * g.astype(jnp.float32) + b.astype(jnp.float32)).astype(x.dtype)

def modulate(h, shift, scale):
    return h * (1 + scale[:, None, :]) + shift[:, None, :]

def split_heads(t):
    return t.reshape(t.shape[0], t.shape[1], NA_HEADS, NA_HEAD_DIM)

def conv_branch(a, conv_w, conv_b, ln_g, ln_b, w_out):
    a1, a2 = jnp.split(a, 2, axis=-1)
    u = a1 * jax.nn.sigmoid(a2)
    pad = CONV_WIDTH // 2
    u = lax.conv_general_dilated(u, conv_w[:, None, :], window_strides=(1,), padding=[(pad, pad)],
                                 dimension_numbers=('NWC', 'WIO', 'NWC'),
                                 feature_group_count=CONV_DIM) + conv_b
    u = jax.nn.silu(layer_norm(u, ln_g, ln_b))
    return u @ w_out

def sgu_branch(uv, ln_g, ln_b, w_s, b_s, w_out):
    u, v = jnp.split(jax.nn.gelu(uv), 2, axis=-1)
    v = layer_norm(v, ln_g, ln_b)
    bsz, n, _ = v.shape
    v = v.reshape(bsz, n // SGU_CHUNK, SGU_CHUNK, SGU_GROUPS, SGU_DIM // SGU_GROUPS)
    v = jnp.einsum('gpq,bnqgc->bnpgc', w_s, v) + b_s.T[None, None, :, :, None]
    return (u * v.reshape(bsz, n, SGU_DIM)) @ w_out

def neighbourhood_attention(q, k, v, kc, vc, rpb):
    bsz, s, h, dh = q.shape
    rows = s // GRID_W
    kh = min(NA_KH, rows)
    ncb = GRID_W // NA_KW
    kbw = 2 * NA_KW
    r = np.arange(rows)
    row_idx = np.clip(r - kh // 2, 0, rows - kh)[:, None] + np.arange(kh)[None]
    dr = row_idx - r[:, None]
    j = np.arange(ncb)
    col_idx = np.clip(j * NA_KW - NA_KW // 2, 0, GRID_W - kbw)[:, None] + np.arange(kbw)[None]
    qc = j[:, None] * NA_KW + np.arange(NA_KW)[None]
    win_start = np.clip(qc - NA_KW // 2, 0, GRID_W - NA_KW)
    off = col_idx[:, None, :] - win_start[:, :, None]
    col_valid = (off >= 0) & (off < NA_KW)
    dc = np.clip(col_idx[:, None, :] - qc[:, :, None] + NA_KW - 1, 0, 2 * NA_KW - 2)
    bias = rpb[:, (dr + NA_KH - 1)[:, None, None, :, None], dc[None, :, :, None, :]]
    bias = jnp.where(col_valid[None, None, :, :, None, :], bias.astype(jnp.float32), NEG_INF)

    qg = q.reshape(bsz, rows, ncb, NA_KW, h, dh) * NA_HEAD_DIM ** -0.5
    kg = k.reshape(bsz, rows, GRID_W, h, dh)
    vg = v.reshape(bsz, rows, GRID_W, h, dh)
    ri = row_idx[:, None, :, None]
    ci = col_idx[None, :, None, :]
    k_blk = kg[:, ri, ci]
    v_blk = vg[:, ri, ci]
    s_loc = jnp.einsum('brjqhd,brjiwhd->bhrjqiw', qg, k_blk).astype(jnp.float32) + bias[None]
    s_loc = s_loc.reshape(bsz, h, rows, ncb, NA_KW, kh * kbw)
    s_ctx = jnp.einsum('brjqhd,bchd->bhrjqc', qg, kc).astype(jnp.float32)
    p = jax.nn.softmax(jnp.concatenate([s_loc, s_ctx], axis=-1), axis=-1).astype(v.dtype)
    p_loc = p[..., :kh * kbw].reshape(bsz, h, rows, ncb, NA_KW, kh, kbw)
    p_ctx = p[..., kh * kbw:]
    o = (jnp.einsum('bhrjqiw,brjiwhd->brjqhd', p_loc, v_blk)
         + jnp.einsum('bhrjqc,bchd->brjqhd', p_ctx, vc))
    return o.reshape(bsz, s, NA_DIM)

def context_attention(q, k, v):
    s = jnp.einsum('bqhd,bkhd->bhqk', q * NA_HEAD_DIM ** -0.5, k).astype(jnp.float32)
    p = jax.nn.softmax(s, axis=-1).astype(v.dtype)
    o = jnp.einsum('bhqk,bkhd->bqhd', p, v)
    return o.reshape(o.shape[0], o.shape[1], NA_DIM)

def mixer_output(z, y_na, conv_w, conv_b, conv_ln_g, conv_ln_b, w_conv_out, sgu_ln_g, sgu_ln_b,
                 sgu_w, sgu_b, w_sgu_out, w_na_out, w_o, b_o):
    y_conv = conv_branch(z[..., :2 * CONV_DIM], conv_w, conv_b, conv_ln_g, conv_ln_b, w_conv_out)
    y_sgu = sgu_branch(z[..., 2 * CONV_DIM:Q_OFF], sgu_ln_g, sgu_ln_b, sgu_w, sgu_b, w_sgu_out)
    y_att = y_na @ w_na_out
    g_conv, g_sgu, g_att = jnp.split(jax.nn.sigmoid(z[..., G_OFF:]), N_BRANCH, axis=-1)
    return (g_conv * y_conv + g_sgu * y_sgu + g_att * y_att) @ w_o + b_o

def sq_relu_ffn(h, w1, b1, w2, b2):
    return jnp.square(jax.nn.relu(h @ w1 + b1)) @ w2 + b2

def first_inputs(seed: int = 0) -> dict:
    key = jax.random.key(seed)
    ks = iter(jax.random.split(key, 40))
    f32 = jnp.float32

    def nrm(shape, scale):
        return jax.random.normal(next(ks), shape, f32) * scale

    L = DEPTH
    return {
        'x': nrm((BATCH, SEQ, D_MODEL), 1.0),
        'c': nrm((BATCH, D_MODEL), 1.0),
        'ctx': nrm((BATCH, CTX_LEN, D_MODEL), 1.0),
        'c_ctx': nrm((D_MODEL,), 1.0),
        'w_mod': nrm((L, D_MODEL, 6 * D_MODEL), 0.5 * D_MODEL ** -0.5),
        'b_mod': nrm((L, 6 * D_MODEL), 0.01),
        'norm1_g': 1.0 + nrm((L, D_MODEL), 0.05),
        'norm2_g': 1.0 + nrm((L, D_MODEL), 0.05),
        'w_in': nrm((L, D_MODEL, IN_DIM), D_MODEL ** -0.5),
        'b_in': nrm((L, IN_DIM), 0.01),
        'conv_w': nrm((L, CONV_WIDTH, CONV_DIM), CONV_WIDTH ** -0.5),
        'conv_b': nrm((L, CONV_DIM), 0.01),
        'conv_ln_g': 1.0 + nrm((L, CONV_DIM), 0.05),
        'conv_ln_b': nrm((L, CONV_DIM), 0.01),
        'w_conv_out': nrm((L, CONV_DIM, D_MODEL), CONV_DIM ** -0.5),
        'sgu_ln_g': 1.0 + nrm((L, SGU_DIM), 0.05),
        'sgu_ln_b': nrm((L, SGU_DIM), 0.01),
        'sgu_w': nrm((L, SGU_GROUPS, SGU_CHUNK, SGU_CHUNK), SGU_CHUNK ** -0.5),
        'sgu_b': 1.0 + nrm((L, SGU_GROUPS, SGU_CHUNK), 0.1),
        'w_sgu_out': nrm((L, SGU_DIM, D_MODEL), SGU_DIM ** -0.5),
        'na_rpb': nrm((L, NA_HEADS, 2 * NA_KH - 1, 2 * NA_KW - 1), 0.5),
        'w_na_out': nrm((L, NA_DIM, D_MODEL), NA_DIM ** -0.5),
        'w_o': nrm((L, D_MODEL, D_MODEL), D_MODEL ** -0.5),
        'b_o': nrm((L, D_MODEL), 0.01),
        'w_ff1': nrm((L, D_MODEL, D_FF), D_MODEL ** -0.5),
        'b_ff1': nrm((L, D_FF), 0.01),
        'w_ff2': nrm((L, D_FF, D_MODEL), D_FF ** -0.5),
        'b_ff2': nrm((L, D_MODEL), 0.01),
        'final_g': 1.0 + nrm((D_MODEL,), 0.05),
    }

def first_block(x, c, ctx, c_ctx, w_mod, b_mod, norm1_g, norm2_g, w_in, b_in, conv_w, conv_b,
              conv_ln_g, conv_ln_b, w_conv_out, sgu_ln_g, sgu_ln_b, sgu_w, sgu_b, w_sgu_out,
              na_rpb, w_na_out, w_o, b_o, w_ff1, b_ff1, w_ff2, b_ff2, final_g):
    silu_c = jax.nn.silu(c)
    silu_cc = jax.nn.silu(c_ctx)[None]
    xl, xc = x, ctx
    for l in range(DEPTH):
        last = l == DEPTH - 1
        mod_l = jnp.split(silu_c @ w_mod[l] + b_mod[l], 6, axis=-1)
        mod_c = jnp.split(silu_cc @ w_mod[l] + b_mod[l], 6, axis=-1)
        branch_params = (conv_w[l], conv_b[l], conv_ln_g[l], conv_ln_b[l], w_conv_out[l],
                         sgu_ln_g[l], sgu_ln_b[l], sgu_w[l], sgu_b[l], w_sgu_out[l],
                         w_na_out[l], w_o[l], b_o[l])
        hl = modulate(rms_norm(xl, norm1_g[l]), mod_l[0], mod_l[1])
        hc = modulate(rms_norm(xc, norm1_g[l]), mod_c[0], mod_c[1])
        zl = hl @ w_in[l] + b_in[l]
        if last:
            zkv = hc @ w_in[l, :, K_OFF:G_OFF] + b_in[l, K_OFF:G_OFF]
            kc, vc = split_heads(zkv[..., :NA_DIM]), split_heads(zkv[..., NA_DIM:])
        else:
            zc = hc @ w_in[l] + b_in[l]
            kc, vc = split_heads(zc[..., K_OFF:V_OFF]), split_heads(zc[..., V_OFF:G_OFF])
        y_na_l = neighbourhood_attention(split_heads(zl[..., Q_OFF:K_OFF]), split_heads(zl[..., K_OFF:V_OFF]),
                                         split_heads(zl[..., V_OFF:G_OFF]), kc, vc, na_rpb[l])
        xl = xl + mod_l[2][:, None, :] * mixer_output(zl, y_na_l, *branch_params)
        hl2 = modulate(rms_norm(xl, norm2_g[l]), mod_l[3], mod_l[4])
        xl = xl + mod_l[5][:, None, :] * sq_relu_ffn(hl2, w_ff1[l], b_ff1[l], w_ff2[l], b_ff2[l])
        if not last:
            y_na_c = context_attention(split_heads(zc[..., Q_OFF:K_OFF]), kc, vc)
            xc = xc + mod_c[2][:, None, :] * mixer_output(zc, y_na_c, *branch_params)
            hc2 = modulate(rms_norm(xc, norm2_g[l]), mod_c[3], mod_c[4])
            xc = xc + mod_c[5][:, None, :] * sq_relu_ffn(hc2, w_ff1[l], b_ff1[l], w_ff2[l], b_ff2[l])
    return rms_norm(xl, final_g)


DEPTH_2 = 2

DSW_HEADS = 8
DSW_HEAD_DIM = D_MODEL // 16
DSW_WIDTH = DSW_HEADS * DSW_HEAD_DIM
DSW_PATTERNS = ((128, 1), (512, 4), (2048, 16))
DSW_BLOCK = 128
GLA_HEADS = 4
GLA_DK = D_MODEL // 16
GLA_DV = D_MODEL // 8
GLA_QK_WIDTH = GLA_HEADS * GLA_DK
GLA_WIDTH = GLA_HEADS * GLA_DV
GLA_RANK = 16
GLA_TAU = 16.0
S5_WIDTH = D_MODEL // 2
S5_GROUP = 16
S5_GROUPS = S5_WIDTH // S5_GROUP
S5_STATE = 64
S5_DT_MIN = 1e-3
S5_DT_MAX = 1e-1
HGRN_HEADS = 8
HGRN_DIM = D_MODEL // 16
HGRN_WIDTH = HGRN_HEADS * HGRN_DIM
CHUNK = 64
AB_WIDTH = DSW_WIDTH + GLA_WIDTH
CD_WIDTH = S5_WIDTH + HGRN_WIDTH
AB_SIZES = (DSW_WIDTH, DSW_WIDTH, DSW_WIDTH, GLA_QK_WIDTH, GLA_QK_WIDTH, GLA_WIDTH, GLA_RANK, AB_WIDTH)
CD_SIZES = (S5_WIDTH, HGRN_WIDTH, HGRN_WIDTH, HGRN_WIDTH, CD_WIDTH)
AB_IN = sum(AB_SIZES)
CD_IN = sum(CD_SIZES)
AB_SPLIT = tuple(int(v) for v in np.cumsum(AB_SIZES)[:-1])
CD_SPLIT = tuple(int(v) for v in np.cumsum(CD_SIZES)[:-1])
N_EVEN = (DEPTH_2 + 1) // 2
N_ODD = DEPTH_2 // 2


def rmsnorm(x, g):
    xf = x.astype(jnp.float32)
    return xf * lax.rsqrt(jnp.mean(xf * xf, axis=-1, keepdims=True) + EPS) * g

def head_rmsnorm(o, g):
    o = o * lax.rsqrt(jnp.mean(o * o, axis=-1, keepdims=True) + EPS)
    return o.reshape(o.shape[0], o.shape[1], -1) * g

def dilated_pattern(q, k, v, window, dilation):
    B, S, H, E = q.shape
    d = dilation
    M = S // d
    wc = window // d
    blk = DSW_BLOCK
    nb = -(-M // blk)
    Mp = nb * blk

    def strided(t):
        return jnp.pad(t.reshape(B, M, d, H, E), ((0, 0), (0, Mp - M), (0, 0), (0, 0), (0, 0)))

    def band(t):
        tp = jnp.pad(t, ((0, 0), (blk, 0), (0, 0), (0, 0), (0, 0)))
        prev = tp[:, :Mp].reshape(B, nb, blk, d, H, E)
        cur = t.reshape(B, nb, blk, d, H, E)
        return jnp.concatenate([prev, cur], axis=2)

    qb = strided(q).reshape(B, nb, blk, d, H, E)
    kb = band(strided(k))
    vb = band(strided(v))
    s = jnp.einsum('bnidhe,bnjdhe->bndhij', qb, kb) * (E ** -0.5)
    i_idx = np.arange(blk)[:, None]
    j_idx = np.arange(2 * blk)[None, :]
    n_idx = np.arange(nb)[:, None, None]
    offset = blk + i_idx - j_idx
    key_pos = (n_idx - 1) * blk + j_idx
    mask = (offset >= 0) & (offset <= wc) & (key_pos >= 0)
    s = jnp.where(mask[None, :, None, None], s, -jnp.inf)
    m = jnp.max(s, axis=-1, keepdims=True)
    p = jnp.exp(s - m)
    den = jnp.sum(p, axis=-1)
    o = jnp.einsum('bndhij,bnjdhe->bnidhe', p, vb) / jnp.transpose(den, (0, 1, 4, 2, 3))[..., None]
    lse = jnp.transpose(m[..., 0] + jnp.log(den), (0, 1, 4, 2, 3))
    o = o.reshape(B, Mp, d, H, E)[:, :M].reshape(B, S, H, E)
    lse = lse.reshape(B, Mp, d, H)[:, :M].reshape(B, S, H)
    return o, lse

def dilated_attention(q, k, v):
    outs, lses = [], []
    for window, dilation in DSW_PATTERNS:
        o, lse = dilated_pattern(q, k, v, window, dilation)
        outs.append(o)
        lses.append(lse)
    w = jax.nn.softmax(jnp.stack(lses, axis=0), axis=0)
    return jnp.einsum('pbsh,pbshe->bshe', w, jnp.stack(outs, axis=0))

def chunked_gated_linear_attention(q, k, v, log_g):
    B, S, H, K = q.shape
    V = v.shape[-1]
    n = S // CHUNK

    def blocks(t):
        return jnp.moveaxis(t.reshape(B, n, CHUNK, H, t.shape[-1]), 1, 0)

    qc, kc, vc = blocks(q), blocks(k), blocks(v)
    bc = jnp.cumsum(blocks(log_g), axis=2)
    causal = np.tril(np.ones((CHUNK, CHUNK), dtype=bool))[None, :, :, None, None]

    def step(state, inp):
        qi, ki, vi, bi = inp
        inter = jnp.einsum('bihk,bhkv->bihv', qi * jnp.exp(bi), state)
        diff = bi[:, :, None] - bi[:, None, :]
        decay = jnp.exp(jnp.where(causal, diff, -jnp.inf))
        scores = jnp.einsum('bihk,bjhk,bijhk->bhij', qi, ki, decay)
        intra = jnp.einsum('bhij,bjhv->bihv', scores, vi)
        b_last = bi[:, -1]
        k_dec = ki * jnp.exp(b_last[:, None] - bi)
        state = state * jnp.exp(b_last)[..., None] + jnp.einsum('bjhk,bjhv->bhkv', k_dec, vi)
        return state, inter + intra

    state0 = jnp.zeros((B, H, K, V), jnp.float32)
    _, out = lax.scan(step, state0, (qc, kc, vc, bc))
    return jnp.moveaxis(out, 0, 1).reshape(B, S, H, V)

def _cmul(ar, ai, br, bi):
    return ar * br - ai * bi, ar * bi + ai * br

def _s5_combine(e1, e2):
    a1r, a1i, b1r, b1i = e1
    a2r, a2i, b2r, b2i = e2
    ar, ai = _cmul(a2r, a2i, a1r, a1i)
    br, bi = _cmul(a2r, a2i, b1r, b1i)
    return ar, ai, br + b2r, bi + b2i

def s5_mixer(u, lam_re, lam_im, log_dt, b_re, b_im, c_re, c_im, d_skip, w_glu, b_glu):
    B, S, _ = u.shape
    f32 = jnp.float32
    lam_re, lam_im = lam_re.astype(f32), lam_im.astype(f32)
    b_re, b_im, c_re, c_im = b_re.astype(f32), b_im.astype(f32), c_re.astype(f32), c_im.astype(f32)
    ug = u.reshape(B, S, S5_GROUPS, S5_GROUP)
    dt = jnp.exp(log_dt.astype(f32))[:, None]
    mag = jnp.exp(lam_re * dt)
    ang = lam_im * dt
    ab_re, ab_im = mag * jnp.cos(ang), mag * jnp.sin(ang)
    inv = 1.0 / (lam_re * lam_re + lam_im * lam_im)
    nr, ni = ab_re - 1.0, ab_im
    co_re = (nr * lam_re + ni * lam_im) * inv
    co_im = (ni * lam_re - nr * lam_im) * inv
    bb_re, bb_im = _cmul(co_re[..., None], co_im[..., None], b_re, b_im)
    ut = jnp.swapaxes(ug, 0, 1)
    bu_re = jnp.einsum('gph,sbgh->sbgp', bb_re, ut)
    bu_im = jnp.einsum('gph,sbgh->sbgp', bb_im, ut)
    a_re = jnp.broadcast_to(ab_re, (S, 1, S5_GROUPS, S5_STATE))
    a_im = jnp.broadcast_to(ab_im, (S, 1, S5_GROUPS, S5_STATE))
    _, _, x_re, x_im = lax.associative_scan(_s5_combine, (a_re, a_im, bu_re, bu_im), axis=0)
    y = (jnp.einsum('ghp,sbgp->bsgh', c_re, x_re) - jnp.einsum('ghp,sbgp->bsgh', c_im, x_im)
         + d_skip * ug)
    y = jax.nn.gelu(y.reshape(B, S, S5_WIDTH))
    return y * jax.nn.sigmoid(y @ w_glu + b_glu)

def ab_layer(h, w_in, gla_w_gate, gla_b_gate, gla_norm_g, w_out):
    B, S, _ = h.shape
    z = h @ w_in
    qa, ka, va, qb, kb, vb, g_low, gate = jnp.split(z, AB_SPLIT, axis=-1)
    sh_a = (B, S, DSW_HEADS, DSW_HEAD_DIM)
    ya = dilated_attention(qa.reshape(sh_a), ka.reshape(sh_a), va.reshape(sh_a)).reshape(B, S, DSW_WIDTH)
    log_a = jax.nn.log_sigmoid(g_low @ gla_w_gate + gla_b_gate) / GLA_TAU
    sh_k = (B, S, GLA_HEADS, GLA_DK)
    ob = chunked_gated_linear_attention((qb * GLA_DK ** -0.5).reshape(sh_k), kb.reshape(sh_k),
                                        vb.reshape(B, S, GLA_HEADS, GLA_DV), log_a.reshape(sh_k))
    yb = head_rmsnorm(ob, gla_norm_g)
    y = jnp.concatenate([ya, yb], axis=-1) * jax.nn.silu(gate)
    return y @ w_out

def cd_layer(h, w_in, lam_re, lam_im, log_dt, b_re, b_im, c_re, c_im, d_skip, w_glu, b_glu,
             lower_bound, hgrn_norm_g, w_out):
    B, S, _ = h.shape
    z = h @ w_in
    u, qd, fd, idd, gate = jnp.split(z, CD_SPLIT, axis=-1)
    yc = s5_mixer(u, lam_re, lam_im, log_dt, b_re, b_im, c_re, c_im, d_skip, w_glu, b_glu)
    f = lower_bound + (1.0 - lower_bound) * jax.nn.sigmoid(fd)
    sh = (B, S, HGRN_HEADS, HGRN_DIM)
    od = chunked_gated_linear_attention(jax.nn.silu(qd).reshape(sh), (1.0 - f).reshape(sh),
                                        idd.reshape(sh), jnp.log(f).reshape(sh))
    yd = head_rmsnorm(od, hgrn_norm_g)
    y = jnp.concatenate([yc, yd], axis=-1) * jax.nn.silu(gate)
    return y @ w_out

def second_inputs(seed: int = 0) -> dict:
    key = jax.random.key(seed)
    ks = jax.random.split(key, 24)
    f32 = jnp.float32

    def nrm(k, shape, s):
        return s * jax.random.normal(k, shape, f32)

    G, P, Hc = S5_GROUPS, S5_STATE, S5_GROUP
    return {
        'x': nrm(ks[0], (BATCH, SEQ, D_MODEL), 1.0),
        'norm_g': 1.0 + nrm(ks[1], (DEPTH_2, D_MODEL), 0.02),
        'final_g': 1.0 + nrm(ks[2], (D_MODEL,), 0.02),
        'ab_w_in': nrm(ks[3], (N_EVEN, D_MODEL, AB_IN), D_MODEL ** -0.5),
        'gla_w_gate': nrm(ks[4], (N_EVEN, GLA_RANK, GLA_QK_WIDTH), GLA_RANK ** -0.5),
        'gla_b_gate': nrm(ks[5], (N_EVEN, GLA_QK_WIDTH), 0.1),
        'gla_norm_g': 1.0 + nrm(ks[6], (N_EVEN, GLA_WIDTH), 0.02),
        'ab_w_out': nrm(ks[7], (N_EVEN, AB_WIDTH, D_MODEL), AB_WIDTH ** -0.5),
        'cd_w_in': nrm(ks[8], (N_ODD, D_MODEL, CD_IN), D_MODEL ** -0.5),
        's5_lam_re': -0.5 + nrm(ks[9], (N_ODD, G, P), 0.01),
        's5_lam_im': math.pi * jnp.arange(P, dtype=f32) + nrm(ks[10], (N_ODD, G, P), 0.01),
        's5_log_dt': jax.random.uniform(ks[11], (N_ODD, G), f32, math.log(S5_DT_MIN), math.log(S5_DT_MAX)),
        's5_b_re': nrm(ks[12], (N_ODD, G, P, Hc), (2 * Hc) ** -0.5),
        's5_b_im': nrm(ks[13], (N_ODD, G, P, Hc), (2 * Hc) ** -0.5),
        's5_c_re': nrm(ks[14], (N_ODD, G, Hc, P), 0.5),
        's5_c_im': nrm(ks[15], (N_ODD, G, Hc, P), 0.5),
        's5_d': nrm(ks[16], (N_ODD, G, Hc), 1.0),
        's5_w_glu': nrm(ks[17], (N_ODD, S5_WIDTH, S5_WIDTH), S5_WIDTH ** -0.5),
        's5_b_glu': nrm(ks[18], (N_ODD, S5_WIDTH), 0.1),
        'hgrn_gamma': nrm(ks[19], (DEPTH_2, HGRN_WIDTH), 1.0),
        'hgrn_norm_g': 1.0 + nrm(ks[20], (N_ODD, HGRN_WIDTH), 0.02),
        'cd_w_out': nrm(ks[21], (N_ODD, CD_WIDTH, D_MODEL), CD_WIDTH ** -0.5),
    }

def second_block(x, norm_g, final_g, ab_w_in, gla_w_gate, gla_b_gate, gla_norm_g, ab_w_out,
              cd_w_in, s5_lam_re, s5_lam_im, s5_log_dt, s5_b_re, s5_b_im, s5_c_re, s5_c_im,
              s5_d, s5_w_glu, s5_b_glu, hgrn_gamma, hgrn_norm_g, cd_w_out):
    h = x.astype(jnp.float32)
    sm = jax.nn.softmax(hgrn_gamma.astype(jnp.float32), axis=0)
    lower_bounds = jnp.cumsum(sm, axis=0) - sm[0]
    for l in range(DEPTH_2):
        hn = rmsnorm(h, norm_g[l])
        j = l // 2
        if l % 2 == 0:
            h = h + ab_layer(hn, ab_w_in[j], gla_w_gate[j], gla_b_gate[j], gla_norm_g[j], ab_w_out[j])
        else:
            h = h + cd_layer(hn, cd_w_in[j], s5_lam_re[j], s5_lam_im[j], s5_log_dt[j], s5_b_re[j],
                             s5_b_im[j], s5_c_re[j], s5_c_im[j], s5_d[j], s5_w_glu[j], s5_b_glu[j],
                             lower_bounds[l], hgrn_norm_g[j], cd_w_out[j])
    return rmsnorm(h, final_g).astype(x.dtype)


_first_inputs = second_inputs


def second_inputs(seed=0):
    import zlib

    import numpy as np

    out = dict(_first_inputs(seed))
    spreads = {}
    factors = {'final_g': 20.998,
     'gla_b_gate': 3.151,
     'gla_norm_g': 6.458,
     's5_lam_re': 200.0,
     's5_b_glu': 200.0,
     'hgrn_norm_g': 99.613,
     's5_lam_im': 64.0,
     's5_log_dt': 64.0,
     's5_b_re': 64.0,
     's5_b_im': 64.0,
     's5_c_re': 64.0,
     's5_c_im': 64.0,
     's5_w_glu': 51.144,
     's5_d': 4.621}
    for name, (base, spread) in spreads.items():
        noise = np.random.default_rng([zlib.crc32(name.encode()), seed]).standard_normal(out[name].shape)
        drawn = base * np.exp(spread * noise) if base else spread * noise
        out[name] = __import__('jax').numpy.asarray(drawn.astype(out[name].dtype))
    for name, factor in factors.items():
        out[name] = (out[name] * factor).astype(out[name].dtype)
    return out


_narrow_inputs = second_inputs


def second_inputs(seed=0):
    out = dict(_narrow_inputs(seed))
    wider = {'final_g': 3.1, 's5_d': 3.12, 's5_w_glu': 3.92, 's5_b_glu': 12.0, 'hgrn_norm_g': 3.42}
    for name, times in wider.items():
        mean = out[name].mean()
        out[name] = (mean + times * (out[name] - mean)).astype(out[name].dtype)
    return out


def setup_inputs(seed=0):
    out = dict(first_inputs(seed))
    for name, value in second_inputs(seed + 1).items():
        if name != "x":
            out[name + "_2"] = value
    return out


def reference(
    x, c, ctx, c_ctx, w_mod, b_mod, norm1_g, norm2_g, w_in, b_in, conv_w, conv_b, conv_ln_g,
    conv_ln_b, w_conv_out, sgu_ln_g, sgu_ln_b, sgu_w, sgu_b, w_sgu_out, na_rpb, w_na_out, w_o,
    b_o, w_ff1, b_ff1, w_ff2, b_ff2, final_g, norm_g_2, final_g_2, ab_w_in_2, gla_w_gate_2,
    gla_b_gate_2, gla_norm_g_2, ab_w_out_2, cd_w_in_2, s5_lam_re_2, s5_lam_im_2, s5_log_dt_2,
    s5_b_re_2, s5_b_im_2, s5_c_re_2, s5_c_im_2, s5_d_2, s5_w_glu_2, s5_b_glu_2, hgrn_gamma_2,
    hgrn_norm_g_2, cd_w_out_2,
):
    x = first_block(
        x, c, ctx, c_ctx, w_mod, b_mod, norm1_g, norm2_g, w_in, b_in, conv_w, conv_b, conv_ln_g,
        conv_ln_b, w_conv_out, sgu_ln_g, sgu_ln_b, sgu_w, sgu_b, w_sgu_out, na_rpb, w_na_out,
        w_o, b_o, w_ff1, b_ff1, w_ff2, b_ff2, final_g,
    )
    return second_block(
        x, norm_g_2, final_g_2, ab_w_in_2, gla_w_gate_2, gla_b_gate_2, gla_norm_g_2, ab_w_out_2,
        cd_w_in_2, s5_lam_re_2, s5_lam_im_2, s5_log_dt_2, s5_b_re_2, s5_b_im_2, s5_c_re_2,
        s5_c_im_2, s5_d_2, s5_w_glu_2, s5_b_glu_2, hgrn_gamma_2, hgrn_norm_g_2, cd_w_out_2,
    )


_drawn_inputs = setup_inputs


def setup_inputs(seed=0):
    import zlib

    import numpy as np

    out = dict(_drawn_inputs(seed))
    spreads = {}
    factors = {'b_in': 5.337,
     'conv_b': 8.0,
     'conv_ln_g': 3.045,
     'conv_ln_b': 8.0,
     'sgu_ln_b': 8.0,
     'na_rpb': 3.451,
     'b_o': 4.946,
     'b_ff1': 3.814,
     'b_ff2': 4.899,
     's5_b_glu_2': 3.553,
     'sgu_ln_g': 3.409}
    for name, (base, spread) in spreads.items():
        noise = np.random.default_rng([zlib.crc32(name.encode()), seed]).standard_normal(out[name].shape)
        drawn = base * np.exp(spread * noise) if base else spread * noise
        out[name] = jnp.asarray(drawn.astype(out[name].dtype))
    for name, factor in factors.items():
        out[name] = (out[name] * factor).astype(out[name].dtype)
    return out
```

```python
from contextlib import ExitStack, contextmanager

import numpy as np

import concourse.bass as bass
import concourse.mybir as mybir

F32 = mybir.dt.float32
I32 = mybir.dt.int32
ACT = mybir.ActivationFunctionType
ALU = mybir.AluOpType
AX_X = mybir.AxisListType.X
ds = bass.ds

P = 128
D = 2048
KT = D // P
HW = D // 2
HT = HW // P
T = 256
FF = 4 * D
EPS = 1e-6
NEG = -1e30
TAPS = 31
PAD = TAPS // 2
GRID = 64
WIN = 16
NHEAD = 16
DRS = 15
DCS = 31
PADW = 127
LEVELS = 8
TWO_PI = 6.283185307179586
ROUND = 12582912.0

A1, A2, SU, SV, WQ, WK, WV, WG = 0, 1024, 2048, 3072, 4096, 5120, 6144, 7168

PACKS = (
    (("b_in", 104), ("norm1_g", 16), ("conv_b", 8)),
    (("b_mod", 96), ("norm2_g", 16), ("b_o", 16)),
    (("b_ff1", 64), ("b_ff2", 16), ("norm_g_2", 32), ("final_g_2", 16)),
    (("c", 16), ("c_ctx", 16), ("conv_ln_g", 8), ("conv_ln_b", 8), ("sgu_ln_g", 8), ("sgu_ln_b", 8),
     ("gla_b_gate_2", 4), ("gla_norm_g_2", 8), ("s5_d_2", 8), ("s5_b_glu_2", 8), ("hgrn_norm_g_2", 8)),
    (("final_g", 16), ("hgrn_gamma_2", 16)),
)
COL = {}
for _n, _pack in enumerate(PACKS):
    _at = _n * P
    for _name, _rows in _pack:
        COL[_name] = _at
        _at += _rows

STREAM = (
    ("mod", "w_mod", 0, 12, 16, 256),
    ("q", "w_in", WQ, 1, 16, 256), ("k", "w_in", WK, 1, 16, 256), ("v", "w_in", WV, 1, 16, 256),
    ("a2", "w_in", A2, 1, 16, 256), ("a1", "w_in", A1, 1, 16, 256),
    ("su", "w_in", SU, 1, 16, 256), ("sv", "w_in", SV, 1, 16, 256),
    ("gate_conv", "w_in", WG, 2, 16, 256), ("out_conv", "w_conv_out", 0, 1, 8, 512),
    ("gate_sgu", "w_in", WG + D, 2, 16, 256), ("out_sgu", "w_sgu_out", 0, 1, 8, 512),
    ("gate_att", "w_in", WG + 2 * D, 2, 16, 256), ("out_att", "w_na_out", 0, 1, 8, 512),
    ("o", "w_o", 0, 2, 16, 256),
    ("ff1", "w_ff1", 0, 8, 16, 256), ("ff2", "w_ff2", 0, 8, 64, 256),
    ("va", "ab_w_in_2", 2048, 1, 16, 256), ("qa", "ab_w_in_2", 0, 1, 16, 256),
    ("ka", "ab_w_in_2", 1024, 1, 16, 256), ("qkb", "ab_w_in_2", 3072, 1, 16, 256),
    ("vb", "ab_w_in_2", 4096, 1, 16, 256), ("gate_ab", "ab_w_in_2", 5136, 2, 16, 256),
    ("ab_out", "ab_w_out_2", 0, 2, 16, 256),
    ("u", "cd_w_in_2", 0, 1, 16, 256), ("glu", "s5_w_glu_2", 0, 1, 8, 256),
    ("qd", "cd_w_in_2", 1024, 1, 16, 256), ("fd", "cd_w_in_2", 2048, 1, 16, 256),
    ("id", "cd_w_in_2", 3072, 1, 16, 256), ("gate_cd", "cd_w_in_2", 4096, 2, 16, 256),
    ("cd_out", "cd_w_out_2", 0, 2, 16, 256),
)
ROUNDS = {s[0]: s[3] for s in STREAM}
GLOW = 5120


class Count:

    def __init__(self, sem, step=1):
        self.sem, self.step, self.n, self.round, self.per = sem, step, 0, None, 0

    def up(self):
        self.n += 1
        return self.step

    def now(self, more=0):
        n = (self.n + more) * self.step
        return n if self.round is None else self.round * (self.per * self.step) + n

    def next(self):
        self.n += 1
        return self.now()


@contextmanager
def rounds(eng, n, per):
    start = {c: c.n for c in per}
    with eng.Fori(0, n) as i:
        for c, k in per.items():
            c.round, c.per = i, k
        yield i
    for c, k in per.items():
        assert c.n - start[c] == k, (c.sem, c.n - start[c], k)
        c.round, c.n = None, start[c] + n * k


def program(nc, dram, out):
    ctx = ExitStack()
    with ctx:
        def sb(name, shape, dt=F32):
            return ctx.enter_context(nc.sbuf_tensor(name, shape, dt))

        def sem(name):
            return ctx.enter_context(nc.semaphore(name))

        ring = sb("ring", [P, 4, 4096])
        arena = sb("arena", [P, 34048])
        cols = sb("cols", [P, len(PACKS) * P])
        mod = sb("mod", [P, 96, 2])
        ident = sb("ident", [P, P])
        ones = sb("ones", [P, P])
        mirror = sb("mirror", [P, P])
        cvec = sb("cvec", [P, KT, 2])
        gain = sb("gain", [P, 3, KT])
        taps = sb("taps", [P, HT, 32])
        bq = sb("bq", [P, HT])
        small = sb("small", [P, 16])
        s5p = sb("s5p", [P, 12, 32])
        padrow = sb("padrow", [120, 2, PADW])
        psum = ctx.enter_context(nc.psum_tensor("psum", [P, 8, 512], F32))
        bias_rows = nc.dram_tensor("bias_rows", (NHEAD, DRS, PADW), F32).ap()

        def at(off, *shape):
            n = int(np.prod(shape))
            v = arena[:, off:off + n]
            if len(shape) == 2:
                return v.rearrange("p (a b) -> p a b", a=shape[0])
            if len(shape) == 3:
                return v.rearrange("p (a b c) -> p a b c", a=shape[0], b=shape[1])
            return v

        X = at(0, KT, T)
        H = at(4096, KT, 2 * T)
        HL, MIX = H[:, :, 0:T], H[:, :, T:2 * T]
        H2 = at(4096, KT, T)
        XN, CN = at(12288, 2, D), at(16384, 2, D)
        PACK = [at(20480 + P * n, P) for n in range(4)] + [at(22016, P)]
        TAPN = at(20992, HW)
        SQ1 = at(12288, KT, T)
        NQ, NK = at(12288, HT, T), at(14336, HT, 2 * T)
        NV = at(18432, 4, HW)
        ATT = at(22528, HT, T)
        VROW = at(22528, HW)
        BIAS = at(24576, NHEAD, 6, GRID)
        ST_Q, ST_K = at(30720, T), at(30976, 2 * T)
        ST_V = at(31488, 4, P)
        ST_B = H[:, 0:4, T:2 * T]
        PR = [at(32000, 512), at(32512, 512)]
        PT = [at(33024, 512), at(33536, 512)]
        GATE = at(12288, KT, T)
        U = at(16384, HT, T + 2 * PAD)
        CV = at(18672, HT, T)
        TMP = at(20720, 2, T)
        MEAN = at(21488, T)
        ZU, ZV = at(24576, HT, T), at(26624, HT, T)
        VT = at(28672, 2, HW)
        WST = at(30720, HT, P)
        SQ = at(31744, HT, T)
        SGN = at(28672, HT, P)
        SGB = at(33792, P)
        RS = at(21232, T)
        WMASK = at(34048 - GRID, GRID)
        HID = at(12288, FF // P, T)
        VA = at(8192, 2, HW)
        QA, KA = at(10240, HT, T), at(12288, HT, T)
        QB, KB = at(14336, 4, T), at(15360, 4, T)
        VB = at(16384, 2, HW)
        GG = at(18432, 4, T)
        GATE2 = at(19456, KT, T)
        Y = at(23552, KT, T)
        DQ, DK, DV = at(27648, T), at(27904, T), at(28160, 2, P)
        DP = [at(28416, T), at(28672, T)]
        DT_ = [at(28928, T), at(29184, T)]
        CNT, MASK = at(29440, 2, T), at(29952, 2, T)
        GLW, GWG, GTMP = at(30464, KT, 16), at(30720, 512), at(31232, 1024)
        GLO = at(33792, T)
        LMASK = at(32768, LEVELS, P)
        SU5 = at(8192, HT, T)
        SX = at(10240, 2, 16, T)
        Y5 = at(18432, KT, T)
        QD, FD = at(22528, HT, T), at(24576, HT, T)
        ID = at(26624, 2, HW)
        GATE3 = at(13312, KT, T)
        BT = at(26624, 2, HT, P)
        CT = at(28672, 2, HT, P)
        PW = at(30720, 2, 32, 16)
        ST = at(31744, 1024)
        QKB = at(14336, HT, T)
        DIFF, DIFF2 = at(31232, 2, T).bitcast(I32), at(31744, 2, T).bitcast(I32)
        IDX = at(28672, 3, P).bitcast(I32)
        IDXF = at(29056, 2, P)
        GG3, GTMP3 = at(18432, 4, T), at(31232, 4, T)
        GLA = {"QL": at(4096, LEVELS + 1, 512), "KL": at(8704, LEVELS + 1, 512), "D": at(27648, 512),
               "F": at(28160, 512), "q": at(28672, 512), "k": at(29184, 512), "V": at(29696, 2, 512),
               "A": at(30720, LEVELS, P), "SC": at(31744, 2, 3, P), "SQ": at(4096, HT, T)}
        HG = {"QL": at(4096, LEVELS + 1, 512), "KL": at(8704, LEVELS + 1, 512), "D": at(28672, 512),
              "F": at(29184, 512), "q": at(29696, 512), "k": at(30208, 512), "V": at(30720, 2, 256),
              "A": at(31232, LEVELS, P), "SC": at(17408, 2, 3, P), "SQ": at(4096, HT, T)}
        YD = Y5[:, HT:KT, :]
        TMP2 = at(29184, T)
        S5N, S5DT = at(10240, 384), at(10624, 2)
        S5BN, S5B = at(10752, 2, 32, 16), at(11776, 1024)
        S5T = at(12800, 32, 16)
        S5C, S5CI = at(13312, HT, P), at(14336, HT, P)
        CMASK = at(15360, P)

        sems = {}

        def sem(name):
            if name not in sems:
                sems[name] = ctx.enter_context(nc.semaphore(name))
            return sems[name]

        class Counts(dict):

            def __missing__(self, name):
                self[name] = Count(sem(name), 16 if name.startswith("load") else 1)
                return self[name]

        block = ctx.enter_context(nc.Block())

        def col(name, k=0, n=1):
            return cols[:, COL[name] + k:COL[name] + k + n]

        def over(ap, n, axis=1):
            a = ap.unsqueeze(axis)
            shape = [int(v) for v in a.shape]
            shape[axis] = n
            return a.broadcast_to(shape)

        def full(c, b):
            return f"bank{b}_full_for_{c}"

        def free(c, b):
            return f"bank{b}_read_by_{c}"

        @block.sync
        def _(sp):
            n = Counts()
            n["slot3_used"].n = 1
            first = True
            for name, array, c0, turns, kt, width in STREAM:
                w = dram[array].rearrange("(k p) n -> p k n", p=P)

                def load(i, s, wait):
                    if wait:
                        sp.wait_ge(sem(f"slot{s}_used"), n[f"slot{s}_used"].next())
                    if kt == 64:
                        src = w[:, 16 * s:16 * s + 16, ds(i * width, width)]
                        dst = ring[:, s, :].rearrange("p (k n) -> p k n", k=16)
                    else:
                        src = w[:, :, ds(i * 4 * width + (c0 + s * width), width)]
                        dst = ring[:, s, 0:kt * width].rearrange("p (k n) -> p k n", k=kt)
                    sp.dma_start(dst, src).then_inc(sem(f"load_slot{s}"), 16)

                if first:
                    for s in range(4):
                        load(0, s, False)
                    with rounds(sp, turns - 1, {n[f"slot{s}_used"]: 1 for s in range(4)}) as i:
                        for s in range(4):
                            load(i + 1, s, True)
                elif turns == 1:
                    for s in range(4):
                        load(0, s, True)
                else:
                    with rounds(sp, turns, {n[f"slot{s}_used"]: 1 for s in range(4)}) as i:
                        for s in range(4):
                            load(i, s, True)
                first = False
            sp.wait_ge(sem("result_ready"), n["result_ready"].next())
            sp.dma_start(out.rearrange("(t p) n -> p t n", p=P), at(12288, 2, D)).then_inc(sem("load_result"), 16)
            sp.wait_ge(sem("load_result"), 16)

        @block.tensor
        def _(pe):
            n = Counts()
            reader = {}

            def take(b, c):
                if reader.get(b, c) != c:
                    pe.wait_ge(sem(free(reader[b], b)), n[full(reader[b], b)].now(1))
                reader[b] = c
                pe.wait_ge(sem(free(c, b)), n[full(c, b)].now(1))


            def leave(ins, s):
                ins.then_inc(sem(f"slot{(s + 3) % 4}_used"), 1)

            def slots(turns, used, body, extra=None):
                per = {n[f"load_slot{s}"]: 1 for s in range(4)}
                for b, c in used:
                    per[n[full(c, b)]] = per.get(n[full(c, b)], 0) + 1
                if turns == 1:
                    for s in range(4):
                        body(0, s)
                else:
                    with rounds(pe, turns, per) as i:
                        for s in range(4):
                            body(i, s)

            def stationary(name, rhs, c, kt=16, width=256, N=T):
                each = min(2, 512 // N) if N > 2 else 2
                nb = width // P // each

                def body(i, s):
                    pe.wait_ge(sem(f"load_slot{s}"), n[f"load_slot{s}"].next())
                    w = ring[:, s, 0:kt * width].rearrange("p (k n) -> p k n", k=kt)
                    for h in range(nb):
                        b = (s * nb + h) % 4
                        take(b, c)
                        for m in range(each):
                            o = (h * each + m) * P
                            for k in range(kt):
                                mm = pe.matmul(psum[:, b, m * N:(m + 1) * N], w[:, k, o:o + P], rhs(k),
                                               start=(k == 0), stop=(k == kt - 1))
                                if h == m == k == 0:
                                    leave(mm, s)
                        mm.then_inc(sem(full(c, b)), n[full(c, b)].up())

                slots(ROUNDS[name], [((s * nb + h) % 4, c) for s in range(4) for h in range(nb)], body)

            def token_major(name, lhs, toks, c, bias=None):
                nb = toks // 2

                def body(i, s):
                    pe.wait_ge(sem(f"load_slot{s}"), n[f"load_slot{s}"].next())
                    w = ring[:, s, :].rearrange("p (k n) -> p k n", k=16)
                    for h in range(nb):
                        b = (s * nb + h) % 4
                        take(b, c)
                        for m in range(2):
                            t = 2 * h + m
                            o = psum[:, b, m * T:(m + 1) * T]
                            for k in range(KT):
                                mm = pe.matmul(o, lhs(k, t), w[:, k, :], start=(k == 0),
                                               stop=(k == KT - 1 and bias is None))
                                if h == m == k == 0:
                                    leave(mm, s)
                            if bias is not None:
                                mm = pe.matmul(o, ones[0:1, :], bias[0:1, s * T:(s + 1) * T], start=False, stop=True)
                        mm.then_inc(sem(full(c, b)), n[full(c, b)].up())

                slots(1, [], body)

            def turn(pieces, b, c):
                take(b, c)
                for k, (piece, off) in enumerate(pieces):
                    r, m = piece.shape[0], piece.shape[1]
                    mm = pe.transpose(psum[0:m, b, off:off + r], piece, ident[0:r, 0:r])
                mm.then_inc(sem(full(c, b)), n[full(c, b)].up())

            def sum_rows(src, b, c, tiles):
                take(b, c)
                for k in range(tiles):
                    mm = pe.matmul(psum[:, b, 0:T], ones[:, :], src[:, k, :], start=(k == 0), stop=(k == tiles - 1))
                mm.then_inc(sem(full(c, b)), n[full(c, b)].up())

            n["consts_ready"].n = 3
            pe.wait_ge(sem("consts_ready"), n["consts_ready"].now())
            n["load_packs"].n = sum(len(p) for p in PACKS)
            pe.wait_ge(sem("load_packs"), n["load_packs"].now())
            for j in range(5):
                rows = sum(r for _, r in PACKS[j])
                turn([(PACK[j][0:rows, :], 0)], j, "dve")
            pe.wait_ge(sem("load_taps"), n["load_taps"].next())
            turn([(TAPN[0:TAPS, j * P:(j + 1) * P], 32 * j) for j in range(HT)], 5, "dve")
            for q, (nat, what) in enumerate(((XN, "load_x"), (CN, "load_ctx"))):
                pe.wait_ge(sem(what), n[what].next())
                for k in range(0, KT, 2):
                    turn([(nat[:, t, (k + m) * P:(k + m + 1) * P], m * T + t * P) for m in range(2) for t in range(2)],
                         (k // 2) % 4, "act")
            pe.wait_ge(sem("cvec_ready"), n["cvec_ready"].next())
            stationary("mod", lambda k: cvec[:, k, :], "dve", N=2)
            for q in range(2):
                pe.wait_ge(sem("squares_ready"), n["squares_ready"].next())
                sum_rows(SQ1, 4 + q, "dve", KT)
            n["normed"].n += 2
            pe.wait_ge(sem("normed"), n["normed"].now())
            stationary("q", lambda k: H[:, k, 0:T], "act")
            stationary("k", lambda k: H[:, k, :], "act", N=2 * T)
            pe.wait_ge(sem("load_vrow"), n["load_vrow"].next())
            token_major("v", lambda k, t: H[:, k, t * P:(t + 1) * P], 4, "act", VROW)
            units = [(h, b) for h in range(2) for b in range(2)]

            def attend(turns, nunits, scores, keys, values, dst_bank):
                per = {n["heads_staged"]: 1, n["probs_ready"]: nunits, n["probs_turned"]: nunits,
                       n[full("dve", dst_bank)]: 1}
                for b in range(2):
                    per[n[full("dve", 4 + b)]] = nunits // 2
                    per[n[full("act", 6 + b)]] = nunits // 2
                with rounds(pe, turns, per):
                    pe.wait_ge(sem("heads_staged"), n["heads_staged"].next())
                    take(dst_bank, "dve")

                    def ahead(u):
                        take(4 + u % 2, "dve")
                        scores(u).then_inc(sem(full("dve", 4 + u % 2)), n[full("dve", 4 + u % 2)].up())

                    ahead(0)
                    for u in range(nunits):
                        if u + 1 < nunits:
                            ahead(u + 1)
                        pe.wait_ge(sem("probs_ready"), n["probs_ready"].next())
                        turn([(keys(u, k), k * P) for k in range(values[0])], 6 + u % 2, "act")
                        pe.wait_ge(sem("probs_turned"), n["probs_turned"].next())
                        for k in range(values[0]):
                            mm = pe.matmul(*values[1](u, k), start=(k == 0), stop=(k == values[0] - 1))
                    mm.then_inc(sem(full("dve", dst_bank)), n[full("dve", dst_bank)].up())

            def na_scores(u):
                h, b = units[u]
                r = slice(64 * h, 64 * h + 64)
                pe.matmul(psum[:, 4 + b, :], ST_Q[r, b * P:(b + 1) * P], ST_K[r, :], start=True, stop=False)
                return pe.matmul(psum[:, 4 + b, 0:T], mirror[:, :], ST_B[:, 2 * h + b, :], start=False,
                                 stop=True)

            def na_values(u, k):
                h, b = units[u]
                return (psum[64 * h:64 * h + 64, 0, b * P:(b + 1) * P], ST_V[:, k, 64 * h:64 * h + 64],
                        PT[b][:, k * P:(k + 1) * P])

            attend(HT, 4, na_scores, lambda u, k: PR[u % 2][:, k * P:(k + 1) * P], (4, na_values), 0)

            def layer_norm(z, sq):
                pe.wait_ge(sem("ln_in"), n["ln_in"].next())
                sum_rows(z, 4, "dve", HT)
                pe.wait_ge(sem("squares_ready"), n["squares_ready"].next())
                sum_rows(sq, 5, "dve", HT)

            hl = lambda k: H[:, k, 0:T]
            stationary("a2", hl, "act")
            stationary("a1", hl, "dve")
            stationary("su", hl, "act")
            stationary("sv", hl, "act")
            n["load_sgu"].n += 2
            pe.wait_ge(sem("load_sgu"), n["load_sgu"].now())
            for q in range(2):
                turn([(SGN[:, 4 * q + g, :], g * P) for g in range(4)], 6 + q, "act")
            layer_norm(ZV, SQ)
            pe.wait_ge(sem("ln_out"), n["ln_out"].next())
            for j in range(0, HT, 2):
                turn([(ZV[:, j + m, t * P:(t + 1) * P], (t * 2 + m) * P) for t in range(2) for m in range(2)],
                     (j // 2) % 4, "act")
            n["sgu_turned"].n += 6
            pe.wait_ge(sem("sgu_turned"), n["sgu_turned"].now())
            for g in range(HT):
                b = g % 4
                take(b, "dve")
                for t in range(2):
                    o = psum[:, b, t * P:(t + 1) * P]
                    pe.matmul(o, VT[:, t, g * P:(g + 1) * P], WST[:, g, :], start=True, stop=False)
                    mm = pe.matmul(o, ident[0:HT, g:g + 1].broadcast_to([HT, P]), SGB[0:HT, :], start=False, stop=True)
                mm.then_inc(sem(full("dve", b)), n[full("dve", b)].up())
            stationary("gate_conv", hl, "act")
            layer_norm(CV, SQ)
            pe.wait_ge(sem("conv_ready"), n["conv_ready"].next())
            stationary("out_conv", lambda k: CV[:, k, :], "dve", kt=8, width=512)
            stationary("gate_sgu", hl, "act")
            pe.wait_ge(sem("sgu_ready"), n["sgu_ready"].next())
            stationary("out_sgu", lambda k: ZU[:, k, :], "dve", kt=8, width=512)
            stationary("gate_att", hl, "act")
            stationary("out_att", lambda k: ATT[:, k, :], "dve", kt=8, width=512)
            pe.wait_ge(sem("mixed"), n["mixed"].next())
            stationary("o", lambda k: MIX[:, k, :], "dve")

            def rms(sq):
                pe.wait_ge(sem("squares_ready"), n["squares_ready"].next())
                sum_rows(sq, 4, "dve", KT)
                pe.wait_ge(sem("normed"), n["normed"].next())

            rms(SQ1)
            stationary("ff1", lambda k: H2[:, k, :], "act")
            pe.wait_ge(sem("hidden_ready"), n["hidden_ready"].next())
            per = {n[f"load_slot{s}"]: 2 for s in range(4)} | {n[full("dve", b)]: 1 for b in range(4)}
            with rounds(pe, ROUNDS["ff2"] // 2, per):
                for g in range(2):
                    for s in range(4):
                        pe.wait_ge(sem(f"load_slot{s}"), n[f"load_slot{s}"].next())
                        w = ring[:, s, :].rearrange("p (k n) -> p k n", k=16)
                        for m in range(2):
                            b = 2 * g + m
                            if s == 0:
                                take(b, "dve")
                            for k in range(16):
                                mm = pe.matmul(psum[:, b, 0:T], w[:, k, m * P:(m + 1) * P], HID[:, 16 * s + k, :],
                                               start=(s == 0 and k == 0), stop=(s == 3 and k == 15))
                                if m == k == 0:
                                    leave(mm, s)
                            if s == 3:
                                mm.then_inc(sem(full("dve", b)), n[full("dve", b)].up())

            rms(SQ1)
            rms(SQ1)
            h2 = lambda k: H2[:, k, :]
            h2t = lambda k, t: H2[:, k, t * P:(t + 1) * P]
            token_major("va", h2t, 2, "act")
            stationary("qa", h2, "act")
            stationary("ka", h2, "act")
            stationary("qkb", h2, "act")
            token_major("vb", h2t, 2, "act")
            n["load_glw"].n += 2
            pe.wait_ge(sem("load_glw"), n["load_glw"].now())
            take(4, "act")
            for k in range(KT):
                mm = pe.matmul(psum[0:16, 4, 0:T], GLW[:, k, :], H2[:, k, :], start=(k == 0), stop=(k == KT - 1))
            mm.then_inc(sem(full("act", 4)), n[full("act", 4)].up())
            stationary("gate_ab", h2, "act")
            pe.wait_ge(sem("low_ready"), n["low_ready"].next())
            for q in range(2):
                take(5 + q, "dve")
                for m in range(2):
                    mm = pe.matmul(psum[:, 5 + q, m * T:(m + 1) * T], GWG[0:16, (2 * q + m) * P:(2 * q + m + 1) * P],
                                   GLO[0:16, :], start=True, stop=True)
                mm.then_inc(sem(full("dve", 5 + q)), n[full("dve", 5 + q)].up())
            attend(HT, 2,
                   lambda u: pe.matmul(psum[:, 4 + u, 0:T], DQ[:, u * P:(u + 1) * P], DK, start=True, stop=True),
                   lambda u, k: DP[u][:, k * P:(k + 1) * P],
                   (2, lambda u, k: (psum[:, 0, u * P:(u + 1) * P], DV[:, k, :], DT_[u][:, k * P:(k + 1) * P])), 0)

            def linear_attention(turns, nv, f):
                per = {n["levels_ready"]: 1, n["head_scores"]: 2}
                for b in (4, 5, 6):
                    per[n[full("dve", b)]] = 4 if b < 6 else 2
                for b in range(nv):
                    per[n[full("dve", b)]] = 1
                with rounds(pe, turns, per):
                    pe.wait_ge(sem("levels_ready"), n["levels_ready"].next())
                    for h in range(2):
                        for b in range(2):
                            o = h * T + b * P
                            for half in range(2):
                                take(4 + half, "dve")
                                for l in range(4):
                                    mm = pe.matmul(psum[:, 4 + half, l * P:(l + 1) * P],
                                                   f["KL"][:, 4 * half + l, o:o + P], f["QL"][:, 4 * half + l, o:o + P],
                                                   start=True, stop=True)
                                mm.then_inc(sem(full("dve", 4 + half)), n[full("dve", 4 + half)].up())
                        take(6, "dve")
                        pe.matmul(psum[:, 6, 0:P], f["KL"][:, LEVELS, h * T:h * T + P],
                                       f["QL"][:, LEVELS, h * T + P:h * T + 2 * P], start=True, stop=True).then_inc(
                            sem(full("dve", 6)), n[full("dve", 6)].up())
                    for h in range(2):
                        pe.wait_ge(sem("head_scores"), n["head_scores"].next())
                        for e in range(nv):
                            tile = h * nv + e
                            bank, o = tile // 2, (tile % 2) * T
                            if tile % 2 == 0:
                                take(bank, "dve")
                            v = lambda t: f["V"][:, t, tile * P:(tile + 1) * P]
                            pe.matmul(psum[:, bank, o:o + P], v(0), f["SC"][:, h, 0, :], start=True, stop=True)
                            pe.matmul(psum[:, bank, o + P:o + 2 * P], v(1), f["SC"][:, h, 1, :], start=True, stop=False)
                            mm = pe.matmul(psum[:, bank, o + P:o + 2 * P], v(0), f["SC"][:, h, 2, :],
                                           start=False, stop=True)
                            if tile % 2 == 1:
                                mm.then_inc(sem(full("dve", bank)), n[full("dve", bank)].up())

            def head_norm(src, heads, each, sq):
                pe.wait_ge(sem("squares_ready"), n["squares_ready"].next())
                for h in range(heads):
                    b = (h // 2) % 4
                    if h % 2 == 0:
                        take(b, "dve")
                    for e in range(each):
                        mm = pe.matmul(psum[:, b, (h % 2) * T:(h % 2 + 1) * T], ones[:, :], sq[:, h * each + e, :],
                                       start=(e == 0), stop=(e == each - 1))
                    if h % 2 == 1:
                        mm.then_inc(sem(full("dve", b)), n[full("dve", b)].up())

            linear_attention(2, 2, GLA)
            head_norm(Y, 4, 2, GLA["SQ"])
            pe.wait_ge(sem("y_ready"), n["y_ready"].next())
            stationary("ab_out", lambda k: Y[:, k, :], "dve")

            rms(SQ1)
            stationary("u", h2, "act")
            n["load_s5"].n += 3
            pe.wait_ge(sem("dt_spread"), n["dt_spread"].next())
            pe.wait_ge(sem("load_s5"), n["load_s5"].now())
            turn([(S5N[0:32, q * P:(q + 1) * P], q * 32) for q in range(3)], 4, "dve")
            for c in range(2):
                pe.wait_ge(sem("b_ready"), n["b_ready"].next())
                for q in range(2):
                    turn([(S5B[:, (4 * q + g) * P:(4 * q + g + 1) * P], g * P) for g in range(4)], 6 + q, "dve")
            n["load_s5c"].n += 4
            pe.wait_ge(sem("load_s5c"), n["load_s5c"].now())
            for c in range(2):
                for q in range(2):
                    turn([((S5C, S5CI)[c][:, 4 * q + g, :], g * P) for g in range(4)], 6 + q, "dve")
            pe.wait_ge(sem("s5_tables"), n["s5_tables"].next())
            for half in range(2):
                for j in range(16):
                    ut, r = half * 4 + j // 4, slice(32 * (j % 4), 32 * (j % 4) + 32)
                    take(j % 4, "act")
                    for c in range(2):
                        mm = pe.matmul(psum[:, j % 4, c * T:(c + 1) * T], BT[r, c, ut, :], SU5[r, ut, :],
                                       start=True, stop=True)
                    mm.then_inc(sem(full("act", j % 4)), n[full("act", j % 4)].up())
                pe.wait_ge(sem("states_ready"), n["states_ready"].next())
                for q in range(4):
                    ut = half * 4 + q
                    b = 4 + q % 2
                    take(b, "dve")
                    for j in range(4):
                        r = slice(32 * j, 32 * j + 32)
                        for c in range(2):
                            mm = pe.matmul(psum[r, b, 0:T], CT[:, c, ut, r], SX[:, c, 4 * q + j, :],
                                           start=(c == 0), stop=(c == 1))
                    mm.then_inc(sem(full("dve", b)), n[full("dve", b)].up())
            pe.wait_ge(sem("s5_gelu"), n["s5_gelu"].next())
            stationary("glu", lambda k: Y5[:, k, :], "act", kt=8)
            stationary("qd", h2, "act")
            stationary("fd", h2, "act")
            token_major("id", h2t, 2, "act")
            stationary("gate_cd", h2, "act")
            linear_attention(4, 1, HG)
            head_norm(Y5, 8, 1, HG["SQ"])
            pe.wait_ge(sem("y_ready"), n["y_ready"].next())
            stationary("cd_out", lambda k: Y5[:, k, :], "dve")
            pe.wait_ge(sem("squares_ready"), n["squares_ready"].next())
            sum_rows(SQ1, 4, "dve", KT)
            pe.wait_ge(sem("normed"), n["normed"].next())
            for t in range(2):
                for k in range(0, KT, 4):
                    turn([(H2[:, k + m, t * P:(t + 1) * P], m * P) for m in range(4)], (k // 4) % 4, "act")

        @block.scalar
        def _(act):
            n = Counts()
            A = act.activation





            def settled(name):
                for b in range(4):
                    act.wait_ge(sem(free("act", b)), n[free("act", b)].now())
                act.sem_inc(sem(name), n[name].up())

            def begin():
                for b in range(8):
                    act.sem_inc(sem(free("act", b)), n[free("act", b)].up())

            def load(dst, src, name):
                act.dma_start(dst, src).then_inc(sem(name), 16)

            def emit(name, fn, nb=1, extra=None):
                per = {}
                for s in range(4):
                    for h in range(nb):
                        b = (s * nb + h) % 4
                        per[n[full("act", b)]] = per.get(n[full("act", b)], 0) + 1
                for k, v in (extra or {}).items():
                    per[n[k]] = v

                def body(i):
                    for s in range(4):
                        for h in range(nb):
                            b = (s * nb + h) % 4
                            act.wait_ge(sem(full("act", b)), n[full("act", b)].next())
                            fn(i, s, h, b)

                if ROUNDS[name] == 1:
                    body(0)
                else:
                    with rounds(act, ROUNDS[name], per) as i:
                        body(i)

            begin()
            first = True
            for j in (3, 1, 0, 2, 4):
                r0 = 0
                for name, rows in PACKS[j]:
                    src = dram[name]
                    load(PACK[j][r0:r0 + rows, :], src.rearrange("(r p) -> r p", p=P), "load_packs")
                    r0 += rows
            load(XN, dram["x"].rearrange("(t p) n -> p t n", p=P), "load_x")
            load(CN, dram["ctx"].rearrange("(t p) n -> p t n", p=P), "load_ctx")
            load(TAPN[0:TAPS, :], dram["conv_w"], "load_taps")
            load(VROW[0:1, :], dram["b_in"][WV:WV + HW].rearrange("(a n) -> a n", a=1), "load_vrow")
            for q in range(2):
                for k in range(0, KT, 2):
                    b = (k // 2) % 4
                    act.wait_ge(sem(full("act", b)), n[full("act", b)].next())
                    src = psum[:, b, :].rearrange("p (a t) -> p a t", a=2)
                    dst = X[:, k:k + 2, :] if q == 0 else H[:, k:k + 2, T:2 * T]
                    ins = act.activation(dst, src, ACT.Copy)
                    ins.then_inc(sem(free("act", b)), n[free("act", b)].up())
            settled("x_turned")
            act.wait_ge(sem("packs_turned"), n["packs_turned"].next())
            for q, name in enumerate(("c", "c_ctx")):
                ins = A(cvec[:, :, q], col(name, 0, KT), ACT.Silu)
                if q == 0:
                    ins.then_inc(sem("scalar_step"), n["scalar_step"].up())
                    act.wait_ge(sem("scalar_step"), n["scalar_step"].now())
                else:
                    ins.then_inc(sem("cvec_ready"), n["cvec_ready"].up())

            def root(what=RS):
                act.wait_ge(sem("norm_var"), n["norm_var"].next())
                A(what, what, ACT.Sqrt).then_inc(sem("norm_std"), n["norm_std"].up())

            root()
            root()
            act.wait_ge(sem("bq_ready"), n["bq_ready"].next())

            def q_out(i, s, h, b):
                for m in range(2):
                    k = 2 * s + m
                    ins = A(NQ[:, k, :], psum[:, b, m * T:(m + 1) * T], ACT.Identity, bias=bq[:, k:k + 1], scale=0.125)
                ins.then_inc(sem(free("act", b)), n[free("act", b)].up())

            def k_out(i, s, h, b):
                k = 2 * s + h
                A(NK[:, k, :], psum[:, b, :], ACT.Identity, bias=col("b_in", WK // P + k)).then_inc(
                    sem(free("act", b)), n[free("act", b)].up())

            def tokens(dst):
                def fn(i, s, h, b):
                    A(dst[:, 2 * h:2 * h + 2, s * T:(s + 1) * T],
                              psum[:, b, :].rearrange("p (t c) -> p t c", t=2), ACT.Copy).then_inc(
                        sem(free("act", b)), n[free("act", b)].up())
                return fn

            def tiles(dst, func, bias=None, scale=lambda s: 1.0, before=None):
                def fn(i, s, h, b):
                    if bias is None:
                        ins = A(dst[:, ds(i * 8 + 2 * s, 2), :], psum[:, b, :].rearrange("p (m t) -> p m t", m=2), func,
                                scale=scale(s))
                    else:
                        for m in range(2):
                            ins = A(dst[:, ds(i * 8 + 2 * s + m, 1), :], psum[:, b, m * T:(m + 1) * T], func,
                                    bias=cols[:, ds(i * 8 + (COL[bias[0]] + bias[1] + 2 * s + m), 1)])
                    ins.then_inc(sem(free("act", b)), n[free("act", b)].up())
                return fn

            emit("q", q_out)
            emit("k", k_out, nb=2)
            emit("v", tokens(NV), nb=2)
            settled("qkv_ready")

            def softmax_rounds(turns, nunits, probs, turned, width):
                per = {n["scores_max"]: nunits, n["exp_done"]: nunits, n["probs_turned"]: nunits}
                for b in range(2):
                    per[n[full("act", 6 + b)]] = nunits // 2
                    per[n[free("act", 6 + b)]] = nunits // 2
                with rounds(act, turns, per):
                    def exp(u):
                        act.wait_ge(sem("scores_max"), n["scores_max"].next())
                        kw = dict(accum_out=small[:, 4 + u % 2:5 + u % 2]) if width == 512 else {}
                        A(probs[u % 2], psum[:, 4 + u % 2, 0:width], ACT.Exp,
                                           bias=small[:, 2 + u % 2:3 + u % 2], **kw).then_inc(
                            sem("exp_done"), n["exp_done"].up())

                    exp(0)
                    for u in range(nunits):
                        if u + 1 < nunits:
                            exp(u + 1)
                        b = 6 + u % 2
                        act.wait_ge(sem(full("act", b)), n[full("act", b)].next())
                        A(turned[u % 2], psum[:, b, 0:width], ACT.Copy).then_inc(
                            sem("probs_turned"), n["probs_turned"].up())
                        act.wait_ge(sem("probs_turned"), n["probs_turned"].now())
                        act.sem_inc(sem(free("act", b)), n[free("act", b)].up())

            softmax_rounds(HT, 4, PR, PT, 512)
            act.wait_ge(sem("att_ready"), n["att_ready"].next())
            load(SGN, dram["sgu_w"].rearrange("g p q -> p g q"), "load_sgu")
            load(SGB[0:HT, :], dram["sgu_b"], "load_sgu")
            emit("a2", tiles(CV, ACT.Sigmoid, ("b_in", A2 // P)))
            settled("sig_ready")
            emit("su", tiles(ZU, ACT.Gelu_apprx_tanh, ("b_in", SU // P)))
            emit("sv", tiles(ZV, ACT.Gelu_apprx_tanh, ("b_in", SV // P)))
            settled("uv_ready")
            for q in range(2):
                act.wait_ge(sem(full("act", 6 + q)), n[full("act", 6 + q)].next())
                ins = A(WST[:, 4 * q:4 * q + 4, :], psum[:, 6 + q, :].rearrange("p (g q) -> p g q", g=4), ACT.Copy)
                ins.then_inc(sem("sgu_turned"), n["sgu_turned"].up())
                act.wait_ge(sem("sgu_turned"), n["sgu_turned"].now())
                act.sem_inc(sem(free("act", 6 + q)), n[free("act", 6 + q)].up())
            root()
            for j in range(0, HT, 2):
                b = (j // 2) % 4
                act.wait_ge(sem(full("act", b)), n[full("act", b)].next())
                ins = A(VT[:, :, j * P:(j + 2) * P], psum[:, b, :].rearrange("p (t m) -> p t m", t=2), ACT.Copy)
                ins.then_inc(sem("sgu_turned"), n["sgu_turned"].up())
                act.wait_ge(sem("sgu_turned"), n["sgu_turned"].now())
                act.sem_inc(sem(free("act", b)), n[free("act", b)].up())

            def gate(name, k0):
                emit(name, tiles(GATE, ACT.Sigmoid, ("b_in", (WG + k0) // P)),
                     extra={free("act", b): 1 for b in range(4)})
                settled("gate_ready")

            gate("gate_conv", 0)
            root()
            act.wait_ge(sem("conv_normed"), n["conv_normed"].next())
            ins = A(CV, CV, ACT.Silu)
            ins.then_inc(sem("conv_ready"), n["conv_ready"].up())
            act.wait_ge(sem("gate_used"), n["gate_used"].next())
            gate("gate_sgu", D)
            act.wait_ge(sem("gate_used"), n["gate_used"].next())
            gate("gate_att", 2 * D)
            root()
            act.wait_ge(sem("gate_used"), n["gate_used"].next())
            load(GLW, dram["ab_w_in_2"][:, GLOW:GLOW + 16].rearrange("(k p) c -> p k c", p=P), "load_glw")
            load(GWG[0:16, :], dram["gla_w_gate_2"], "load_glw")

            def ff1(i, s, h, b):
                for m in range(2):
                    ins = A(HID[:, ds(i * 8 + 2 * s + m, 1), :], psum[:, b, m * T:(m + 1) * T], ACT.Relu,
                            bias=cols[:, ds(i * 8 + (COL["b_ff1"] + 2 * s + m), 1)])
                ins.then_inc(sem(free("act", b)), n[free("act", b)].up())
                act.wait_ge(sem(free("act", b)), n[free("act", b)].now())
                act.sem_inc(sem("hidden_raw"), n["hidden_raw"].up())

            emit("ff1", ff1, extra={**{free("act", b): 1 for b in range(4)}, "hidden_raw": 4})
            root()
            root()
            emit("va", tokens(VA))
            emit("qa", tiles(QA, ACT.Copy, scale=lambda s: float(P) ** -0.5))
            emit("ka", tiles(KA, ACT.Copy))
            emit("qkb", tiles(QKB, ACT.Copy, scale=lambda s: float(P) ** -0.5 if s < 2 else 1.0))
            emit("vb", tokens(VB))
            act.wait_ge(sem(full("act", 4)), n[full("act", 4)].next())
            A(GLO[0:16, :], psum[0:16, 4, 0:T], ACT.Copy).then_inc(sem("low_ready"), n["low_ready"].up())
            act.wait_ge(sem("low_ready"), n["low_ready"].now())
            act.sem_inc(sem(free("act", 4)), n[free("act", 4)].up())
            emit("gate_ab", tiles(GATE2, ACT.Silu), extra={free("act", b): 1 for b in range(4)})
            settled("ab_ready")
            act.wait_ge(sem("decay_in"), n["decay_in"].next())
            A(GTMP, GTMP, ACT.Exp, scale=-1.0).then_inc(sem("scalar_step"), n["scalar_step"].up())
            act.wait_ge(sem("scalar_step"), n["scalar_step"].now())
            A(GTMP, GTMP, ACT.Ln, bias=1.0).then_inc(sem("decay_ln"), n["decay_ln"].up())
            act.wait_ge(sem("decay_in"), n["decay_in"].next())
            A(GG, GG3, ACT.Exp, scale=-1.0 / 16.0).then_inc(sem("decay_exp"), n["decay_exp"].up())
            softmax_rounds(HT, 2, DP, DT_, 256)
            root(GLA["SQ"][:, 0:4, :])
            root()
            act.wait_ge(sem("y_used"), n["y_used"].next())
            load(S5N[0:32, 0:P], dram["s5_lam_re_2"].rearrange("(j a) p -> j (a p)", a=2), "load_s5")
            load(S5N[0:32, P:2 * P], dram["s5_lam_im_2"].rearrange("(j a) p -> j (a p)", a=2), "load_s5")
            load(S5DT[0:32, :], dram["s5_log_dt_2"].rearrange("(j a) -> j a", a=2), "load_s5")
            for q, name in enumerate(("s5_b_re_2", "s5_b_im_2")):
                load(S5BN[:, q, :, :], dram[name].rearrange("(j a) p h -> (a p) j h", a=2), "load_s5b")
            for q, name in enumerate(("s5_c_re_2", "s5_c_im_2")):
                for r in range(2):
                    load((S5C, S5CI)[q][:, :, r * 64:r * 64 + 64],
                         dram[name].rearrange("(u g) h p -> (g h) u p", g=8), "load_s5c")
            emit("u", tiles(SU5, ACT.Copy))
            settled("u_ready")
            act.wait_ge(sem("s5_dt"), n["s5_dt"].next())
            A(s5p[:, 2, :], s5p[:, 2, :], ACT.Exp).then_inc(sem("s5_act"), n["s5_act"].up())
            act.wait_ge(sem("s5_dt"), n["s5_dt"].next())
            A(s5p[:, 3, :], s5p[:, 3, :], ACT.Exp).then_inc(sem("scalar_step"), n["scalar_step"].up())
            act.wait_ge(sem("scalar_step"), n["scalar_step"].now())
            A(s5p[:, 5, :], s5p[:, 5, :], ACT.Sin).then_inc(sem("scalar_step"), n["scalar_step"].up())
            act.wait_ge(sem("scalar_step"), n["scalar_step"].now())
            A(s5p[:, 4, :], s5p[:, 4, :], ACT.Sin).then_inc(sem("s5_act"), n["s5_act"].up())
            for half in range(2):
                for j in range(16):
                    act.wait_ge(sem(full("act", j % 4)), n[full("act", j % 4)].next())
                    if j == 0 and half == 1:
                        act.wait_ge(sem("half_done"), n["half_done"].next())
                    A(SX[:, :, j, :], psum[:, j % 4, :].rearrange("p (c t) -> p c t", c=2), ACT.Copy).then_inc(
                        sem(free("act", j % 4)), n[free("act", j % 4)].up())
                settled("inputs_ready")
            act.wait_ge(sem("s5_sum"), n["s5_sum"].next())
            A(Y5[:, 0:HT, :], Y5[:, 0:HT, :], ACT.Gelu_apprx_tanh).then_inc(sem("s5_gelu"), n["s5_gelu"].up())
            emit("glu", tiles(QD, ACT.Sigmoid, ("s5_b_glu_2", 0)))
            settled("glu_ready")
            act.wait_ge(sem("glu_used"), n["glu_used"].next())
            emit("qd", tiles(QD, ACT.Silu))
            emit("fd", tiles(FD, ACT.Sigmoid))
            emit("id", tokens(ID))
            emit("gate_cd", tiles(GATE3, ACT.Silu), extra={free("act", b): 1 for b in range(4)})
            settled("cd_ready")
            act.wait_ge(sem("gamma_in"), n["gamma_in"].next())
            A(small[:, 0:16], small[:, 0:16], ACT.Exp).then_inc(sem("gamma_exp"), n["gamma_exp"].up())
            root(HG["SQ"])
            root()
            OUTB = at(12288, 2, D)
            act.wait_ge(sem("y_used"), n["y_used"].next())
            for t in range(2):
                for k in range(0, KT, 4):
                    b = (k // 4) % 4
                    act.wait_ge(sem(full("act", b)), n[full("act", b)].next())
                    A(OUTB[:, t, k * P:(k + 4) * P], psum[:, b, :], ACT.Copy).then_inc(
                        sem(free("act", b)), n[free("act", b)].up())
            for b in range(4):
                act.wait_ge(sem(free("act", b)), n[free("act", b)].now())
            act.sem_inc(sem("result_ready"), 1)

        @block.gpsimd
        def _(pool):
            n = Counts()


            pool.memset(ident[:, :], 0.0).then_inc(sem("pool_step"), n["pool_step"].up())
            pool.wait_ge(sem("pool_step"), n["pool_step"].now())
            pool.memset(ones[:, :], 1.0).then_inc(sem("consts_ready"), n["consts_ready"].up())
            pool.wait_ge(sem("consts_ready"), n["consts_ready"].now())
            pool.affine_select(out=ident[:, :], in_=ident[:, :], compare_op=ALU.not_equal, fill=1.0, base=0,
                                  pattern=[[-1, P]], channel_multiplier=1).then_inc(
                sem("consts_ready"), n["consts_ready"].up())
            pool.wait_ge(sem("consts_ready"), n["consts_ready"].now())
            pool.memset(mirror[:, :], 0.0).then_inc(sem("pool_step"), n["pool_step"].up())
            pool.wait_ge(sem("pool_step"), n["pool_step"].now())
            for r in range(2):
                q = slice(64 * r, 64 * r + 64)
                pool.affine_select(out=mirror[q, q], in_=mirror[q, q], compare_op=ALU.not_equal, fill=1.0,
                                      base=1 - GRID, pattern=[[1, 64]], channel_multiplier=1).then_inc(
                    sem("pool_step" if r == 0 else "consts_ready"), n["pool_step" if r == 0 else "consts_ready"].up())
                pool.wait_ge(sem("pool_step" if r == 0 else "consts_ready"), n["pool_step" if r == 0 else "consts_ready"].now())
            pool.memset(padrow[:, :, :], 0.0).then_inc(sem("pool_step"), n["pool_step"].up())
            pool.wait_ge(sem("pool_step"), n["pool_step"].now())
            pool.dma_start(padrow[:, :, 48:48 + DCS],
                           dram["na_rpb"].rearrange("h d k -> (h d) k").rearrange("(p a) k -> p a k", a=2)).then_inc(
                sem("load_rpb"), 16)
            pool.wait_ge(sem("load_rpb"), 16)
            pool.dma_start(bias_rows.rearrange("h d k -> (h d) k").rearrange("(p a) k -> p a k", a=2),
                           padrow[:, :, :]).then_inc(sem("load_rows"), 16)
            pool.wait_ge(sem("load_rows"), 16)
            for h in range(NHEAD):
                for r in range(2):
                    src = bass.AP(bias_rows.tensor, h * DRS * PADW + (5 - r) * PADW,
                                  [[1, GRID], [PADW, 6], [1, GRID]])
                    pool.dma_start(BIAS[64 * r:64 * r + 64, h, :, :], src).then_inc(sem("load_bias"), 16)
            pool.memset(WMASK, 0.0).then_inc(sem("pool_step"), n["pool_step"].up())
            pool.wait_ge(sem("pool_step"), n["pool_step"].now())
            for r in range(2):
                q = slice(64 * r, 64 * r + 64)
                pool.affine_select(out=WMASK[q, 0:48], in_=WMASK[q, 0:48], compare_op=ALU.is_ge, fill=NEG,
                                      base=WIN // 2 - (GRID - 1), pattern=[[1, 48]], channel_multiplier=1).then_inc(
                    sem("pool_step"), n["pool_step"].up())
                pool.wait_ge(sem("pool_step"), n["pool_step"].now())
                pool.affine_select(out=WMASK[q, 16:64], in_=WMASK[q, 16:64], compare_op=ALU.is_ge, fill=NEG,
                                      base=WIN // 2 - 1 - 16 + GRID - 1, pattern=[[-1, 48]], channel_multiplier=-1).then_inc(
                    sem("pool_step" if r == 0 else "window_mask"), n["pool_step" if r == 0 else "window_mask"].up())
                pool.wait_ge(sem("pool_step" if r == 0 else "window_mask"), n["pool_step" if r == 0 else "window_mask"].now())
            n["gate_used"].n = 3
            pool.wait_ge(sem("gate_used"), n["gate_used"].now())
            pool.iota(DIFF, pattern=[[P, 2], [-1, T]], base=0, channel_multiplier=1).then_inc(
                sem("iotas"), n["iotas"].up())
            pool.wait_ge(sem("iotas"), n["iotas"].now())
            pool.iota(IDX[:, 0, :], pattern=[[1, P]], base=0, channel_multiplier=0).then_inc(
                sem("iotas"), n["iotas"].up())
            pool.wait_ge(sem("iotas"), n["iotas"].now())
            pool.iota(IDX[:, 1, :], pattern=[[0, P]], base=0, channel_multiplier=1).then_inc(
                sem("iotas"), n["iotas"].up())
            pool.wait_ge(sem("iotas"), n["iotas"].now())
            pool.iota(IDX[:, 2, :], pattern=[[1, P]], base=0, channel_multiplier=-1).then_inc(
                sem("iotas"), n["iotas"].up())
            pool.wait_ge(sem("iotas"), n["iotas"].now())

        @block.vector
        def _(v):
            n = Counts()





            for b in range(8):
                v.sem_inc(sem(free("dve", b)), 1)
                n[free("dve", b)].n = 1

            def evac(name, fn, nb=1, steps=0, extra=None):
                per = {n["vector_step"]: steps}
                for s in range(4):
                    for h in range(nb):
                        for f in (full, free):
                            c = n[f("dve", (s * nb + h) % 4)]
                            per[c] = per.get(c, 0) + 1
                for k, q in (extra or {}).items():
                    per[n[k]] = q

                def body(i):
                    for s in range(4):
                        for h in range(nb):
                            b = (s * nb + h) % 4
                            v.wait_ge(sem(full("dve", b)), n[full("dve", b)].next())
                            fn(i, s, h, b)

                if ROUNDS[name] == 1:
                    body(0)
                else:
                    with rounds(v, ROUNDS[name], per) as i:
                        body(i)

            for j in range(5):
                v.wait_ge(sem(full("dve", j)), n[full("dve", j)].next())
                rows = sum(r for _, r in PACKS[j])
                v.tensor_copy(cols[:, j * P:j * P + rows], psum[:, j, 0:rows]).then_inc(
                    sem(free("dve", j)), n[free("dve", j)].up())
                v.wait_ge(sem(free("dve", j)), n[free("dve", j)].now())
            v.sem_inc(sem("packs_turned"), n["packs_turned"].up())
            v.wait_ge(sem(full("dve", 5)), n[full("dve", 5)].next())
            v.tensor_copy(taps[:, :, 0:TAPS], psum[:, 5, 0:256].rearrange("p (a b) -> p a b", a=HT)[:, :, 0:TAPS]).then_inc(
                sem(free("dve", 5)), n[free("dve", 5)].up())
            v.wait_ge(sem(free("dve", 5)), n[free("dve", 5)].now())

            def mod_out(i, s, h, b):
                v.tensor_tensor(mod[:, ds(i * 8 + 2 * s, 2), :],
                                        psum[:, b, 0:4].rearrange("p (a c) -> p a c", a=2),
                                        over(cols[:, ds(i * 8 + (COL["b_mod"] + 2 * s), 2)], 2, 2), ALU.add).then_inc(
                    sem(free("dve", b)), n[free("dve", b)].up())
                v.wait_ge(sem(free("dve", b)), n[free("dve", b)].now())

            evac("mod", mod_out)
            for g, (m0, q, name) in enumerate(((16, 0, "norm1_g"), (16, 1, "norm1_g"), (64, 0, "norm2_g"))):
                v.scalar_tensor_tensor(out=gain[:, g, :], in0=mod[:, m0:m0 + KT, q], scalar=1.0, in1=col(name, 0, KT),
                                          op0=ALU.add, op1=ALU.mult).then_inc(
                    sem("vector_step"), n["vector_step"].up())
                v.wait_ge(sem("vector_step"), n["vector_step"].now())
            v.tensor_scalar(bq[:, :], col("b_in", WQ // P, HT), 0.125, None, ALU.mult).then_inc(
                sem("bq_ready"), n["bq_ready"].up())
            v.wait_ge(sem("bq_ready"), n["bq_ready"].now())

            def finish_root(b, count):
                v.wait_ge(sem(full("dve", b)), n[full("dve", b)].next())
                v.tensor_scalar(RS, psum[:, b, 0:T], 1.0 / count, EPS, ALU.mult, ALU.add).then_inc(
                    sem("norm_var"), n["norm_var"].up())
                v.wait_ge(sem("norm_var"), n["norm_var"].now())
                v.wait_ge(sem("norm_std"), n["norm_std"].next())
                v.reciprocal(RS, RS).then_inc(sem(free("dve", b)), n[free("dve", b)].up())
                v.wait_ge(sem(free("dve", b)), n[free("dve", b)].now())

            def rms_norm(src, dst, sq, b, a, shift, tiles=KT):
                v.tensor_tensor(sq, src, src, ALU.mult).then_inc(sem("squares_ready"), n["squares_ready"].up())
                v.wait_ge(sem("squares_ready"), n["squares_ready"].now())
                finish_root(b, tiles * P)
                v.tensor_tensor(dst, src, over(RS, tiles), ALU.mult).then_inc(
                    sem("vector_step"), n["vector_step"].up())
                v.wait_ge(sem("vector_step"), n["vector_step"].now())
                for k in range(tiles):
                    if shift is None:
                        ins = v.tensor_scalar(dst[:, k, :], dst[:, k, :], a(k), None, ALU.mult)
                    else:
                        ins = v.tensor_scalar(dst[:, k, :], dst[:, k, :], a(k), shift(k), ALU.mult, ALU.add)
                ins.then_inc(sem("normed"), n["normed"].up())
                v.wait_ge(sem("normed"), n["normed"].now())

            v.wait_ge(sem("x_turned"), n["x_turned"].next())
            for q, src in enumerate((X, H[:, :, T:2 * T])):
                rms_norm(src, H[:, :, q * T:(q + 1) * T], SQ1, 4 + q, lambda k: gain[:, q, k:k + 1],
                         lambda k: mod[:, k, q:q + 1])
            n["load_bias"].n += 32
            v.wait_ge(sem("load_bias"), n["load_bias"].now())
            v.wait_ge(sem("window_mask"), n["window_mask"].next())
            bv = at(24576, NHEAD * 6, GRID)
            v.tensor_tensor(bv, bv, over(WMASK, NHEAD * 6), ALU.add).then_inc(
                sem("vector_step"), n["vector_step"].up())
            v.wait_ge(sem("vector_step"), n["vector_step"].now())
            v.wait_ge(sem("qkv_ready"), n["qkv_ready"].next())

            def softmax_rounds(turns, nunits, stage, add, weigh, probs, dst, dst_bank, steps, width):
                per = {n["vector_step"]: steps, n["scores_max"]: nunits, n["exp_done"]: nunits,
                       n["probs_ready"]: nunits, n["heads_staged"]: 1, n[full("dve", dst_bank)]: 1,
                       n[free("dve", dst_bank)]: 1}
                for b in range(2):
                    per[n[full("dve", 4 + b)]] = nunits // 2
                    per[n[free("dve", 4 + b)]] = nunits // 2
                with rounds(v, turns, per) as i:
                    stage(i)

                    def top(u):
                        b = 4 + u % 2
                        v.wait_ge(sem(full("dve", b)), n[full("dve", b)].next())
                        add(i, u, b)
                        v.tensor_reduce(small[:, u % 2:u % 2 + 1], psum[:, b, 0:width], AX_X, ALU.max).then_inc(
                            sem("vector_step"), n["vector_step"].up())
                        v.wait_ge(sem("vector_step"), n["vector_step"].now())
                        v.tensor_scalar(small[:, 2 + u % 2:3 + u % 2], small[:, u % 2:u % 2 + 1], -1.0, None,
                                           ALU.mult).then_inc(sem("scores_max"), n["scores_max"].up())
                        v.wait_ge(sem("scores_max"), n["scores_max"].now())

                    top(0)
                    for u in range(nunits):
                        if u + 1 < nunits:
                            top(u + 1)
                        v.wait_ge(sem("exp_done"), n["exp_done"].next())
                        weigh(u)
                        v.reciprocal(small[:, 6 + u % 2:7 + u % 2], small[:, 4 + u % 2:5 + u % 2]).then_inc(
                            sem(free("dve", 4 + u % 2)), n[free("dve", 4 + u % 2)].up())
                        v.wait_ge(sem(free("dve", 4 + u % 2)), n[free("dve", 4 + u % 2)].now())
                        v.tensor_scalar(probs[u % 2], probs[u % 2], small[:, 6 + u % 2:7 + u % 2], None, ALU.mult).then_inc(
                            sem("probs_ready"), n["probs_ready"].up())
                        v.wait_ge(sem("probs_ready"), n["probs_ready"].now())
                    v.wait_ge(sem(full("dve", dst_bank)), n[full("dve", dst_bank)].next())
                    v.tensor_copy(dst[:, ds(i, 1), :], psum[:, dst_bank, 0:T]).then_inc(
                        sem(free("dve", dst_bank)), n[free("dve", dst_bank)].up())
                    v.wait_ge(sem(free("dve", dst_bank)), n[free("dve", dst_bank)].now())

            def na_stage(i):
                v.tensor_copy(ST_Q, NQ[:, ds(i, 1), :])
                v.tensor_copy(ST_K, NK[:, ds(i, 1), :])
                for b in range(2):
                    v.tensor_copy(ST_B[:, b:b + 3:2, :].rearrange("p h (k c) -> p h k c", k=4),
                                  BIAS[:, ds(2 * i, 2), 2 - 2 * b:6 - 2 * b, :])
                v.tensor_copy(ST_V, NV[:, :, ds(i * P, P)]).then_inc(sem("heads_staged"), n["heads_staged"].up())
                v.wait_ge(sem("heads_staged"), n["heads_staged"].now())

            softmax_rounds(HT, 4, na_stage, lambda i, u, b: None, lambda u: None, PR, ATT, 0, 4, 512)
            v.sem_inc(sem("att_ready"), n["att_ready"].up())
            v.memset(U[:, :, 0:PAD], 0.0)
            v.memset(U[:, :, T + PAD:T + 2 * PAD], 0.0).then_inc(sem("vector_step"), n["vector_step"].up())
            v.wait_ge(sem("vector_step"), n["vector_step"].now())
            v.wait_ge(sem("sig_ready"), n["sig_ready"].next())

            def glu_in(i, s, h, b):
                for m in range(2):
                    k = 2 * s + m
                    ins = v.scalar_tensor_tensor(out=U[:, k, PAD:PAD + T], in0=psum[:, b, m * T:(m + 1) * T],
                                                 scalar=col("b_in", A1 // P + k), in1=CV[:, k, :], op0=ALU.add,
                                                 op1=ALU.mult)
                ins.then_inc(sem(free("dve", b)), n[free("dve", b)].up())
                v.wait_ge(sem(free("dve", b)), n[free("dve", b)].now())

            evac("a1", glu_in)

            def layer_norm(z, sq, g, b_):
                v.sem_inc(sem("ln_in"), n["ln_in"].up())
                v.wait_ge(sem(full("dve", 4)), n[full("dve", 4)].next())
                v.tensor_scalar(MEAN, psum[:, 4, 0:T], 1.0 / HW, None, ALU.mult).then_inc(
                    sem(free("dve", 4)), n[free("dve", 4)].up())
                v.wait_ge(sem(free("dve", 4)), n[free("dve", 4)].now())
                v.tensor_tensor(z, z, over(MEAN, HT), ALU.subtract).then_inc(
                    sem("vector_step"), n["vector_step"].up())
                v.wait_ge(sem("vector_step"), n["vector_step"].now())
                v.tensor_tensor(sq, z, z, ALU.mult).then_inc(sem("squares_ready"), n["squares_ready"].up())
                v.wait_ge(sem("squares_ready"), n["squares_ready"].now())
                finish_root(5, HW)
                v.tensor_tensor(z, z, over(RS, HT), ALU.mult).then_inc(sem("vector_step"), n["vector_step"].up())
                v.wait_ge(sem("vector_step"), n["vector_step"].now())
                for k in range(HT):
                    ins = v.tensor_scalar(z[:, k, :], z[:, k, :], col(g, k), col(b_, k), ALU.mult, ALU.add)
                ins.then_inc(sem("vector_step"), n["vector_step"].up())
                v.wait_ge(sem("vector_step"), n["vector_step"].now())

            v.wait_ge(sem("uv_ready"), n["uv_ready"].next())
            layer_norm(ZV, SQ, "sgu_ln_g", "sgu_ln_b")
            v.sem_inc(sem("ln_out"), n["ln_out"].up())
            for g in range(HT):
                b = g % 4
                v.wait_ge(sem(full("dve", b)), n[full("dve", b)].next())
                v.tensor_tensor(ZU[:, g, :], ZU[:, g, :], psum[:, b, 0:T], ALU.mult).then_inc(
                    sem(free("dve", b)), n[free("dve", b)].up())
                v.wait_ge(sem(free("dve", b)), n[free("dve", b)].now())
            v.sem_inc(sem("sgu_ready"), n["sgu_ready"].up())
            for k in range(HT):
                v.tensor_scalar(CV[:, k, :], U[:, k, 0:T], taps[:, k, 0:1], col("conv_b", k), ALU.mult,
                                        ALU.add).then_inc(sem("vector_step"), n["vector_step"].up())
            with rounds(v, TAPS - 1, {n["vector_step"]: HT}) as j:
                for k in range(HT):
                    v.wait_ge(sem("vector_step"), n["vector_step"].now(1 - HT))
                    v.scalar_tensor_tensor(out=CV[:, k, :], in0=U[:, k, ds(j + 1, T)],
                                                   scalar=taps[:, k, ds(j + 1, 1)], in1=CV[:, k, :], op0=ALU.mult,
                                                   op1=ALU.add).then_inc(sem("vector_step"), n["vector_step"].up())
            v.wait_ge(sem("vector_step"), n["vector_step"].now())
            layer_norm(CV, SQ, "conv_ln_g", "conv_ln_b")
            v.sem_inc(sem("conv_normed"), n["conv_normed"].up())

            def branch(name, first):
                v.wait_ge(sem("gate_ready"), n["gate_ready"].next())

                def fn(i, s, h, b):
                    k = 4 * s + 2 * h
                    p = psum[:, b, :].rearrange("p (m t) -> p m t", m=2)
                    g = GATE[:, k:k + 2, :]
                    m = MIX[:, k:k + 2, :]
                    if first:
                        v.tensor_tensor(m, p, g, ALU.mult).then_inc(sem(free("dve", b)), n[free("dve", b)].up())
                        v.wait_ge(sem(free("dve", b)), n[free("dve", b)].now())
                    else:
                        v.tensor_tensor(g, p, g, ALU.mult).then_inc(sem(free("dve", b)), n[free("dve", b)].up())
                        v.wait_ge(sem(free("dve", b)), n[free("dve", b)].now())
                        v.tensor_tensor(m, m, g, ALU.add).then_inc(sem("vector_step"), n["vector_step"].up())
                        v.wait_ge(sem("vector_step"), n["vector_step"].now())

                evac(name, fn, nb=2)
                v.sem_inc(sem("gate_used"), n["gate_used"].up())

            branch("out_conv", True)
            branch("out_sgu", False)
            branch("out_att", False)
            v.sem_inc(sem("mixed"), n["mixed"].up())

            def residual(m0, bias):
                def fn(i, s, h, b):
                    for m in range(2):
                        k = i * 8 + 2 * s + m
                        ins = v.tensor_scalar(TMP[:, m, :], psum[:, b, m * T:(m + 1) * T],
                                              cols[:, ds(i * 8 + (COL[bias] + 2 * s + m), 1)],
                                              mod[:, ds(i * 8 + (m0 + 2 * s + m), 1), 0:1].rearrange("p a b -> p (a b)"),
                                              ALU.add, ALU.mult)
                    ins.then_inc(sem(free("dve", b)), n[free("dve", b)].up())
                    v.wait_ge(sem(free("dve", b)), n[free("dve", b)].now())
                    x = X[:, ds(i * 8 + 2 * s, 2), :]
                    v.tensor_tensor(x, x, TMP, ALU.add).then_inc(sem("vector_step"), n["vector_step"].up())
                    v.wait_ge(sem("vector_step"), n["vector_step"].now())
                return fn

            evac("o", residual(32, "b_o"), steps=4)
            rms_norm(X, H2, SQ1, 4, lambda k: gain[:, 2, k:k + 1], lambda k: mod[:, 48 + k, 0:1])
            with rounds(v, ROUNDS["ff1"], {n["hidden_raw"]: 4, n["vector_step"]: 4}) as i:
                for s in range(4):
                    v.wait_ge(sem("hidden_raw"), n["hidden_raw"].next())
                    z = HID[:, ds(i * 8 + 2 * s, 2), :]
                    v.tensor_tensor(z, z, z, ALU.mult).then_inc(sem("vector_step"), n["vector_step"].up())
                    v.wait_ge(sem("vector_step"), n["vector_step"].now())
            v.sem_inc(sem("hidden_ready"), n["hidden_ready"].up())
            per = {n["vector_step"]: 4} | {n[f("dve", b)]: 1 for f in (full, free) for b in range(4)}
            with rounds(v, ROUNDS["ff2"] // 2, per) as i:
                for q in range(4):
                    v.wait_ge(sem(full("dve", q)), n[full("dve", q)].next())
                    v.tensor_scalar(TMP2, psum[:, q, 0:T], cols[:, ds(i * 4 + (COL["b_ff2"] + q), 1)],
                                            mod[:, ds(i * 4 + (80 + q), 1), 0:1].rearrange("p a b -> p (a b)"),
                                            ALU.add, ALU.mult).then_inc(sem(free("dve", q)), n[free("dve", q)].up())
                    v.wait_ge(sem(free("dve", q)), n[free("dve", q)].now())
                    x = X[:, ds(i * 4 + q, 1), :].rearrange("p a t -> p (a t)")
                    v.tensor_tensor(x, x, TMP2, ALU.add).then_inc(sem("vector_step"), n["vector_step"].up())
                    v.wait_ge(sem("vector_step"), n["vector_step"].now())

            rms_norm(X, X, SQ1, 4, lambda k: col("final_g", k), None)
            rms_norm(X, H2, SQ1, 4, lambda k: col("norm_g_2", k), None)
            n["iotas"].n += 4
            v.wait_ge(sem("iotas"), n["iotas"].now())
            v.tensor_copy(MASK, DIFF).then_inc(sem("vector_step"), n["vector_step"].up())
            v.wait_ge(sem("vector_step"), n["vector_step"].now())
            v.tensor_scalar(CNT, MASK, float(P), None, ALU.is_le).then_inc(sem("vector_step"), n["vector_step"].up())
            v.wait_ge(sem("vector_step"), n["vector_step"].now())
            for w in (3, 15):
                v.tensor_scalar(DIFF2, DIFF, w, None, ALU.bitwise_and).then_inc(
                    sem("vector_step"), n["vector_step"].up())
                v.wait_ge(sem("vector_step"), n["vector_step"].now())
                v.scalar_tensor_tensor(out=CNT, in0=DIFF2, scalar=0.0, in1=CNT, op0=ALU.is_equal, op1=ALU.add).then_inc(
                    sem("vector_step"), n["vector_step"].up())
                v.wait_ge(sem("vector_step"), n["vector_step"].now())
            v.scalar_tensor_tensor(out=CNT, in0=MASK, scalar=0.0, in1=CNT, op0=ALU.is_ge, op1=ALU.mult).then_inc(
                sem("vector_step"), n["vector_step"].up())
            v.wait_ge(sem("vector_step"), n["vector_step"].now())
            v.tensor_scalar(MASK, CNT, 0.0, NEG, ALU.is_equal, ALU.mult).then_inc(
                sem("vector_step"), n["vector_step"].up())
            v.wait_ge(sem("vector_step"), n["vector_step"].now())
            v.tensor_tensor(IDX[:, 0, :], IDX[:, 0, :], IDX[:, 1, :], ALU.bitwise_xor).then_inc(
                sem("vector_step"), n["vector_step"].up())
            v.wait_ge(sem("vector_step"), n["vector_step"].now())
            v.tensor_copy(IDXF[:, 0, :], IDX[:, 0, :]).then_inc(sem("vector_step"), n["vector_step"].up())
            v.wait_ge(sem("vector_step"), n["vector_step"].now())
            v.tensor_scalar(IDXF[:, 1, :], IDX[:, 2, :], 0.0, None, ALU.is_gt).then_inc(
                sem("vector_step"), n["vector_step"].up())
            v.wait_ge(sem("vector_step"), n["vector_step"].now())
            v.tensor_copy(LMASK[:, 0, :], ident[:, :]).then_inc(sem("vector_step"), n["vector_step"].up())
            v.wait_ge(sem("vector_step"), n["vector_step"].now())
            for l in range(1, LEVELS):
                s = float(2 ** (l - 1))
                v.scalar_tensor_tensor(out=LMASK[:, l, :], in0=IDXF[:, 0, :], scalar=s, in1=IDXF[:, 1, :],
                                          op0=ALU.is_ge, op1=ALU.mult).then_inc(
                    sem("vector_step"), n["vector_step"].up())
                v.wait_ge(sem("vector_step"), n["vector_step"].now())
                v.scalar_tensor_tensor(out=LMASK[:, l, :], in0=IDXF[:, 0, :], scalar=2 * s, in1=LMASK[:, l, :],
                                          op0=ALU.is_lt, op1=ALU.mult).then_inc(
                    sem("vector_step"), n["vector_step"].up())
                v.wait_ge(sem("vector_step"), n["vector_step"].now())
            n["load_decay"] = n["load_decay"]
            for q in range(2):
                v.wait_ge(sem(full("dve", 5 + q)), n[full("dve", 5 + q)].next())
                p = psum[:, 5 + q, :].rearrange("p (m t) -> p m t", m=2)
                g = GG3[:, 2 * q:2 * q + 2, :]
                for m in range(2):
                    v.tensor_scalar(g[:, m, :], p[:, m, :], col("gla_b_gate_2", 2 * q + m), None, ALU.add).then_inc(
                        sem("vector_step"), n["vector_step"].up())
                    v.wait_ge(sem("vector_step"), n["vector_step"].now())
                v.scalar_tensor_tensor(out=GTMP3[:, 2 * q:2 * q + 2, :], in0=g, scalar=-1.0, in1=g, op0=ALU.mult,
                                       op1=ALU.max)
                v.tensor_scalar(g, g, -1.0, 0.0, ALU.mult, ALU.max).then_inc(
                    sem(free("dve", 5 + q)), n[free("dve", 5 + q)].up())
                v.wait_ge(sem(free("dve", 5 + q)), n[free("dve", 5 + q)].now())
            v.sem_inc(sem("decay_in"), n["decay_in"].up())
            v.wait_ge(sem("decay_ln"), n["decay_ln"].next())
            v.tensor_tensor(GG3, GG3, GTMP3, ALU.add).then_inc(sem("decay_in"), n["decay_in"].up())
            v.wait_ge(sem("decay_in"), n["decay_in"].now())
            v.wait_ge(sem("ab_ready"), n["ab_ready"].next())

            def dil_stage(i):
                v.tensor_copy(DQ, QA[:, ds(i, 1), :])
                v.tensor_copy(DK, KA[:, ds(i, 1), :])
                v.tensor_copy(DV, VA[:, :, ds(i * P, P)]).then_inc(sem("heads_staged"), n["heads_staged"].up())
                v.wait_ge(sem("heads_staged"), n["heads_staged"].now())

            def dil_mask(i, u, b):
                v.tensor_tensor(psum[:, b, 0:T], psum[:, b, 0:T], MASK[:, u, :], ALU.add).then_inc(
                    sem("vector_step"), n["vector_step"].up())
                v.wait_ge(sem("vector_step"), n["vector_step"].now())

            def dil_weigh(u):
                v.tensor_tensor(DP[u], DP[u], CNT[:, u, :], ALU.mult).then_inc(
                    sem("vector_step"), n["vector_step"].up())
                v.wait_ge(sem("vector_step"), n["vector_step"].now())
                v.tensor_reduce(small[:, 4 + u:5 + u], DP[u], AX_X, ALU.add).then_inc(
                    sem("vector_step"), n["vector_step"].up())
                v.wait_ge(sem("vector_step"), n["vector_step"].now())

            softmax_rounds(HT, 2, dil_stage, dil_mask, dil_weigh, DP, Y, 0, 8, 256)

            def linear_attention(turns, nv, f, q_of, g_of, k_of, v_of, dst, steps):
                per = {n["vector_step"]: steps, n["levels_ready"]: 1, n["head_scores"]: 2}
                for b in (4, 5, 6):
                    for fn in (full, free):
                        per[n[fn("dve", b)]] = 4 if b < 6 else 2
                for b in range(nv):
                    for fn in (full, free):
                        per[n[fn("dve", b)]] = 1
                Dd, Ff, QL, KL = f["D"], f["F"], f["QL"], f["KL"]
                with rounds(v, turns, per) as i:
                    q_of(i, f["q"])
                    k_of(i, f["k"])
                    g_of(i, Dd)
                    v_of(i, f["V"])
                    v.memset(Ff, 1.0).then_inc(sem("vector_step"), n["vector_step"].up())
                    v.wait_ge(sem("vector_step"), n["vector_step"].now())
                    v.tensor_copy(QL[:, 0, :], f["q"]).then_inc(sem("vector_step"), n["vector_step"].up())
                    v.wait_ge(sem("vector_step"), n["vector_step"].now())
                    v.tensor_copy(KL[:, 0, :], f["k"]).then_inc(sem("vector_step"), n["vector_step"].up())
                    v.wait_ge(sem("vector_step"), n["vector_step"].now())
                    for l in range(1, LEVELS + 1):
                        s = 2 ** (l - 1)
                        v.tensor_tensor(QL[:, l, :], f["q"], Dd, ALU.mult)
                        ins = v.tensor_tensor(KL[:, l, :], f["k"], Ff, ALU.mult)
                        if l == LEVELS:
                            ins.then_inc(sem("levels_ready"), n["levels_ready"].up())
                            v.wait_ge(sem("levels_ready"), n["levels_ready"].now())
                            break
                        ins.then_inc(sem("vector_step"), n["vector_step"].up())
                        v.wait_ge(sem("vector_step"), n["vector_step"].now())
                        dv = Dd.rearrange("p (n w s) -> p n w s", w=2, s=s)
                        fv = Ff.rearrange("p (n w s) -> p n w s", w=2, s=s)
                        shape = [P, 512 // (2 * s), s]
                        v.tensor_tensor(fv[:, :, 0, :], fv[:, :, 0, :], dv[:, :, 1, s - 1:s].broadcast_to(shape),
                                           ALU.mult).then_inc(sem("vector_step"), n["vector_step"].up())
                        v.wait_ge(sem("vector_step"), n["vector_step"].now())
                        v.tensor_tensor(dv[:, :, 1, :], dv[:, :, 1, :], dv[:, :, 0, s - 1:s].broadcast_to(shape),
                                           ALU.mult).then_inc(sem("vector_step"), n["vector_step"].up())
                        v.wait_ge(sem("vector_step"), n["vector_step"].now())
                    for h in range(2):
                        for b in range(2):
                            for half in range(2):
                                v.wait_ge(sem(full("dve", 4 + half)), n[full("dve", 4 + half)].next())
                                v.tensor_tensor(f["A"][:, 4 * half:4 * half + 4, :],
                                                        psum[:, 4 + half, :].rearrange("p (l i) -> p l i", l=4),
                                                        LMASK[:, 4 * half:4 * half + 4, :], ALU.mult).then_inc(
                                    sem(free("dve", 4 + half)), n[free("dve", 4 + half)].up())
                                v.wait_ge(sem(free("dve", 4 + half)), n[free("dve", 4 + half)].now())
                            v.tensor_reduce(f["SC"][:, h, b, :], f["A"].rearrange("p l i -> p i l"), AX_X, ALU.add).then_inc(
                                sem("vector_step"), n["vector_step"].up())
                            v.wait_ge(sem("vector_step"), n["vector_step"].now())
                        v.wait_ge(sem(full("dve", 6)), n[full("dve", 6)].next())
                        v.tensor_copy(f["SC"][:, h, 2, :], psum[:, 6, 0:P]).then_inc(
                            sem(free("dve", 6)), n[free("dve", 6)].up())
                        v.wait_ge(sem(free("dve", 6)), n[free("dve", 6)].now())
                        v.sem_inc(sem("head_scores"), n["head_scores"].up())
                    for b in range(nv):
                        v.wait_ge(sem(full("dve", b)), n[full("dve", b)].next())
                        v.tensor_copy(dst[:, ds(i * (2 * nv) + 2 * b, 2), :],
                                              psum[:, b, :].rearrange("p (m t) -> p m t", m=2)).then_inc(
                            sem(free("dve", b)), n[free("dve", b)].up())
                        v.wait_ge(sem(free("dve", b)), n[free("dve", b)].now())

            def flat(t):
                return t.rearrange("p (a b) -> p a b", a=2)

            v.wait_ge(sem("decay_exp"), n["decay_exp"].next())
            linear_attention(2, 2, GLA,
                             lambda i, o: v.tensor_copy(flat(o), QB[:, ds(2 * i, 2), :]),
                             lambda i, o: v.tensor_copy(flat(o), GG[:, ds(2 * i, 2), :]),
                             lambda i, o: v.tensor_copy(flat(o), KB[:, ds(2 * i, 2), :]),
                             lambda i, o: v.tensor_copy(o, VB[:, :, ds(i * 512, 512)]),
                             Y[:, HT:KT, :], 28)

            def head_norm(y, heads, each, sq, name):
                v.tensor_tensor(sq, y, y, ALU.mult).then_inc(sem("squares_ready"), n["squares_ready"].up())
                v.wait_ge(sem("squares_ready"), n["squares_ready"].now())
                for h in range(0, heads, 2):
                    b = (h // 2) % 4
                    v.wait_ge(sem(full("dve", b)), n[full("dve", b)].next())
                    v.tensor_scalar(sq[:, h:h + 2, :], psum[:, b, :].rearrange("p (m t) -> p m t", m=2),
                                            1.0 / (each * P), EPS, ALU.mult, ALU.add).then_inc(
                        sem(free("dve", b)), n[free("dve", b)].up())
                    v.wait_ge(sem(free("dve", b)), n[free("dve", b)].now())
                v.sem_inc(sem("norm_var"), n["norm_var"].up())
                v.wait_ge(sem("norm_std"), n["norm_std"].next())
                v.reciprocal(sq[:, 0:heads, :], sq[:, 0:heads, :]).then_inc(sem("vector_step"), n["vector_step"].up())
                v.wait_ge(sem("vector_step"), n["vector_step"].now())
                for h in range(heads):
                    for e in range(each):
                        k = h * each + e
                        ins = v.scalar_tensor_tensor(out=y[:, k, :], in0=y[:, k, :], scalar=col(name, k),
                                                     in1=sq[:, h, :], op0=ALU.mult, op1=ALU.mult)
                ins.then_inc(sem("vector_step"), n["vector_step"].up())
                v.wait_ge(sem("vector_step"), n["vector_step"].now())

            head_norm(Y[:, HT:KT, :], 4, 2, GLA["SQ"], "gla_norm_g_2")
            v.tensor_tensor(Y, Y, GATE2, ALU.mult).then_inc(sem("y_ready"), n["y_ready"].up())
            v.wait_ge(sem("y_ready"), n["y_ready"].now())

            def add_in(i, s, h, b):
                x = X[:, ds(i * 8 + 2 * s, 2), :]
                v.tensor_tensor(x, psum[:, b, :].rearrange("p (m t) -> p m t", m=2), x, ALU.add).then_inc(
                    sem(free("dve", b)), n[free("dve", b)].up())
                v.wait_ge(sem(free("dve", b)), n[free("dve", b)].now())

            evac("ab_out", add_in)

            rms_norm(X, H2, SQ1, 4, lambda k: col("norm_g_2", KT + k), None)
            v.sem_inc(sem("y_used"), n["y_used"].up())
            n["load_s5"].n += 3
            v.wait_ge(sem("load_s5"), n["load_s5"].now())
            v.tensor_copy(S5N[0:32, 2 * P:3 * P].rearrange("p (a b) -> p a b", a=2),
                             over(S5DT[0:32, :], 64, 2)).then_inc(sem("dt_spread"), n["dt_spread"].up())
            v.wait_ge(sem("dt_spread"), n["dt_spread"].now())
            v.wait_ge(sem(full("dve", 4)), n[full("dve", 4)].next())
            v.tensor_copy(s5p[:, 0:3, :], psum[:, 4, 0:96].rearrange("p (a b) -> p a b", a=3)).then_inc(
                sem(free("dve", 4)), n[free("dve", 4)].up())
            v.wait_ge(sem(free("dve", 4)), n[free("dve", 4)].now())
            v.sem_inc(sem("s5_dt"), n["s5_dt"].up())
            v.wait_ge(sem("s5_act"), n["s5_act"].next())
            col5 = lambda k: s5p[:, k, :]
            def TT(o, a, b, op):
                v.tensor_tensor(o, a, b, op).then_inc(sem("vector_step"), n["vector_step"].up())
                v.wait_ge(sem("vector_step"), n["vector_step"].now())

            TT(col5(3), col5(0), col5(2), ALU.mult)
            TT(col5(4), col5(1), col5(2), ALU.mult)
            v.tensor_scalar(col5(10), col5(4), 1.0 / TWO_PI, ROUND, ALU.mult, ALU.add).then_inc(
                sem("vector_step"), n["vector_step"].up())
            v.wait_ge(sem("vector_step"), n["vector_step"].now())
            v.tensor_scalar(col5(10), col5(10), ROUND, None, ALU.subtract).then_inc(
                sem("vector_step"), n["vector_step"].up())
            v.wait_ge(sem("vector_step"), n["vector_step"].now())
            for part in (6.28125, 0.0019350051879882812, 3.019916050561823e-07):
                v.scalar_tensor_tensor(out=col5(4), in0=col5(10), scalar=-part, in1=col5(4), op0=ALU.mult,
                                          op1=ALU.add).then_inc(sem("vector_step"), n["vector_step"].up())
                v.wait_ge(sem("vector_step"), n["vector_step"].now())
            v.tensor_scalar(col5(5), col5(4), 3.1415925, -3.1415925, ALU.min, ALU.max).then_inc(
                sem("vector_step"), n["vector_step"].up())
            v.wait_ge(sem("vector_step"), n["vector_step"].now())
            v.scalar_tensor_tensor(out=col5(4), in0=col5(5), scalar=-1.0, in1=col5(5), op0=ALU.mult, op1=ALU.max).then_inc(
                sem("vector_step"), n["vector_step"].up())
            v.wait_ge(sem("vector_step"), n["vector_step"].now())
            v.tensor_scalar(col5(4), col5(4), -1.0, TWO_PI / 4, ALU.mult, ALU.add).then_inc(
                sem("vector_step"), n["vector_step"].up())
            v.wait_ge(sem("vector_step"), n["vector_step"].now())
            v.sem_inc(sem("s5_dt"), n["s5_dt"].up())
            v.wait_ge(sem("s5_act"), n["s5_act"].next())
            TT(col5(6), col5(3), col5(4), ALU.mult)
            TT(col5(7), col5(3), col5(5), ALU.mult)
            TT(col5(10), col5(0), col5(0), ALU.mult)
            TT(col5(11), col5(1), col5(1), ALU.mult)
            TT(col5(10), col5(10), col5(11), ALU.add)
            v.reciprocal(col5(10), col5(10)).then_inc(sem("vector_step"), n["vector_step"].up())
            v.wait_ge(sem("vector_step"), n["vector_step"].now())
            v.tensor_scalar(col5(11), col5(6), 1.0, None, ALU.subtract).then_inc(
                sem("vector_step"), n["vector_step"].up())
            v.wait_ge(sem("vector_step"), n["vector_step"].now())
            TT(col5(8), col5(11), col5(0), ALU.mult)
            TT(col5(9), col5(7), col5(1), ALU.mult)
            TT(col5(8), col5(8), col5(9), ALU.add)
            TT(col5(8), col5(8), col5(10), ALU.mult)
            TT(col5(11), col5(11), col5(1), ALU.mult)
            TT(col5(9), col5(7), col5(0), ALU.mult)
            TT(col5(9), col5(9), col5(11), ALU.subtract)
            TT(col5(9), col5(9), col5(10), ALU.mult)
            n["load_s5b"].n += 2
            v.wait_ge(sem("load_s5b"), n["load_s5b"].now())
            bb = S5B.rearrange("p (j a h) -> p j a h", a=2, h=16)
            v.memset(S5B, 0.0).then_inc(sem("vector_step"), n["vector_step"].up())
            v.wait_ge(sem("vector_step"), n["vector_step"].now())
            for c in range(2):
                for a in range(2):
                    r = slice(64 * a, 64 * a + 64)
                    o = bb[r, :, a, :]
                    t = S5T[r, :, :]
                    re, im = over(s5p[r, 8, :], 16, 2), over(s5p[r, 9, :], 16, 2)
                    v.tensor_tensor(o, S5BN[r, c, :, :], re, ALU.mult).then_inc(
                        sem("vector_step"), n["vector_step"].up())
                    v.wait_ge(sem("vector_step"), n["vector_step"].now())
                    v.tensor_tensor(t, S5BN[r, 1 - c, :, :], im, ALU.mult).then_inc(
                        sem("vector_step"), n["vector_step"].up())
                    v.wait_ge(sem("vector_step"), n["vector_step"].now())
                    v.tensor_tensor(o, o, t, ALU.subtract if c == 0 else ALU.add).then_inc(
                        sem("vector_step"), n["vector_step"].up())
                    v.wait_ge(sem("vector_step"), n["vector_step"].now())
                v.sem_inc(sem("b_ready"), n["b_ready"].up())
                for q in range(2):
                    v.wait_ge(sem(full("dve", 6 + q)), n[full("dve", 6 + q)].next())
                    v.tensor_copy(BT[:, c, 4 * q:4 * q + 4, :],
                                          psum[:, 6 + q, :].rearrange("p (g s) -> p g s", g=4)).then_inc(
                        sem(free("dve", 6 + q)), n[free("dve", 6 + q)].up())
                    v.wait_ge(sem(free("dve", 6 + q)), n[free("dve", 6 + q)].now())
            v.memset(CMASK, 0.0).then_inc(sem("vector_step"), n["vector_step"].up())
            v.wait_ge(sem("vector_step"), n["vector_step"].now())
            for a in range(2):
                v.memset(CMASK[64 * a:64 * a + 64, :].rearrange("p (n a h) -> p n a h", a=2, h=16)[:, :, a, :], 1.0).then_inc(
                    sem("vector_step"), n["vector_step"].up())
                v.wait_ge(sem("vector_step"), n["vector_step"].now())
            for c in range(2):
                for q in range(2):
                    v.wait_ge(sem(full("dve", 6 + q)), n[full("dve", 6 + q)].next())
                    v.scalar_tensor_tensor(out=CT[:, c, 4 * q:4 * q + 4, :],
                                                   in0=psum[:, 6 + q, :].rearrange("p (g s) -> p g s", g=4),
                                                   scalar=1.0 if c == 0 else -1.0, in1=over(CMASK, 4), op0=ALU.mult,
                                                   op1=ALU.mult).then_inc(
                        sem(free("dve", 6 + q)), n[free("dve", 6 + q)].up())
                    v.wait_ge(sem(free("dve", 6 + q)), n[free("dve", 6 + q)].now())

            def times(o_re, o_im, a_re, a_im, b_re, b_im, t):
                v.tensor_tensor(t, a_im, b_im, ALU.mult).then_inc(sem("vector_step"), n["vector_step"].up())
                v.wait_ge(sem("vector_step"), n["vector_step"].now())
                v.tensor_tensor(o_re, a_re, b_re, ALU.mult).then_inc(sem("vector_step"), n["vector_step"].up())
                v.wait_ge(sem("vector_step"), n["vector_step"].now())
                v.tensor_tensor(o_re, o_re, t, ALU.subtract).then_inc(sem("vector_step"), n["vector_step"].up())
                v.wait_ge(sem("vector_step"), n["vector_step"].now())
                v.tensor_tensor(t, a_im, b_re, ALU.mult).then_inc(sem("vector_step"), n["vector_step"].up())
                v.wait_ge(sem("vector_step"), n["vector_step"].now())
                v.tensor_tensor(o_im, a_re, b_im, ALU.mult).then_inc(sem("vector_step"), n["vector_step"].up())
                v.wait_ge(sem("vector_step"), n["vector_step"].now())
                v.tensor_tensor(o_im, o_im, t, ALU.add).then_inc(sem("vector_step"), n["vector_step"].up())
                v.wait_ge(sem("vector_step"), n["vector_step"].now())

            v.tensor_copy(PW[:, 0, :, 0:1], s5p[:, 6, :].unsqueeze(2)).then_inc(
                sem("vector_step"), n["vector_step"].up())
            v.wait_ge(sem("vector_step"), n["vector_step"].now())
            v.tensor_copy(PW[:, 1, :, 0:1], s5p[:, 7, :].unsqueeze(2)).then_inc(
                sem("vector_step"), n["vector_step"].up())
            v.wait_ge(sem("vector_step"), n["vector_step"].now())
            w = 1
            while w < 16:
                sh = [P, 32, w]
                times(PW[:, 0, :, w:2 * w], PW[:, 1, :, w:2 * w], PW[:, 0, :, 0:w], PW[:, 1, :, 0:w],
                      PW[:, 0, :, w - 1:w].broadcast_to(sh), PW[:, 1, :, w - 1:w].broadcast_to(sh),
                      ST[:, 0:32 * w].rearrange("p (a b) -> p a b", a=32))
                w *= 2
            v.sem_inc(sem("s5_tables"), n["s5_tables"].up())

            def advance(dst, src, a_re, a_im, t):
                for o, x0, x1, op in ((0, 0, 1, ALU.subtract), (1, 1, 0, ALU.add)):
                    v.tensor_tensor(t, src[x0], a_re, ALU.mult).then_inc(sem("vector_step"), n["vector_step"].up())
                    v.wait_ge(sem("vector_step"), n["vector_step"].now())
                    v.tensor_tensor(dst[o], dst[o], t, ALU.add).then_inc(sem("vector_step"), n["vector_step"].up())
                    v.wait_ge(sem("vector_step"), n["vector_step"].now())
                    v.tensor_tensor(t, src[x1], a_im, ALU.mult).then_inc(sem("vector_step"), n["vector_step"].up())
                    v.wait_ge(sem("vector_step"), n["vector_step"].now())
                    v.tensor_tensor(dst[o], dst[o], t, op).then_inc(sem("vector_step"), n["vector_step"].up())
                    v.wait_ge(sem("vector_step"), n["vector_step"].now())

            v.wait_ge(sem("u_ready"), n["u_ready"].next())
            for half in range(2):
                v.wait_ge(sem("inputs_ready"), n["inputs_ready"].next())
                j0 = 16 * half
                xs = SX.rearrange("p c j (m r) -> p c j m r", r=16)
                with rounds(v, 15, {n["vector_step"]: 8}) as r:
                    t = ST[:, 0:256].rearrange("p (j m) -> p j m", j=16)
                    sh = [P, 16, 16]
                    advance([xs[:, c, :, :, ds(r + 1, 1)].rearrange("p j m r -> p j (m r)") for c in range(2)],
                            [xs[:, c, :, :, ds(r, 1)].rearrange("p j m r -> p j (m r)") for c in range(2)],
                            PW[:, 0, j0:j0 + 16, 0:1].broadcast_to(sh), PW[:, 1, j0:j0 + 16, 0:1].broadcast_to(sh), t)
                with rounds(v, 15, {n["vector_step"]: 8}) as m:
                    t = ST[:, 0:16]
                    last = [xs[:, c, :, :, 15:16].rearrange("p j m r -> p j (m r)") for c in range(2)]
                    advance([last[c][:, :, ds(m + 1, 1)].rearrange("p j m -> p (j m)") for c in range(2)],
                            [last[c][:, :, ds(m, 1)].rearrange("p j m -> p (j m)") for c in range(2)],
                            PW[:, 0, j0:j0 + 16, 15], PW[:, 1, j0:j0 + 16, 15], t)
                with rounds(v, 16, {n["vector_step"]: 8}) as j:
                    t = ST[:, 0:225].rearrange("p (m r) -> p m r", m=15)
                    sh = [P, 15, 15]
                    sx = lambda c, m0, r0, r1: xs[:, c, ds(j, 1), m0:m0 + 15, r0:r1].rearrange("p j m r -> p (j m) r")
                    pw = lambda c: PW[:, c, ds(j + j0, 1), 0:15].broadcast_to(sh)
                    advance([sx(c, 1, 0, 15) for c in range(2)],
                            [sx(c, 0, 15, 16).broadcast_to(sh) for c in range(2)], pw(0), pw(1), t)
                v.sem_inc(sem("states_ready"), n["states_ready"].up())
                for q in range(4):
                    ut = 4 * half + q
                    v.wait_ge(sem(full("dve", 4 + q % 2)), n[full("dve", 4 + q % 2)].next())
                    v.scalar_tensor_tensor(out=Y5[:, ut, :], in0=SU5[:, ut, :], scalar=col("s5_d_2", ut),
                                                   in1=psum[:, 4 + q % 2, 0:T], op0=ALU.mult, op1=ALU.add).then_inc(
                        sem(free("dve", 4 + q % 2)), n[free("dve", 4 + q % 2)].up())
                    v.wait_ge(sem(free("dve", 4 + q % 2)), n[free("dve", 4 + q % 2)].now())
                v.sem_inc(sem("half_done"), n["half_done"].up())
            v.sem_inc(sem("s5_sum"), n["s5_sum"].up())
            v.wait_ge(sem("glu_ready"), n["glu_ready"].next())
            v.tensor_tensor(Y5[:, 0:HT, :], Y5[:, 0:HT, :], QD, ALU.mult).then_inc(
                sem("glu_used"), n["glu_used"].up())
            v.wait_ge(sem("glu_used"), n["glu_used"].now())
            v.wait_ge(sem("cd_ready"), n["cd_ready"].next())
            g0, g1 = col("hgrn_gamma_2", 0, HT), col("hgrn_gamma_2", HT, HT)
            v.tensor_tensor(s5p[:, 0, 0:HT], g0, g1, ALU.max).then_inc(sem("vector_step"), n["vector_step"].up())
            v.wait_ge(sem("vector_step"), n["vector_step"].now())
            v.tensor_tensor(small[:, 0:HT], g0, s5p[:, 0, 0:HT], ALU.subtract).then_inc(
                sem("vector_step"), n["vector_step"].up())
            v.wait_ge(sem("vector_step"), n["vector_step"].now())
            v.tensor_tensor(small[:, HT:16], g1, s5p[:, 0, 0:HT], ALU.subtract).then_inc(
                sem("gamma_in"), n["gamma_in"].up())
            v.wait_ge(sem("gamma_in"), n["gamma_in"].now())
            v.wait_ge(sem("gamma_exp"), n["gamma_exp"].next())
            v.tensor_tensor(s5p[:, 0, 0:HT], small[:, 0:HT], small[:, HT:16], ALU.add).then_inc(
                sem("vector_step"), n["vector_step"].up())
            v.wait_ge(sem("vector_step"), n["vector_step"].now())
            v.reciprocal(s5p[:, 0, 0:HT], s5p[:, 0, 0:HT]).then_inc(sem("vector_step"), n["vector_step"].up())
            v.wait_ge(sem("vector_step"), n["vector_step"].now())
            v.tensor_tensor(s5p[:, 1, 0:16].rearrange("p (a b) -> p a b", a=2),
                               small[:, 0:16].rearrange("p (a b) -> p a b", a=2), over(s5p[:, 0, 0:HT], 2), ALU.mult).then_inc(
                sem("vector_step"), n["vector_step"].up())
            v.wait_ge(sem("vector_step"), n["vector_step"].now())
            v.tensor_tensor(s5p[:, 2, 0:HT], s5p[:, 1, 0:HT], s5p[:, 1, HT:16], ALU.add).then_inc(
                sem("vector_step"), n["vector_step"].up())
            v.wait_ge(sem("vector_step"), n["vector_step"].now())
            v.tensor_tensor(s5p[:, 2, 0:HT], s5p[:, 2, 0:HT], s5p[:, 1, 0:HT], ALU.subtract).then_inc(
                sem("vector_step"), n["vector_step"].up())
            v.wait_ge(sem("vector_step"), n["vector_step"].now())
            v.tensor_scalar(s5p[:, 3, 0:HT], s5p[:, 2, 0:HT], -1.0, 1.0, ALU.mult, ALU.add).then_inc(
                sem("vector_step"), n["vector_step"].up())
            v.wait_ge(sem("vector_step"), n["vector_step"].now())
            for k in range(HT):
                ins = v.tensor_scalar(FD[:, k, :], FD[:, k, :], s5p[:, 3, k:k + 1], s5p[:, 2, k:k + 1], ALU.mult,
                                      ALU.add)
            ins.then_inc(sem("vector_step"), n["vector_step"].up())
            v.wait_ge(sem("vector_step"), n["vector_step"].now())
            linear_attention(4, 1, HG,
                             lambda i, o: v.tensor_copy(flat(o), QD[:, ds(2 * i, 2), :]),
                             lambda i, o: v.tensor_copy(flat(o), FD[:, ds(2 * i, 2), :]),
                             lambda i, o: v.tensor_scalar(flat(o), FD[:, ds(2 * i, 2), :], -1.0, 1.0, ALU.mult, ALU.add),
                             lambda i, o: v.tensor_copy(o, ID[:, :, ds(i * 256, 256)]),
                             YD, 28)
            head_norm(YD, 8, 1, HG["SQ"], "hgrn_norm_g_2")
            v.tensor_tensor(Y5[:, 0:HT, :], Y5[:, 0:HT, :], GATE3[:, 0:HT, :], ALU.mult).then_inc(
                sem("vector_step"), n["vector_step"].up())
            v.wait_ge(sem("vector_step"), n["vector_step"].now())
            v.tensor_tensor(Y5[:, HT:KT, :], YD, GATE3[:, HT:KT, :], ALU.mult).then_inc(
                sem("y_ready"), n["y_ready"].up())
            v.wait_ge(sem("y_ready"), n["y_ready"].now())
            evac("cd_out", add_in)
            rms_norm(X, H2, SQ1, 4, lambda k: col("final_g_2", k), None)
            v.sem_inc(sem("y_used"), n["y_used"].up())


NAMES = ("x", "c", "ctx", "c_ctx", "w_mod", "b_mod", "norm1_g", "norm2_g", "w_in", "b_in", "conv_w", "conv_b",
         "conv_ln_g", "conv_ln_b", "w_conv_out", "sgu_ln_g", "sgu_ln_b", "sgu_w", "sgu_b", "w_sgu_out", "na_rpb",
         "w_na_out", "w_o", "b_o", "w_ff1", "b_ff1", "w_ff2", "b_ff2", "final_g", "norm_g_2", "final_g_2", "ab_w_in_2",
         "gla_w_gate_2", "gla_b_gate_2", "gla_norm_g_2", "ab_w_out_2", "cd_w_in_2", "s5_lam_re_2", "s5_lam_im_2",
         "s5_log_dt_2", "s5_b_re_2", "s5_b_im_2", "s5_c_re_2", "s5_c_im_2", "s5_d_2", "s5_w_glu_2", "s5_b_glu_2",
         "hgrn_gamma_2", "hgrn_norm_g_2", "cd_w_out_2")
FLAT = ("norm_g_2", "hgrn_gamma_2", "s5_d_2")


def layout(inputs):
    arrays = {}
    for name in NAMES:
        a = np.ascontiguousarray(inputs[name])
        if a.ndim > 1 and a.shape[0] == 1:
            a = a.reshape(a.shape[1:])
        if name in FLAT:
            a = a.reshape(-1)
        arrays[name] = a
    return arrays


def kernel(**inputs):
    import concourse.bacc as bacc
    from concourse.bass_utils import run_bass_kernel_spmd

    nc = bacc.Bacc("TRN2", target_bir_lowering=False, num_devices=1)
    arrays = layout(inputs)
    dram = {n: nc.dram_tensor(n, a.shape, F32, kind="ExternalInput").ap() for n, a in arrays.items()}
    out = nc.dram_tensor("out", (T, D), F32, kind="ExternalOutput").ap()
    program(nc, dram, out)
    r = run_bass_kernel_spmd(nc, [arrays], core_ids=[0])
    return r.results[0]["out"].reshape(1, T, D)
```

```python
from contextlib import ExitStack, contextmanager

import numpy as np

import concourse.bass as bass
import concourse.mybir as mybir

F32 = mybir.dt.float32
I32 = mybir.dt.int32
ACT = mybir.ActivationFunctionType
ALU = mybir.AluOpType
AX_X = mybir.AxisListType.X
ds = bass.ds

P = 128
D = 2048
KT = D // P
HW = D // 2
HT = HW // P
T = 256
FF = 4 * D
EPS = 1e-6
NEG = -1e30
TAPS = 31
PAD = TAPS // 2
GRID = 64
WIN = 16
NHEAD = 16
DRS = 15
DCS = 31
PADW = 127
LEVELS = 8
TWO_PI = 6.283185307179586
ROUND = 12582912.0

A1, A2, SU, SV, WQ, WK, WV, WG = 0, 1024, 2048, 3072, 4096, 5120, 6144, 7168

PACKS = (
    (("b_in", 104), ("norm1_g", 16), ("conv_b", 8)),
    (("b_mod", 96), ("norm2_g", 16), ("b_o", 16)),
    (("b_ff1", 64), ("b_ff2", 16), ("norm_g_2", 32), ("final_g_2", 16)),
    (("c", 16), ("c_ctx", 16), ("conv_ln_g", 8), ("conv_ln_b", 8), ("sgu_ln_g", 8), ("sgu_ln_b", 8),
     ("gla_b_gate_2", 4), ("gla_norm_g_2", 8), ("s5_d_2", 8), ("s5_b_glu_2", 8), ("hgrn_norm_g_2", 8)),
    (("final_g", 16), ("hgrn_gamma_2", 16)),
)
COL = {}
for _n, _pack in enumerate(PACKS):
    _at = _n * P
    for _name, _rows in _pack:
        COL[_name] = _at
        _at += _rows

STREAM = (
    ("mod", "w_mod", 0, 24, 16, 128),
    ("q", "w_in", WQ, 2, 16, 128), ("k", "w_in", WK, 2, 16, 128), ("v", "w_in", WV, 2, 16, 128),
    ("a2", "w_in", A2, 2, 16, 128), ("a1", "w_in", A1, 2, 16, 128),
    ("su", "w_in", SU, 2, 16, 128), ("sv", "w_in", SV, 2, 16, 128),
    ("gate_conv", "w_in", WG, 4, 16, 128), ("out_conv", "w_conv_out", 0, 2, 8, 256),
    ("gate_sgu", "w_in", WG + D, 4, 16, 128), ("out_sgu", "w_sgu_out", 0, 2, 8, 256),
    ("gate_att", "w_in", WG + 2 * D, 4, 16, 128), ("out_att", "w_na_out", 0, 2, 8, 256),
    ("o", "w_o", 0, 4, 16, 128),
    ("ff1", "w_ff1", 0, 16, 16, 128), ("ff2", "w_ff2", 0, 16, 64, 128),
    ("va", "ab_w_in_2", 2048, 2, 16, 128), ("qa", "ab_w_in_2", 0, 2, 16, 128),
    ("ka", "ab_w_in_2", 1024, 2, 16, 128), ("qkb", "ab_w_in_2", 3072, 2, 16, 128),
    ("vb", "ab_w_in_2", 4096, 2, 16, 128), ("gate_ab", "ab_w_in_2", 5136, 4, 16, 128),
    ("ab_out", "ab_w_out_2", 0, 4, 16, 128),
    ("u", "cd_w_in_2", 0, 2, 16, 128),
    ("qd", "cd_w_in_2", 1024, 2, 16, 128), ("fd", "cd_w_in_2", 2048, 2, 16, 128),
    ("id", "cd_w_in_2", 3072, 2, 16, 128), ("gate_cd", "cd_w_in_2", 4096, 4, 16, 128),
    ("glu", "s5_w_glu_2", 0, 1, 8, 256),
    ("cd_out", "cd_w_out_2", 0, 4, 16, 128),
)
ROUNDS = {s[0]: s[3] for s in STREAM}
WIDE = {s[0]: s[5] // P for s in STREAM}
GLOW = 5120


class Count:

    def __init__(self, sem, step=1):
        self.sem, self.step, self.n, self.round, self.per = sem, step, 0, None, 0

    def up(self):
        self.n += 1
        return self.step

    def now(self, more=0):
        n = (self.n + more) * self.step
        return n if self.round is None else self.round * (self.per * self.step) + n

    def next(self):
        self.n += 1
        return self.now()


@contextmanager
def rounds(eng, n, per):
    start = {c: c.n for c in per}
    with eng.Fori(0, n) as i:
        for c, k in per.items():
            c.round, c.per = i, k
        yield i
    for c, k in per.items():
        assert c.n - start[c] == k, (c.sem, c.n - start[c], k)
        c.round, c.n = None, start[c] + n * k


def program(nc, dram, out):
    ctx = ExitStack()
    with ctx:
        def sb(name, shape, dt=F32):
            return ctx.enter_context(nc.sbuf_tensor(name, shape, dt))

        ring = sb("ring", [P, 4, 2048])
        arena = sb("arena", [P, 38912])
        cols = sb("cols", [P, len(PACKS) * P])
        mod = sb("mod", [P, 96, 2])
        ident = sb("ident", [P, P])
        ones = sb("ones", [P, P])
        mirror = sb("mirror", [P, P])
        cvec = sb("cvec", [P, KT, 2])
        gain = sb("gain", [P, 3, KT])
        taps = sb("taps", [P, HT, 32])
        bq = sb("bq", [P, HT])
        small = sb("small", [P, 16])
        s5p = sb("s5p", [P, 12, 32])
        padrow = sb("padrow", [120, 2, PADW])
        psum = ctx.enter_context(nc.psum_tensor("psum", [P, 8, 512], F32))
        bias_rows = nc.dram_tensor("bias_rows", (NHEAD, DRS, PADW), F32).ap()

        def at(off, *shape):
            n = int(np.prod(shape))
            v = arena[:, off:off + n]
            if len(shape) == 2:
                return v.rearrange("p (a b) -> p a b", a=shape[0])
            if len(shape) == 3:
                return v.rearrange("p (a b c) -> p a b c", a=shape[0], b=shape[1])
            return v

        X = at(0, KT, T)
        H = at(4096, KT, 2 * T)
        H2 = at(4096, KT, T)
        FIN = at(4096, KT, T)
        C = at(34048, KT, T)
        MIX = at(34048, KT, T)
        SUMSQ, SQT = at(38144, 1, T), at(38400, T)
        SUMSQ_C = at(38656, 1, T)
        MODROW = at(4096, 96 * P)
        XN, CN = at(12288, 2, D), at(16384, 2, D)
        PACK = [at(20480 + P * n, P) for n in range(4)] + [at(22016, P)]
        TAPN = at(20992, HW)
        SQ1 = at(12288, KT, T)
        XR = at(16384, KT, T)
        NQ, NK = at(12288, HT, T), at(14336, HT, 2 * T)
        NV = at(18432, 4, HW)
        ATT = at(22528, HT, T)
        VROW = at(22528, HW)
        BIAS = at(24576, NHEAD, 6, GRID)
        ST_Q, ST_K = at(30720, T), at(30976, 2 * T)
        ST_V = at(31488, 4, P)
        ST_B = at(34048, 4, T)
        PR = [at(32000, 512), at(32512, 512)]
        PT = [at(33024, 512), at(33536, 512)]
        GATE = at(12288, KT, T)
        U = at(16384, HT, T + 2 * PAD)
        CV = at(18672, HT, T)
        TMP = at(20720, 2, T)
        MEAN = at(21488, T)
        ZU, ZV = at(24576, HT, T), at(26624, HT, T)
        VT = at(28672, 2, HW)
        WST = at(30720, HT, P)
        SQ = at(31744, HT, T)
        SGN = at(28672, HT, P)
        SGB = at(33792, P)
        RS = at(21232, T)
        WMASK = at(34048 - GRID, GRID)
        HID = at(12288, FF // P, T)
        RELU = at(34048, 4, T)
        VA = at(8192, 2, HW)
        QA, KA = at(10240, HT, T), at(12288, HT, T)
        QB, KB = at(14336, 4, T), at(15360, 4, T)
        VB = at(16384, 2, HW)
        GG = at(18432, 4, T)
        GATE2 = at(19456, KT, T)
        Y = at(23552, KT, T)
        DQ, DK, DV = at(27648, T), at(27904, T), at(28160, 2, P)
        DP = [at(28416, T), at(28672, T)]
        DT_ = [at(28928, T), at(29184, T)]
        CNT, MASK = at(29440, 2, T), at(29952, 2, T)
        GLW, GWG, GTMP = at(30464, 256), at(30720, 512), at(31232, 1024)
        GLO = at(33792, T)
        LMASK = at(32768, LEVELS, P)
        SU5 = at(8192, HT, T)
        SX = at(10240, 2, 16, T)
        Y5 = at(18432, HT, T)
        SIG = at(15360, HT, T)
        Y5P = at(8192, KT, T)
        QD, FD = at(22528, HT, T), at(24576, HT, T)
        ID = at(20480, 2, HW)
        GATE3 = at(34048, KT, T)
        BT = at(26624, 2, HT, P)
        CT = at(28672, 2, HT, P)
        PW = at(30720, 2, 32, 16)
        ST = at(31744, 1024)
        QKB = at(14336, HT, T)
        DIFF, DIFF2 = at(31232, 2, T).bitcast(I32), at(31744, 2, T).bitcast(I32)
        IDX = at(28672, 3, P).bitcast(I32)
        IDXF = at(29056, 2, P)
        GG3, GTMP3 = at(18432, 4, T), at(31232, 4, T)
        GLA = {"QL": at(4096, LEVELS + 1, 512), "KL": at(8704, LEVELS + 1, 512), "D": at(27648, 512),
               "F": at(28160, 512), "V": at(29696, 2, 512),
               "A": at(30720, LEVELS, P), "SC": at(31744, 2, 3, P), "SQ": at(4096, HT, T)}
        HG = {"QL": at(4096, LEVELS + 1, 512), "KL": at(8704, LEVELS + 1, 512), "D": at(28672, 512),
              "F": at(29184, 512), "V": at(30720, 2, 256),
              "A": at(31232, LEVELS, P), "SC": at(17408, 2, 3, P), "SQ": at(4096, HT, T)}
        YD = at(13312, HT, T)
        TMP2 = at(29184, T)
        S5N, S5DT = at(10240, 384), at(10624, 2)
        S5BN, S5B = at(10752, 2, 32, 16), at(11776, 1024)
        S5T = at(12800, 32, 16)
        S5C, S5CI = at(13312, HT, P), at(14336, HT, P)
        CMASK = at(15360, P)

        sems = {}

        def sem(name):
            if name not in sems:
                sems[name] = ctx.enter_context(nc.semaphore(name))
            return sems[name]

        class Counts(dict):

            def __missing__(self, name):
                self[name] = Count(sem(name), 16 if name.startswith("load") else 1)
                return self[name]

        block = ctx.enter_context(nc.Block())

        def col(name, k=0, n=1):
            return cols[:, COL[name] + k:COL[name] + k + n]

        def over(ap, n, axis=1):
            a = ap.unsqueeze(axis)
            shape = [int(v) for v in a.shape]
            shape[axis] = n
            return a.broadcast_to(shape)

        def full(c, b):
            return f"bank{b}_full_for_{c}"

        def free(c, b):
            return f"bank{b}_read_by_{c}"

        @block.sync
        def _(sp):
            n = Counts()
            n["slot3_used"].n = 1
            first = True
            for name, array, c0, turns, kt, width in STREAM:
                w = dram[array].rearrange("(k p) n -> p k n", p=P)

                def load(i, s, wait):
                    if wait:
                        sp.wait_ge(sem(f"slot{s}_used"), n[f"slot{s}_used"].next())
                    if name == "mod":
                        src = w[:, 4 * s:4 * s + 4, ds(i * 512, 512)]
                    elif kt == 64:
                        src = w[:, 16 * s:16 * s + 16, ds(i * width, width)]
                    else:
                        src = w[:, :, ds(i * 4 * width + (c0 + s * width), width)]
                    dst = ring[:, s, :].rearrange("p (k n) -> p k n", n=512 if name == "mod" else width)
                    sp.dma_start(dst, src).then_inc(sem(f"load_slot{s}"), 16)

                if first:
                    for s in range(4):
                        load(0, s, False)
                    with rounds(sp, turns - 1, {n[f"slot{s}_used"]: 1 for s in range(4)}) as i:
                        for s in range(4):
                            load(i + 1, s, True)
                elif turns == 1:
                    for s in range(4):
                        load(0, s, True)
                else:
                    with rounds(sp, turns, {n[f"slot{s}_used"]: 1 for s in range(4)}) as i:
                        for s in range(4):
                            load(i, s, True)
                first = False
            sp.wait_ge(sem("result_ready"), n["result_ready"].next())
            sp.dma_start(out.rearrange("(t p) n -> p t n", p=P), at(12288, 2, D)).then_inc(sem("load_result"), 16)
            sp.wait_ge(sem("load_result"), 16)

        @block.tensor
        def _(pe):
            n = Counts()
            reader = {}

            def take(b, c):
                if reader.get(b, c) != c:
                    pe.wait_ge(sem(free(reader[b], b)), n[full(reader[b], b)].now(1))
                reader[b] = c
                pe.wait_ge(sem(free(c, b)), n[full(c, b)].now(1))

            def leave(ins, s):
                ins.then_inc(sem(f"slot{(s + 3) % 4}_used"), 1)

            def slots(name, c, body):
                per = {n[f"load_slot{s}"]: 1 for s in range(4)} | {n[full(c, s)]: 1 for s in range(4)}
                if ROUNDS[name] == 1:
                    for s in range(4):
                        body(0, s)
                else:
                    with rounds(pe, ROUNDS[name], per) as i:
                        for s in range(4):
                            body(i, s)

            def slot(s, width):
                pe.wait_ge(sem(f"load_slot{s}"), n[f"load_slot{s}"].next())
                return ring[:, s, :].rearrange("p (k n) -> p k n", n=width)

            def stationary(name, x, c, N=T, columns=slice(0, T)):
                kt, width = (8, 256) if WIDE[name] == 2 else (16, P)

                def body(i, s):
                    w = slot(s, width)
                    take(s, c)
                    for m in range(WIDE[name]):
                        for k in range(kt):
                            mm = pe.matmul(psum[:, s, m * N:(m + 1) * N], w[:, k, m * P:(m + 1) * P], x[:, k, columns],
                                           start=(k == 0), stop=(k == kt - 1))
                            if m == k == 0:
                                leave(mm, s)
                    mm.then_inc(sem(full(c, s)), n[full(c, s)].up())

                slots(name, c, body)

            def token_major(name, x, toks, c, bias=None):
                def body(i, s):
                    w = slot(s, P)
                    take(s, c)
                    for t in range(toks):
                        o = psum[:, s, t * P:(t + 1) * P]
                        for k in range(KT):
                            mm = pe.matmul(o, x[:, k, t * P:(t + 1) * P], w[:, k, :], start=(k == 0),
                                           stop=(k == KT - 1 and bias is None))
                            if t == k == 0:
                                leave(mm, s)
                        if bias is not None:
                            mm = pe.matmul(o, ones[0:1, :], bias[0:1, ds(i * 512 + s * P, P)], start=False, stop=True)
                    mm.then_inc(sem(full(c, s)), n[full(c, s)].up())

                slots(name, c, body)

            def turn(pieces, b, c):
                take(b, c)
                for k, (piece, off) in enumerate(pieces):
                    r, m = piece.shape[0], piece.shape[1]
                    mm = pe.transpose(psum[0:m, b, off:off + r], piece, ident[0:r, 0:r])
                mm.then_inc(sem(full(c, b)), n[full(c, b)].up())

            def sum_rows(src, b, c, tiles):
                take(b, c)
                for k in range(tiles):
                    mm = pe.matmul(psum[:, b, 0:T], ones[:, :], src[:, k, :], start=(k == 0), stop=(k == tiles - 1))
                mm.then_inc(sem(full(c, b)), n[full(c, b)].up())

            n["consts_ready"].n = 3
            pe.wait_ge(sem("consts_ready"), n["consts_ready"].now())
            n["load_packs"].n = sum(len(p) for p in PACKS)
            pe.wait_ge(sem("load_packs"), n["load_packs"].now())
            for j in range(5):
                rows = sum(r for _, r in PACKS[j])
                turn([(PACK[j][0:rows, :], 0)], j, "dve")
            pe.wait_ge(sem("load_taps"), n["load_taps"].next())
            turn([(TAPN[0:TAPS, j * P:(j + 1) * P], 32 * j) for j in range(HT)], 5, "dve")
            for q, (nat, what) in enumerate(((XN, "load_x"), (CN, "load_ctx"))):
                pe.wait_ge(sem(what), n[what].next())
                for k in range(0, KT, 2):
                    turn([(nat[:, t, (k + m) * P:(k + m + 1) * P], m * T + t * P) for m in range(2) for t in range(2)],
                         (k // 2) % 4, "act")
            pe.wait_ge(sem("cvec_ready"), n["cvec_ready"].next())
            per = {n[f"load_slot{s}"]: 2 for s in range(4)} | {n[full("act", b)]: 1 for b in range(2)}
            with rounds(pe, ROUNDS["mod"] // 2, per):
                for g in range(2):
                    take(g, "act")
                    for s in range(4):
                        w = slot(s, 512)
                        for k in range(4):
                            mm = pe.matmul(psum[0:2, g, :], cvec[:, 4 * s + k, :], w[:, k, :], start=(s == k == 0),
                                           stop=(s == k == 3))
                            if k == 0:
                                leave(mm, s)
                    mm.then_inc(sem(full("act", g)), n[full("act", g)].up())
            for q, total in enumerate((SUMSQ, SUMSQ_C)):
                pe.wait_ge(sem("squares_ready"), n["squares_ready"].next())
                sum_rows(total, 4 + q, "dve", 1)
            pe.wait_ge(sem("mod_rows"), n["mod_rows"].next())
            turn([(MODROW[0:2, j * P:(j + 1) * P], 2 * j) for j in range(96)], 4, "dve")
            pe.wait_ge(sem("normed"), n["normed"].next())
            stationary("q", H, "act")
            pe.wait_ge(sem("normed"), n["normed"].next())
            stationary("k", H, "act", N=2 * T, columns=slice(0, 2 * T))
            pe.wait_ge(sem("load_vrow"), n["load_vrow"].next())
            token_major("v", H, 4, "act", VROW)
            units = [(h, b) for h in range(2) for b in range(2)]

            def attend(turns, nunits, scores, keys, values, dst_bank):
                per = {n["heads_staged"]: 1, n["probs_ready"]: nunits, n["probs_turned"]: nunits,
                       n[full("dve", dst_bank)]: 1}
                for b in range(2):
                    per[n[full("dve", 4 + b)]] = nunits // 2
                    per[n[full("act", 6 + b)]] = nunits // 2
                with rounds(pe, turns, per):
                    pe.wait_ge(sem("heads_staged"), n["heads_staged"].next())
                    take(dst_bank, "dve")

                    def ahead(u):
                        take(4 + u % 2, "dve")
                        scores(u).then_inc(sem(full("dve", 4 + u % 2)), n[full("dve", 4 + u % 2)].up())

                    ahead(0)
                    for u in range(nunits):
                        if u + 1 < nunits:
                            ahead(u + 1)
                        pe.wait_ge(sem("probs_ready"), n["probs_ready"].next())
                        turn([(keys(u, k), k * P) for k in range(values[0])], 6 + u % 2, "act")
                        pe.wait_ge(sem("probs_turned"), n["probs_turned"].next())
                        for k in range(values[0]):
                            mm = pe.matmul(*values[1](u, k), start=(k == 0), stop=(k == values[0] - 1))
                    mm.then_inc(sem(full("dve", dst_bank)), n[full("dve", dst_bank)].up())

            def na_scores(u):
                h, b = units[u]
                r = slice(64 * h, 64 * h + 64)
                pe.matmul(psum[:, 4 + b, :], ST_Q[r, b * P:(b + 1) * P], ST_K[r, :], start=True, stop=False)
                return pe.matmul(psum[:, 4 + b, 0:T], mirror[:, :], ST_B[:, 2 * h + b, :], start=False,
                                 stop=True)

            def na_values(u, k):
                h, b = units[u]
                return (psum[64 * h:64 * h + 64, 0, b * P:(b + 1) * P], ST_V[:, k, 64 * h:64 * h + 64],
                        PT[b][:, k * P:(k + 1) * P])

            attend(HT, 4, na_scores, lambda u, k: PR[u % 2][:, k * P:(k + 1) * P], (4, na_values), 0)

            def layer_norm(z, sq):
                pe.wait_ge(sem("ln_in"), n["ln_in"].next())
                sum_rows(z, 4, "dve", HT)
                pe.wait_ge(sem("squares_ready"), n["squares_ready"].next())
                sum_rows(sq, 5, "dve", HT)

            stationary("a2", H, "act")
            stationary("a1", H, "dve")
            stationary("su", H, "act")
            stationary("sv", H, "act")
            n["load_sgu"].n += 2
            pe.wait_ge(sem("load_sgu"), n["load_sgu"].now())
            for q in range(2):
                turn([(SGN[:, 4 * q + g, :], g * P) for g in range(4)], 6 + q, "act")
            layer_norm(ZV, SQ)
            pe.wait_ge(sem("ln_out"), n["ln_out"].next())
            for j in range(0, HT, 2):
                turn([(ZV[:, j + m, t * P:(t + 1) * P], (t * 2 + m) * P) for t in range(2) for m in range(2)],
                     (j // 2) % 4, "act")
            n["sgu_turned"].n += 6
            pe.wait_ge(sem("sgu_turned"), n["sgu_turned"].now())
            for g in range(HT):
                b = g % 4
                take(b, "dve")
                for t in range(2):
                    o = psum[:, b, t * P:(t + 1) * P]
                    pe.matmul(o, VT[:, t, g * P:(g + 1) * P], WST[:, g, :], start=True, stop=False)
                    mm = pe.matmul(o, ident[0:HT, g:g + 1].broadcast_to([HT, P]), SGB[0:HT, :], start=False, stop=True)
                mm.then_inc(sem(full("dve", b)), n[full("dve", b)].up())
            stationary("gate_conv", H, "act")
            layer_norm(CV, SQ)
            pe.wait_ge(sem("conv_ready"), n["conv_ready"].next())
            stationary("out_conv", CV, "dve")
            stationary("gate_sgu", H, "act")
            pe.wait_ge(sem("sgu_ready"), n["sgu_ready"].next())
            stationary("out_sgu", ZU, "dve")
            stationary("gate_att", H, "act")
            stationary("out_att", ATT, "dve")
            pe.wait_ge(sem("mixed"), n["mixed"].next())
            stationary("o", MIX, "dve")

            def rms(sq, tiles):
                pe.wait_ge(sem("squares_ready"), n["squares_ready"].next())
                sum_rows(sq, 4, "dve", tiles)
                pe.wait_ge(sem("normed"), n["normed"].next())

            rms(SUMSQ, 1)
            stationary("ff1", H2, "act")
            pe.wait_ge(sem("hidden_ready"), n["hidden_ready"].next())
            per = {n[f"load_slot{s}"]: 2 for s in range(4)} | {n[full("dve", b)]: 1 for b in range(2)}
            with rounds(pe, ROUNDS["ff2"] // 2, per):
                for g in range(2):
                    take(g, "dve")
                    for s in range(4):
                        w = slot(s, P)
                        for k in range(16):
                            mm = pe.matmul(psum[:, g, 0:T], w[:, k, :], HID[:, 16 * s + k, :], start=(s == k == 0),
                                           stop=(s == 3 and k == 15))
                            if k == 0:
                                leave(mm, s)
                    mm.then_inc(sem(full("dve", g)), n[full("dve", g)].up())

            rms(SUMSQ, 1)
            rms(SQ1, KT)
            token_major("va", H2, 2, "act")
            stationary("qa", H2, "act")
            stationary("ka", H2, "act")
            stationary("qkb", H2, "act")
            token_major("vb", H2, 2, "act")
            n["load_glw"].n += 2
            pe.wait_ge(sem("load_glw"), n["load_glw"].now())
            take(4, "act")
            for k in range(KT):
                mm = pe.matmul(psum[0:16, 4, 0:T], GLW[:, 16 * k:16 * k + 16], H2[:, k, :], start=(k == 0),
                               stop=(k == KT - 1))
            mm.then_inc(sem(full("act", 4)), n[full("act", 4)].up())
            stationary("gate_ab", H2, "act")
            pe.wait_ge(sem("low_ready"), n["low_ready"].next())
            for q in range(2):
                take(5 + q, "dve")
                for m in range(2):
                    mm = pe.matmul(psum[:, 5 + q, m * T:(m + 1) * T], GWG[0:16, (2 * q + m) * P:(2 * q + m + 1) * P],
                                   GLO[0:16, :], start=True, stop=True)
                mm.then_inc(sem(full("dve", 5 + q)), n[full("dve", 5 + q)].up())
            attend(HT, 2,
                   lambda u: pe.matmul(psum[:, 4 + u, 0:T], DQ[:, u * P:(u + 1) * P], DK, start=True, stop=True),
                   lambda u, k: DP[u][:, k * P:(k + 1) * P],
                   (2, lambda u, k: (psum[:, 0, u * P:(u + 1) * P], DV[:, k, :], DT_[u][:, k * P:(k + 1) * P])), 0)

            def linear_attention(turns, nv, f):
                per = {n["levels_ready"]: 1, n["head_scores"]: 2}
                for b in (4, 5, 6):
                    per[n[full("dve", b)]] = 4 if b < 6 else 2
                for b in range(nv):
                    per[n[full("dve", b)]] = 1
                with rounds(pe, turns, per):
                    pe.wait_ge(sem("levels_ready"), n["levels_ready"].next())
                    for h in range(2):
                        for b in range(2):
                            o = h * T + b * P
                            for half in range(2):
                                take(4 + half, "dve")
                                for l in range(4):
                                    mm = pe.matmul(psum[:, 4 + half, l * P:(l + 1) * P],
                                                   f["KL"][:, 4 * half + l, o:o + P], f["QL"][:, 4 * half + l, o:o + P],
                                                   start=True, stop=True)
                                mm.then_inc(sem(full("dve", 4 + half)), n[full("dve", 4 + half)].up())
                        take(6, "dve")
                        pe.matmul(psum[:, 6, 0:P], f["KL"][:, LEVELS, h * T:h * T + P],
                                       f["QL"][:, LEVELS, h * T + P:h * T + 2 * P], start=True, stop=True).then_inc(
                            sem(full("dve", 6)), n[full("dve", 6)].up())
                    for h in range(2):
                        pe.wait_ge(sem("head_scores"), n["head_scores"].next())
                        for e in range(nv):
                            tile = h * nv + e
                            bank, o = tile // 2, (tile % 2) * T
                            if tile % 2 == 0:
                                take(bank, "dve")
                            v = lambda t: f["V"][:, t, tile * P:(tile + 1) * P]
                            pe.matmul(psum[:, bank, o:o + P], v(0), f["SC"][:, h, 0, :], start=True, stop=True)
                            pe.matmul(psum[:, bank, o + P:o + 2 * P], v(1), f["SC"][:, h, 1, :], start=True, stop=False)
                            mm = pe.matmul(psum[:, bank, o + P:o + 2 * P], v(0), f["SC"][:, h, 2, :],
                                           start=False, stop=True)
                            if tile % 2 == 1:
                                mm.then_inc(sem(full("dve", bank)), n[full("dve", bank)].up())

            def head_norm(src, heads, each, sq):
                pe.wait_ge(sem("squares_ready"), n["squares_ready"].next())
                for h in range(heads):
                    b = (h // 2) % 4
                    if h % 2 == 0:
                        take(b, "dve")
                    for e in range(each):
                        mm = pe.matmul(psum[:, b, (h % 2) * T:(h % 2 + 1) * T], ones[:, :], sq[:, h * each + e, :],
                                       start=(e == 0), stop=(e == each - 1))
                    if h % 2 == 1:
                        mm.then_inc(sem(full("dve", b)), n[full("dve", b)].up())

            linear_attention(2, 2, GLA)
            head_norm(Y, 4, 2, GLA["SQ"])
            pe.wait_ge(sem("y_ready"), n["y_ready"].next())
            stationary("ab_out", Y, "dve")

            rms(SUMSQ, 1)
            stationary("u", H2, "act")
            n["load_s5"].n += 3
            pe.wait_ge(sem("dt_spread"), n["dt_spread"].next())
            pe.wait_ge(sem("load_s5"), n["load_s5"].now())
            turn([(S5N[0:32, q * P:(q + 1) * P], q * 32) for q in range(3)], 4, "dve")
            for c in range(2):
                pe.wait_ge(sem("b_ready"), n["b_ready"].next())
                for q in range(2):
                    turn([(S5B[:, (4 * q + g) * P:(4 * q + g + 1) * P], g * P) for g in range(4)], 6 + q, "dve")
            n["load_s5c"].n += 4
            pe.wait_ge(sem("load_s5c"), n["load_s5c"].now())
            for c in range(2):
                for q in range(2):
                    turn([((S5C, S5CI)[c][:, 4 * q + g, :], g * P) for g in range(4)], 6 + q, "dve")
            pe.wait_ge(sem("s5_tables"), n["s5_tables"].next())
            for half in range(2):
                for j in range(16):
                    ut, r = half * 4 + j // 4, slice(32 * (j % 4), 32 * (j % 4) + 32)
                    take(j % 4, "act")
                    for c in range(2):
                        mm = pe.matmul(psum[:, j % 4, c * T:(c + 1) * T], BT[r, c, ut, :], SU5[r, ut, :],
                                       start=True, stop=True)
                    mm.then_inc(sem(full("act", j % 4)), n[full("act", j % 4)].up())
                if half == 0:
                    stationary("qd", H2, "act")
                    stationary("fd", H2, "act")
                else:
                    token_major("id", H2, 2, "act")
                    stationary("gate_cd", H2, "act")
                pe.wait_ge(sem("states_ready"), n["states_ready"].next())
                for q in range(4):
                    ut = half * 4 + q
                    b = 4 + q % 2
                    take(b, "dve")
                    for j in range(4):
                        r = slice(32 * j, 32 * j + 32)
                        for c in range(2):
                            mm = pe.matmul(psum[r, b, 0:T], CT[:, c, ut, r], SX[:, c, 4 * q + j, :],
                                           start=(c == 0), stop=(c == 1))
                    mm.then_inc(sem(full("dve", b)), n[full("dve", b)].up())
            pe.wait_ge(sem("glu_in"), n["glu_in"].next())
            stationary("glu", Y5, "act")
            linear_attention(4, 1, HG)
            head_norm(YD, 8, 1, HG["SQ"])
            pe.wait_ge(sem("y_ready"), n["y_ready"].next())
            stationary("cd_out", Y5P, "dve")
            pe.wait_ge(sem("squares_ready"), n["squares_ready"].next())
            sum_rows(SUMSQ, 4, "dve", 1)
            pe.wait_ge(sem("normed"), n["normed"].next())
            for t in range(2):
                for k in range(0, KT, 4):
                    turn([(FIN[:, k + m, t * P:(t + 1) * P], m * P) for m in range(4)], (k // 4) % 4, "act")

        @block.scalar
        def _(act):
            n = Counts()
            A = act.activation

            def settled(name):
                for b in range(4):
                    act.wait_ge(sem(free("act", b)), n[free("act", b)].now())
                act.sem_inc(sem(name), n[name].up())

            def begin():
                for b in range(8):
                    act.sem_inc(sem(free("act", b)), n[free("act", b)].up())

            def load(dst, src, name):
                act.dma_start(dst, src).then_inc(sem(name), 16)

            def emit(name, fn, extra=None):
                per = {n[f("act", s)]: 1 for s in range(4) for f in (full, free)}
                for k, v in (extra or {}).items():
                    per[n[k]] = v

                def body(i):
                    for s in range(4):
                        act.wait_ge(sem(full("act", s)), n[full("act", s)].next())
                        fn(i, s).then_inc(sem(free("act", s)), n[free("act", s)].up())

                if ROUNDS[name] == 1:
                    body(0)
                else:
                    with rounds(act, ROUNDS[name], per) as i:
                        body(i)

            def one(t, k):
                return t[:, ds(k, 1), :].rearrange("p a t -> p (a t)")

            begin()
            for j in (3, 1, 0, 2, 4):
                r0 = 0
                for name, rows in PACKS[j]:
                    src = dram[name]
                    load(PACK[j][r0:r0 + rows, :], src.rearrange("(r p) -> r p", p=P), "load_packs")
                    r0 += rows
            load(XN, dram["x"].rearrange("(t p) n -> p t n", p=P), "load_x")
            load(CN, dram["ctx"].rearrange("(t p) n -> p t n", p=P), "load_ctx")
            load(TAPN[0:TAPS, :], dram["conv_w"], "load_taps")
            load(VROW[0:1, :], dram["b_in"][WV:WV + HW].rearrange("(a n) -> a n", a=1), "load_vrow")
            for q in range(2):
                for k in range(0, KT, 2):
                    b = (k // 2) % 4
                    act.wait_ge(sem(full("act", b)), n[full("act", b)].next())
                    src = psum[:, b, :].rearrange("p (a t) -> p a t", a=2)
                    dst = (X, C)[q][:, k:k + 2, :]
                    ins = act.activation(dst, src, ACT.Copy)
                    ins.then_inc(sem(free("act", b)), n[free("act", b)].up())
            settled("x_turned")
            act.wait_ge(sem("packs_turned"), n["packs_turned"].next())
            for q, name in enumerate(("c", "c_ctx")):
                A(cvec[:, :, q], col(name, 0, KT), ACT.Silu).then_inc(sem("scalar_step"), n["scalar_step"].up())
                act.wait_ge(sem("scalar_step"), n["scalar_step"].now())
            act.sem_inc(sem("cvec_ready"), n["cvec_ready"].up())
            per = {n[f("act", b)]: 1 for b in range(2) for f in (full, free)}
            with rounds(act, ROUNDS["mod"] // 2, per) as i:
                for g in range(2):
                    act.wait_ge(sem(full("act", g)), n[full("act", g)].next())
                    A(MODROW[0:2, ds(i * 1024 + g * 512, 512)], psum[0:2, g, :], ACT.Copy).then_inc(
                        sem(free("act", g)), n[free("act", g)].up())
            settled("mod_rows")

            def root(what=RS):
                act.wait_ge(sem("norm_var"), n["norm_var"].next())
                A(what, what, ACT.Sqrt).then_inc(sem("norm_std"), n["norm_std"].up())

            root()
            root(MEAN)
            act.wait_ge(sem("bq_ready"), n["bq_ready"].next())

            def tokens(dst, toks=2):
                return lambda i, s: A(dst[:, :, ds(i * 512 + s * P, P)],
                                      psum[:, s, 0:toks * P].rearrange("p (t c) -> p t c", t=toks), ACT.Copy)

            def tiles(name, dst, func, bias=None, scale=1.0):
                def fn(i, s):
                    for m in range(WIDE[name]):
                        k = i * (4 * WIDE[name]) + (s * WIDE[name] + m)
                        kw = {} if bias is None else {"bias": bias[0][:, ds(i * (4 * WIDE[name]) + (
                            s * WIDE[name] + m + bias[1]), 1)]}
                        ins = A(one(dst, k), psum[:, s, m * T:(m + 1) * T], func, scale=scale, **kw)
                    return ins
                return fn

            emit("q", tiles("q", NQ, ACT.Identity, (bq, 0), 0.125))
            emit("k", lambda i, s: A(one(NK, i * 4 + s), psum[:, s, :], ACT.Identity,
                                     bias=cols[:, ds(i * 4 + (COL["b_in"] + WK // P + s), 1)]))
            emit("v", tokens(NV, 4))
            settled("qkv_ready")

            def softmax_rounds(turns, nunits, probs, turned, width):
                per = {n["scores_max"]: nunits, n["exp_done"]: nunits, n["probs_turned"]: nunits}
                for b in range(2):
                    per[n[full("act", 6 + b)]] = nunits // 2
                    per[n[free("act", 6 + b)]] = nunits // 2
                with rounds(act, turns, per):
                    def exp(u):
                        act.wait_ge(sem("scores_max"), n["scores_max"].next())
                        kw = dict(accum_out=small[:, 4 + u % 2:5 + u % 2]) if width == 512 else {}
                        A(probs[u % 2], psum[:, 4 + u % 2, 0:width], ACT.Exp,
                                           bias=small[:, 2 + u % 2:3 + u % 2], **kw).then_inc(
                            sem("exp_done"), n["exp_done"].up())

                    exp(0)
                    for u in range(nunits):
                        if u + 1 < nunits:
                            exp(u + 1)
                        b = 6 + u % 2
                        act.wait_ge(sem(full("act", b)), n[full("act", b)].next())
                        A(turned[u % 2], psum[:, b, 0:width], ACT.Copy).then_inc(
                            sem("probs_turned"), n["probs_turned"].up())
                        act.wait_ge(sem("probs_turned"), n["probs_turned"].now())
                        act.sem_inc(sem(free("act", b)), n[free("act", b)].up())

            softmax_rounds(HT, 4, PR, PT, 512)
            act.wait_ge(sem("att_ready"), n["att_ready"].next())
            load(SGN, dram["sgu_w"].rearrange("g p q -> p g q"), "load_sgu")
            load(SGB[0:HT, :], dram["sgu_b"], "load_sgu")
            emit("a2", tiles("a2", CV, ACT.Sigmoid, (cols, COL["b_in"] + A2 // P)))
            settled("sig_ready")
            emit("su", tiles("su", ZU, ACT.Gelu_apprx_tanh, (cols, COL["b_in"] + SU // P)))
            emit("sv", tiles("sv", ZV, ACT.Gelu_apprx_tanh, (cols, COL["b_in"] + SV // P)))
            settled("uv_ready")
            for q in range(2):
                act.wait_ge(sem(full("act", 6 + q)), n[full("act", 6 + q)].next())
                ins = A(WST[:, 4 * q:4 * q + 4, :], psum[:, 6 + q, :].rearrange("p (g q) -> p g q", g=4), ACT.Copy)
                ins.then_inc(sem("sgu_turned"), n["sgu_turned"].up())
                act.wait_ge(sem("sgu_turned"), n["sgu_turned"].now())
                act.sem_inc(sem(free("act", 6 + q)), n[free("act", 6 + q)].up())
            root()
            for j in range(0, HT, 2):
                b = (j // 2) % 4
                act.wait_ge(sem(full("act", b)), n[full("act", b)].next())
                ins = A(VT[:, :, j * P:(j + 2) * P], psum[:, b, :].rearrange("p (t m) -> p t m", t=2), ACT.Copy)
                ins.then_inc(sem("sgu_turned"), n["sgu_turned"].up())
                act.wait_ge(sem("sgu_turned"), n["sgu_turned"].now())
                act.sem_inc(sem(free("act", b)), n[free("act", b)].up())

            def gate(name, k0):
                emit(name, tiles(name, GATE, ACT.Sigmoid, (cols, COL["b_in"] + (WG + k0) // P)))
                settled("gate_ready")

            gate("gate_conv", 0)
            root()
            act.wait_ge(sem("conv_normed"), n["conv_normed"].next())
            A(CV, CV, ACT.Silu).then_inc(sem("conv_ready"), n["conv_ready"].up())
            act.wait_ge(sem("conv_ready"), n["conv_ready"].now())
            act.wait_ge(sem("gate_used"), n["gate_used"].next())
            gate("gate_sgu", D)
            act.wait_ge(sem("gate_used"), n["gate_used"].next())
            gate("gate_att", 2 * D)
            root()
            act.wait_ge(sem("gate_used"), n["gate_used"].next())
            load(GLW, dram["ab_w_in_2"][:, GLOW:GLOW + 16].rearrange("(k p) c -> p k c", p=P), "load_glw")
            load(GWG[0:16, :], dram["gla_w_gate_2"], "load_glw")

            def ff1(i, s):
                act.wait_ge(sem("hidden_taken"), n["hidden_taken"].next())
                ins = A(RELU[:, s, :], psum[:, s, 0:T], ACT.Relu, bias=cols[:, ds(i * 4 + (COL["b_ff1"] + s), 1)])
                ins.then_inc(sem("hidden_raw"), n["hidden_raw"].up())
                act.wait_ge(sem("hidden_raw"), n["hidden_raw"].now())
                return act.nop()

            emit("ff1", ff1, extra={"hidden_raw": 4, "hidden_taken": 4})
            root()
            root()
            emit("va", tokens(VA))
            emit("qa", tiles("qa", QA, ACT.Copy, scale=float(P) ** -0.5))
            emit("ka", tiles("ka", KA, ACT.Copy))
            emit("qkb", tiles("qkb", QKB, ACT.Copy))
            emit("vb", tokens(VB))
            act.wait_ge(sem(full("act", 4)), n[full("act", 4)].next())
            A(GLO[0:16, :], psum[0:16, 4, 0:T], ACT.Copy).then_inc(sem("low_ready"), n["low_ready"].up())
            act.wait_ge(sem("low_ready"), n["low_ready"].now())
            act.sem_inc(sem(free("act", 4)), n[free("act", 4)].up())
            emit("gate_ab", tiles("gate_ab", GATE2, ACT.Silu))
            settled("ab_ready")
            act.wait_ge(sem("decay_in"), n["decay_in"].next())
            A(GTMP, GTMP, ACT.Exp, scale=-1.0).then_inc(sem("scalar_step"), n["scalar_step"].up())
            act.wait_ge(sem("scalar_step"), n["scalar_step"].now())
            A(GTMP, GTMP, ACT.Ln, bias=1.0).then_inc(sem("decay_ln"), n["decay_ln"].up())
            act.wait_ge(sem("decay_in"), n["decay_in"].next())
            A(GG, GG3, ACT.Exp, scale=-1.0 / 16.0).then_inc(sem("decay_exp"), n["decay_exp"].up())
            softmax_rounds(HT, 2, DP, DT_, 256)
            root(GLA["SQ"][:, 0:4, :])
            root()
            act.wait_ge(sem("y_used"), n["y_used"].next())
            load(S5N[0:32, 0:P], dram["s5_lam_re_2"].rearrange("(j a) p -> j (a p)", a=2), "load_s5")
            load(S5N[0:32, P:2 * P], dram["s5_lam_im_2"].rearrange("(j a) p -> j (a p)", a=2), "load_s5")
            load(S5DT[0:32, :], dram["s5_log_dt_2"].rearrange("(j a) -> j a", a=2), "load_s5")
            for q, name in enumerate(("s5_b_re_2", "s5_b_im_2")):
                load(S5BN[:, q, :, :], dram[name].rearrange("(j a) p h -> (a p) j h", a=2), "load_s5b")
            for q, name in enumerate(("s5_c_re_2", "s5_c_im_2")):
                for r in range(2):
                    load((S5C, S5CI)[q][:, :, r * 64:r * 64 + 64],
                         dram[name].rearrange("(u g) h p -> (g h) u p", g=8), "load_s5c")
            emit("u", tiles("u", SU5, ACT.Copy))
            settled("u_ready")
            act.wait_ge(sem("s5_dt"), n["s5_dt"].next())
            A(s5p[:, 2, :], s5p[:, 2, :], ACT.Exp).then_inc(sem("s5_act"), n["s5_act"].up())
            act.wait_ge(sem("s5_dt"), n["s5_dt"].next())
            A(s5p[:, 3, :], s5p[:, 3, :], ACT.Exp).then_inc(sem("scalar_step"), n["scalar_step"].up())
            act.wait_ge(sem("scalar_step"), n["scalar_step"].now())
            A(s5p[:, 5, :], s5p[:, 5, :], ACT.Sin).then_inc(sem("scalar_step"), n["scalar_step"].up())
            act.wait_ge(sem("scalar_step"), n["scalar_step"].now())
            A(s5p[:, 4, :], s5p[:, 4, :], ACT.Sin).then_inc(sem("s5_act"), n["s5_act"].up())
            for half in range(2):
                for j in range(16):
                    act.wait_ge(sem(full("act", j % 4)), n[full("act", j % 4)].next())
                    A(SX[:, :, j, :], psum[:, j % 4, :].rearrange("p (c t) -> p c t", c=2), ACT.Copy).then_inc(
                        sem(free("act", j % 4)), n[free("act", j % 4)].up())
                settled("inputs_ready")
                if half == 0:
                    emit("qd", tiles("qd", QD, ACT.Silu))
                    emit("fd", tiles("fd", FD, ACT.Sigmoid))
                else:
                    emit("id", tokens(ID))
                    emit("gate_cd", tiles("gate_cd", GATE3, ACT.Silu))
                    settled("cd_ready")
            act.wait_ge(sem("s5_sum"), n["s5_sum"].next())
            A(Y5, Y5, ACT.Gelu_apprx_tanh).then_inc(sem("s5_gelu"), n["s5_gelu"].up())
            emit("glu", tiles("glu", SIG, ACT.Sigmoid, (cols, COL["s5_b_glu_2"])))
            settled("glu_ready")
            act.wait_ge(sem("gamma_in"), n["gamma_in"].next())
            A(small[:, 0:16], small[:, 0:16], ACT.Exp).then_inc(sem("gamma_exp"), n["gamma_exp"].up())
            root(HG["SQ"])
            root()
            OUTB = at(12288, 2, D)
            act.wait_ge(sem("y_used"), n["y_used"].next())
            for t in range(2):
                for k in range(0, KT, 4):
                    b = (k // 4) % 4
                    act.wait_ge(sem(full("act", b)), n[full("act", b)].next())
                    A(OUTB[:, t, k * P:(k + 4) * P], psum[:, b, :], ACT.Copy).then_inc(
                        sem(free("act", b)), n[free("act", b)].up())
            for b in range(4):
                act.wait_ge(sem(free("act", b)), n[free("act", b)].now())
            act.sem_inc(sem("result_ready"), 1)

        @block.gpsimd
        def _(pool):
            n = Counts()

            pool.memset(ident[:, :], 0.0).then_inc(sem("pool_step"), n["pool_step"].up())
            pool.wait_ge(sem("pool_step"), n["pool_step"].now())
            pool.memset(ones[:, :], 1.0).then_inc(sem("consts_ready"), n["consts_ready"].up())
            pool.wait_ge(sem("consts_ready"), n["consts_ready"].now())
            pool.affine_select(out=ident[:, :], in_=ident[:, :], compare_op=ALU.not_equal, fill=1.0, base=0,
                                  pattern=[[-1, P]], channel_multiplier=1).then_inc(
                sem("consts_ready"), n["consts_ready"].up())
            pool.wait_ge(sem("consts_ready"), n["consts_ready"].now())
            pool.memset(mirror[:, :], 0.0).then_inc(sem("pool_step"), n["pool_step"].up())
            pool.wait_ge(sem("pool_step"), n["pool_step"].now())
            for r in range(2):
                q = slice(64 * r, 64 * r + 64)
                pool.affine_select(out=mirror[q, q], in_=mirror[q, q], compare_op=ALU.not_equal, fill=1.0,
                                      base=1 - GRID, pattern=[[1, 64]], channel_multiplier=1).then_inc(
                    sem("pool_step" if r == 0 else "consts_ready"), n["pool_step" if r == 0 else "consts_ready"].up())
                pool.wait_ge(sem("pool_step" if r == 0 else "consts_ready"), n["pool_step" if r == 0 else "consts_ready"].now())
            pool.memset(padrow[:, :, :], 0.0).then_inc(sem("pool_step"), n["pool_step"].up())
            pool.wait_ge(sem("pool_step"), n["pool_step"].now())
            pool.dma_start(padrow[:, :, 48:48 + DCS],
                           dram["na_rpb"].rearrange("h d k -> (h d) k").rearrange("(p a) k -> p a k", a=2)).then_inc(
                sem("load_rpb"), 16)
            pool.wait_ge(sem("load_rpb"), 16)
            pool.dma_start(bias_rows.rearrange("h d k -> (h d) k").rearrange("(p a) k -> p a k", a=2),
                           padrow[:, :, :]).then_inc(sem("load_rows"), 16)
            pool.wait_ge(sem("load_rows"), 16)
            for h in range(NHEAD):
                for r in range(2):
                    src = bass.AP(bias_rows.tensor, h * DRS * PADW + (5 - r) * PADW,
                                  [[1, GRID], [PADW, 6], [1, GRID]])
                    pool.dma_start(BIAS[64 * r:64 * r + 64, h, :, :], src).then_inc(sem("load_bias"), 16)
            pool.memset(WMASK, 0.0).then_inc(sem("pool_step"), n["pool_step"].up())
            pool.wait_ge(sem("pool_step"), n["pool_step"].now())
            for r in range(2):
                q = slice(64 * r, 64 * r + 64)
                pool.affine_select(out=WMASK[q, 0:48], in_=WMASK[q, 0:48], compare_op=ALU.is_ge, fill=NEG,
                                      base=WIN // 2 - (GRID - 1), pattern=[[1, 48]], channel_multiplier=1).then_inc(
                    sem("pool_step"), n["pool_step"].up())
                pool.wait_ge(sem("pool_step"), n["pool_step"].now())
                pool.affine_select(out=WMASK[q, 16:64], in_=WMASK[q, 16:64], compare_op=ALU.is_ge, fill=NEG,
                                      base=WIN // 2 - 1 - 16 + GRID - 1, pattern=[[-1, 48]], channel_multiplier=-1).then_inc(
                    sem("pool_step" if r == 0 else "window_mask"), n["pool_step" if r == 0 else "window_mask"].up())
                pool.wait_ge(sem("pool_step" if r == 0 else "window_mask"), n["pool_step" if r == 0 else "window_mask"].now())
            def numbers():
                n["gate_used"].n = 3
                pool.wait_ge(sem("gate_used"), n["gate_used"].now())
                pool.iota(DIFF, pattern=[[P, 2], [-1, T]], base=0, channel_multiplier=1).then_inc(
                    sem("iotas"), n["iotas"].up())
                pool.wait_ge(sem("iotas"), n["iotas"].now())
                pool.iota(IDX[:, 0, :], pattern=[[1, P]], base=0, channel_multiplier=0).then_inc(
                    sem("iotas"), n["iotas"].up())
                pool.wait_ge(sem("iotas"), n["iotas"].now())
                pool.iota(IDX[:, 1, :], pattern=[[0, P]], base=0, channel_multiplier=1).then_inc(
                    sem("iotas"), n["iotas"].up())
                pool.wait_ge(sem("iotas"), n["iotas"].now())
                pool.iota(IDX[:, 2, :], pattern=[[1, P]], base=0, channel_multiplier=-1).then_inc(
                    sem("iotas"), n["iotas"].up())
                pool.wait_ge(sem("iotas"), n["iotas"].now())

            numbers()

        @block.vector
        def _(v):
            n = Counts()

            for b in range(8):
                v.sem_inc(sem(free("dve", b)), 1)
                n[free("dve", b)].n = 1

            def evac(name, fn, steps=0):
                per = {n["vector_step"]: steps} | {n[f("dve", s)]: 1 for s in range(4) for f in (full, free)}

                def body(i):
                    for s in range(4):
                        v.wait_ge(sem(full("dve", s)), n[full("dve", s)].next())
                        fn(i, s)

                if ROUNDS[name] == 1:
                    body(0)
                else:
                    with rounds(v, ROUNDS[name], per) as i:
                        body(i)

            def one(t, k):
                return t[:, ds(k, 1), :].rearrange("p a t -> p (a t)")

            for j in range(5):
                v.wait_ge(sem(full("dve", j)), n[full("dve", j)].next())
                rows = sum(r for _, r in PACKS[j])
                v.tensor_copy(cols[:, j * P:j * P + rows], psum[:, j, 0:rows]).then_inc(
                    sem(free("dve", j)), n[free("dve", j)].up())
                v.wait_ge(sem(free("dve", j)), n[free("dve", j)].now())
            v.sem_inc(sem("packs_turned"), n["packs_turned"].up())
            v.wait_ge(sem(full("dve", 5)), n[full("dve", 5)].next())
            v.tensor_copy(taps[:, :, 0:TAPS], psum[:, 5, 0:256].rearrange("p (a b) -> p a b", a=HT)[:, :, 0:TAPS]).then_inc(
                sem(free("dve", 5)), n[free("dve", 5)].up())
            v.wait_ge(sem(free("dve", 5)), n[free("dve", 5)].now())

            def finish_root(b, count, rs=RS):
                v.wait_ge(sem(full("dve", b)), n[full("dve", b)].next())
                v.tensor_scalar(rs, psum[:, b, 0:T], 1.0 / count, EPS, ALU.mult, ALU.add).then_inc(
                    sem("norm_var"), n["norm_var"].up())
                v.wait_ge(sem("norm_var"), n["norm_var"].now())
                v.wait_ge(sem("norm_std"), n["norm_std"].next())
                v.reciprocal(rs, rs).then_inc(sem(free("dve", b)), n[free("dve", b)].up())
                v.wait_ge(sem(free("dve", b)), n[free("dve", b)].now())

            def square(x, total=SUMSQ):
                v.tensor_tensor(SQT, x, x, ALU.mult).then_inc(sem("vector_step"), n["vector_step"].up())
                v.wait_ge(sem("vector_step"), n["vector_step"].now())
                v.tensor_tensor(total[:, 0, :], total[:, 0, :], SQT, ALU.add).then_inc(
                    sem("vector_step"), n["vector_step"].up())
                v.wait_ge(sem("vector_step"), n["vector_step"].now())

            def no_squares(total=SUMSQ):
                v.memset(total, 0.0).then_inc(sem("vector_step"), n["vector_step"].up())
                v.wait_ge(sem("vector_step"), n["vector_step"].now())

            def rms_norm(src, dst, b, a, shift, summed=True):
                if summed:
                    v.sem_inc(sem("squares_ready"), n["squares_ready"].up())
                else:
                    v.tensor_tensor(SQ1, src, src, ALU.mult).then_inc(
                        sem("squares_ready"), n["squares_ready"].up())
                    v.wait_ge(sem("squares_ready"), n["squares_ready"].now())
                finish_root(b, D)
                if shift is not None:
                    v.tensor_tensor(SQ1, src, over(RS, KT), ALU.mult).then_inc(
                        sem("vector_step"), n["vector_step"].up())
                    v.wait_ge(sem("vector_step"), n["vector_step"].now())
                for k in range(KT):
                    if shift is None:
                        ins = v.scalar_tensor_tensor(out=dst[:, k, :], in0=src[:, k, :], scalar=a(k), in1=RS,
                                                     op0=ALU.mult, op1=ALU.mult)
                    else:
                        ins = v.tensor_scalar(dst[:, k, :], SQ1[:, k, :], a(k), shift(k), ALU.mult, ALU.add)
                ins.then_inc(sem("normed"), n["normed"].up())
                v.wait_ge(sem("normed"), n["normed"].now())

            v.wait_ge(sem("x_turned"), n["x_turned"].next())
            for src, total in ((X, SUMSQ), (C, SUMSQ_C)):
                no_squares(total)
                for k in range(KT):
                    square(src[:, k, :], total)
                v.sem_inc(sem("squares_ready"), n["squares_ready"].up())
            for q, rs in enumerate((RS, MEAN)):
                finish_root(4 + q, D, rs)
            v.wait_ge(sem(full("dve", 4)), n[full("dve", 4)].next())
            v.tensor_tensor(mod[:, :, :], psum[:, 4, 0:192].rearrange("p (a c) -> p a c", c=2),
                            over(col("b_mod", 0, 96), 2, 2), ALU.add).then_inc(
                sem(free("dve", 4)), n[free("dve", 4)].up())
            v.wait_ge(sem(free("dve", 4)), n[free("dve", 4)].now())
            for g, (m0, q, name) in enumerate(((16, 0, "norm1_g"), (16, 1, "norm1_g"), (64, 0, "norm2_g"))):
                v.scalar_tensor_tensor(out=gain[:, g, :], in0=mod[:, m0:m0 + KT, q], scalar=1.0, in1=col(name, 0, KT),
                                          op0=ALU.add, op1=ALU.mult).then_inc(
                    sem("vector_step"), n["vector_step"].up())
                v.wait_ge(sem("vector_step"), n["vector_step"].now())
            v.tensor_scalar(bq[:, :], col("b_in", WQ // P, HT), 0.125, None, ALU.mult).then_inc(
                sem("bq_ready"), n["bq_ready"].up())
            v.wait_ge(sem("bq_ready"), n["bq_ready"].now())

            for q, (src, rs) in enumerate(((X, RS), (C, MEAN))):
                v.tensor_tensor(XR, src, over(rs, KT), ALU.mult).then_inc(
                    sem("vector_step"), n["vector_step"].up())
                v.wait_ge(sem("vector_step"), n["vector_step"].now())
                for k in range(KT):
                    ins = v.tensor_scalar(H[:, k, q * T:(q + 1) * T], XR[:, k, :], gain[:, q, k:k + 1],
                                          mod[:, k, q:q + 1], ALU.mult, ALU.add)
                ins.then_inc(sem("normed"), n["normed"].up())
                v.wait_ge(sem("normed"), n["normed"].now())

            n["load_bias"].n += 32
            v.wait_ge(sem("load_bias"), n["load_bias"].now())
            v.wait_ge(sem("window_mask"), n["window_mask"].next())
            bv = at(24576, NHEAD * 6, GRID)
            v.tensor_tensor(bv, bv, over(WMASK, NHEAD * 6), ALU.add).then_inc(
                sem("vector_step"), n["vector_step"].up())
            v.wait_ge(sem("vector_step"), n["vector_step"].now())
            v.wait_ge(sem("qkv_ready"), n["qkv_ready"].next())

            def softmax_rounds(turns, nunits, stage, add, weigh, probs, dst, dst_bank, steps, width):
                per = {n["vector_step"]: steps, n["scores_max"]: nunits, n["exp_done"]: nunits,
                       n["probs_ready"]: nunits, n["heads_staged"]: 1, n[full("dve", dst_bank)]: 1,
                       n[free("dve", dst_bank)]: 1}
                for b in range(2):
                    per[n[full("dve", 4 + b)]] = nunits // 2
                    per[n[free("dve", 4 + b)]] = nunits // 2
                with rounds(v, turns, per) as i:
                    stage(i)

                    def top(u):
                        b = 4 + u % 2
                        v.wait_ge(sem(full("dve", b)), n[full("dve", b)].next())
                        add(i, u, b)
                        v.tensor_reduce(small[:, u % 2:u % 2 + 1], psum[:, b, 0:width], AX_X, ALU.max).then_inc(
                            sem("vector_step"), n["vector_step"].up())
                        v.wait_ge(sem("vector_step"), n["vector_step"].now())
                        v.tensor_scalar(small[:, 2 + u % 2:3 + u % 2], small[:, u % 2:u % 2 + 1], -1.0, None,
                                           ALU.mult).then_inc(sem("scores_max"), n["scores_max"].up())
                        v.wait_ge(sem("scores_max"), n["scores_max"].now())

                    top(0)
                    for u in range(nunits):
                        if u + 1 < nunits:
                            top(u + 1)
                        v.wait_ge(sem("exp_done"), n["exp_done"].next())
                        weigh(u)
                        v.reciprocal(small[:, 6 + u % 2:7 + u % 2], small[:, 4 + u % 2:5 + u % 2]).then_inc(
                            sem(free("dve", 4 + u % 2)), n[free("dve", 4 + u % 2)].up())
                        v.wait_ge(sem(free("dve", 4 + u % 2)), n[free("dve", 4 + u % 2)].now())
                        v.tensor_scalar(probs[u % 2], probs[u % 2], small[:, 6 + u % 2:7 + u % 2], None, ALU.mult).then_inc(
                            sem("probs_ready"), n["probs_ready"].up())
                        v.wait_ge(sem("probs_ready"), n["probs_ready"].now())
                    v.wait_ge(sem(full("dve", dst_bank)), n[full("dve", dst_bank)].next())
                    v.tensor_copy(one(dst, i), psum[:, dst_bank, 0:T]).then_inc(
                        sem(free("dve", dst_bank)), n[free("dve", dst_bank)].up())
                    v.wait_ge(sem(free("dve", dst_bank)), n[free("dve", dst_bank)].now())

            def na_stage(i):
                v.tensor_copy(ST_Q, NQ[:, ds(i, 1), :])
                v.tensor_copy(ST_K, NK[:, ds(i, 1), :])
                for b in range(2):
                    v.tensor_copy(ST_B[:, b:b + 3:2, :].rearrange("p h (k c) -> p h k c", k=4),
                                  BIAS[:, ds(2 * i, 2), 2 - 2 * b:6 - 2 * b, :])
                v.tensor_copy(ST_V, NV[:, :, ds(i * P, P)]).then_inc(sem("heads_staged"), n["heads_staged"].up())
                v.wait_ge(sem("heads_staged"), n["heads_staged"].now())

            softmax_rounds(HT, 4, na_stage, lambda i, u, b: None, lambda u: None, PR, ATT, 0, 4, 512)
            v.sem_inc(sem("att_ready"), n["att_ready"].up())
            v.memset(U[:, :, 0:PAD], 0.0)
            v.memset(U[:, :, T + PAD:T + 2 * PAD], 0.0).then_inc(sem("vector_step"), n["vector_step"].up())
            v.wait_ge(sem("vector_step"), n["vector_step"].now())
            v.wait_ge(sem("sig_ready"), n["sig_ready"].next())

            def glu_in(i, s):
                v.scalar_tensor_tensor(out=U[:, ds(i * 4 + s, 1), PAD:PAD + T].rearrange("p a t -> p (a t)"),
                                               in0=psum[:, s, 0:T],
                                               scalar=cols[:, ds(i * 4 + (COL["b_in"] + A1 // P + s), 1)],
                                               in1=one(CV, i * 4 + s), op0=ALU.add, op1=ALU.mult).then_inc(
                    sem(free("dve", s)), n[free("dve", s)].up())
                v.wait_ge(sem(free("dve", s)), n[free("dve", s)].now())

            evac("a1", glu_in)

            def layer_norm(z, sq, g, b_):
                v.sem_inc(sem("ln_in"), n["ln_in"].up())
                v.wait_ge(sem(full("dve", 4)), n[full("dve", 4)].next())
                v.tensor_scalar(MEAN, psum[:, 4, 0:T], 1.0 / HW, None, ALU.mult).then_inc(
                    sem(free("dve", 4)), n[free("dve", 4)].up())
                v.wait_ge(sem(free("dve", 4)), n[free("dve", 4)].now())
                v.tensor_tensor(z, z, over(MEAN, HT), ALU.subtract).then_inc(
                    sem("vector_step"), n["vector_step"].up())
                v.wait_ge(sem("vector_step"), n["vector_step"].now())
                v.tensor_tensor(sq, z, z, ALU.mult).then_inc(sem("squares_ready"), n["squares_ready"].up())
                v.wait_ge(sem("squares_ready"), n["squares_ready"].now())
                finish_root(5, HW)
                v.tensor_tensor(z, z, over(RS, HT), ALU.mult).then_inc(sem("vector_step"), n["vector_step"].up())
                v.wait_ge(sem("vector_step"), n["vector_step"].now())
                for k in range(HT):
                    ins = v.tensor_scalar(z[:, k, :], z[:, k, :], col(g, k), col(b_, k), ALU.mult, ALU.add)
                ins.then_inc(sem("vector_step"), n["vector_step"].up())
                v.wait_ge(sem("vector_step"), n["vector_step"].now())

            v.wait_ge(sem("uv_ready"), n["uv_ready"].next())
            layer_norm(ZV, SQ, "sgu_ln_g", "sgu_ln_b")
            v.sem_inc(sem("ln_out"), n["ln_out"].up())
            for g in range(HT):
                b = g % 4
                v.wait_ge(sem(full("dve", b)), n[full("dve", b)].next())
                v.tensor_tensor(ZU[:, g, :], ZU[:, g, :], psum[:, b, 0:T], ALU.mult).then_inc(
                    sem(free("dve", b)), n[free("dve", b)].up())
                v.wait_ge(sem(free("dve", b)), n[free("dve", b)].now())
            v.sem_inc(sem("sgu_ready"), n["sgu_ready"].up())
            for k in range(HT):
                v.tensor_scalar(CV[:, k, :], U[:, k, 0:T], taps[:, k, 0:1], col("conv_b", k), ALU.mult,
                                        ALU.add).then_inc(sem("vector_step"), n["vector_step"].up())
            with rounds(v, TAPS - 1, {n["vector_step"]: HT}) as j:
                for k in range(HT):
                    v.wait_ge(sem("vector_step"), n["vector_step"].now(1 - HT))
                    v.scalar_tensor_tensor(out=CV[:, k, :], in0=U[:, k, ds(j + 1, T)],
                                                   scalar=taps[:, k, ds(j + 1, 1)], in1=CV[:, k, :], op0=ALU.mult,
                                                   op1=ALU.add).then_inc(sem("vector_step"), n["vector_step"].up())
            v.wait_ge(sem("vector_step"), n["vector_step"].now())
            layer_norm(CV, SQ, "conv_ln_g", "conv_ln_b")
            v.sem_inc(sem("conv_normed"), n["conv_normed"].up())

            def branch(name, first):
                v.wait_ge(sem("gate_ready"), n["gate_ready"].next())

                def fn(i, s):
                    p = psum[:, s, :].rearrange("p (m t) -> p m t", m=2)
                    g = GATE[:, ds(i * 8 + 2 * s, 2), :]
                    m = MIX[:, ds(i * 8 + 2 * s, 2), :]
                    if first:
                        v.tensor_tensor(m, p, g, ALU.mult).then_inc(sem(free("dve", s)), n[free("dve", s)].up())
                        v.wait_ge(sem(free("dve", s)), n[free("dve", s)].now())
                    else:
                        v.tensor_tensor(g, p, g, ALU.mult).then_inc(sem(free("dve", s)), n[free("dve", s)].up())
                        v.wait_ge(sem(free("dve", s)), n[free("dve", s)].now())
                        v.tensor_tensor(m, m, g, ALU.add).then_inc(sem("vector_step"), n["vector_step"].up())
                        v.wait_ge(sem("vector_step"), n["vector_step"].now())

                evac(name, fn, steps=0 if first else 4)
                v.sem_inc(sem("gate_used"), n["gate_used"].up())

            branch("out_conv", True)
            branch("out_sgu", False)
            branch("out_att", False)
            v.sem_inc(sem("mixed"), n["mixed"].up())

            def residual(m0, bias):
                def fn(i, s):
                    v.tensor_scalar(TMP[:, 0, :], psum[:, s, 0:T],
                                            cols[:, ds(i * 4 + (COL[bias] + s), 1)],
                                            mod[:, ds(i * 4 + (m0 + s), 1), 0:1].rearrange("p a b -> p (a b)"),
                                            ALU.add, ALU.mult).then_inc(sem(free("dve", s)), n[free("dve", s)].up())
                    v.wait_ge(sem(free("dve", s)), n[free("dve", s)].now())
                    x = one(X, i * 4 + s)
                    v.tensor_tensor(x, x, TMP[:, 0, :], ALU.add).then_inc(sem("vector_step"), n["vector_step"].up())
                    v.wait_ge(sem("vector_step"), n["vector_step"].now())
                    square(x)
                return fn

            no_squares()
            evac("o", residual(32, "b_o"), steps=12)
            rms_norm(X, H2, 4, lambda k: gain[:, 2, k:k + 1], lambda k: mod[:, 48 + k, 0:1])
            for s in range(4):
                v.sem_inc(sem("hidden_taken"), n["hidden_taken"].up())
            with rounds(v, ROUNDS["ff1"], {n["hidden_raw"]: 4, n["hidden_taken"]: 4}) as i:
                for s in range(4):
                    v.wait_ge(sem("hidden_raw"), n["hidden_raw"].next())
                    v.tensor_tensor(one(HID, i * 4 + s), RELU[:, s, :], RELU[:, s, :], ALU.mult).then_inc(
                        sem("hidden_taken"), n["hidden_taken"].up())
                    v.wait_ge(sem("hidden_taken"), n["hidden_taken"].now())
            v.sem_inc(sem("hidden_ready"), n["hidden_ready"].up())
            no_squares()
            per = {n["vector_step"]: 6} | {n[f("dve", b)]: 1 for f in (full, free) for b in range(2)}
            with rounds(v, ROUNDS["ff2"] // 2, per) as i:
                for q in range(2):
                    v.wait_ge(sem(full("dve", q)), n[full("dve", q)].next())
                    v.tensor_scalar(TMP2, psum[:, q, 0:T], cols[:, ds(i * 2 + (COL["b_ff2"] + q), 1)],
                                            mod[:, ds(i * 2 + (80 + q), 1), 0:1].rearrange("p a b -> p (a b)"),
                                            ALU.add, ALU.mult).then_inc(sem(free("dve", q)), n[free("dve", q)].up())
                    v.wait_ge(sem(free("dve", q)), n[free("dve", q)].now())
                    x = one(X, i * 2 + q)
                    v.tensor_tensor(x, x, TMP2, ALU.add).then_inc(sem("vector_step"), n["vector_step"].up())
                    v.wait_ge(sem("vector_step"), n["vector_step"].now())
                    square(x)

            rms_norm(X, X, 4, lambda k: col("final_g", k), None)
            rms_norm(X, H2, 4, lambda k: col("norm_g_2", k), None, summed=False)
            n["iotas"].n += 4
            v.wait_ge(sem("iotas"), n["iotas"].now())
            v.tensor_copy(MASK, DIFF).then_inc(sem("vector_step"), n["vector_step"].up())
            v.wait_ge(sem("vector_step"), n["vector_step"].now())
            v.tensor_scalar(CNT, MASK, float(P), None, ALU.is_le).then_inc(sem("vector_step"), n["vector_step"].up())
            v.wait_ge(sem("vector_step"), n["vector_step"].now())
            for w in (3, 15):
                v.tensor_scalar(DIFF2, DIFF, w, None, ALU.bitwise_and).then_inc(
                    sem("vector_step"), n["vector_step"].up())
                v.wait_ge(sem("vector_step"), n["vector_step"].now())
                v.scalar_tensor_tensor(out=CNT, in0=DIFF2, scalar=0.0, in1=CNT, op0=ALU.is_equal, op1=ALU.add).then_inc(
                    sem("vector_step"), n["vector_step"].up())
                v.wait_ge(sem("vector_step"), n["vector_step"].now())
            v.scalar_tensor_tensor(out=CNT, in0=MASK, scalar=0.0, in1=CNT, op0=ALU.is_ge, op1=ALU.mult).then_inc(
                sem("vector_step"), n["vector_step"].up())
            v.wait_ge(sem("vector_step"), n["vector_step"].now())
            v.tensor_scalar(MASK, CNT, 0.0, NEG, ALU.is_equal, ALU.mult).then_inc(
                sem("vector_step"), n["vector_step"].up())
            v.wait_ge(sem("vector_step"), n["vector_step"].now())
            v.tensor_tensor(IDX[:, 0, :], IDX[:, 0, :], IDX[:, 1, :], ALU.bitwise_xor).then_inc(
                sem("vector_step"), n["vector_step"].up())
            v.wait_ge(sem("vector_step"), n["vector_step"].now())
            v.tensor_copy(IDXF[:, 0, :], IDX[:, 0, :]).then_inc(sem("vector_step"), n["vector_step"].up())
            v.wait_ge(sem("vector_step"), n["vector_step"].now())
            v.tensor_scalar(IDXF[:, 1, :], IDX[:, 2, :], 0.0, None, ALU.is_gt).then_inc(
                sem("vector_step"), n["vector_step"].up())
            v.wait_ge(sem("vector_step"), n["vector_step"].now())
            v.tensor_copy(LMASK[:, 0, :], ident[:, :]).then_inc(sem("vector_step"), n["vector_step"].up())
            v.wait_ge(sem("vector_step"), n["vector_step"].now())
            for l in range(1, LEVELS):
                s = float(2 ** (l - 1))
                v.scalar_tensor_tensor(out=LMASK[:, l, :], in0=IDXF[:, 0, :], scalar=s, in1=IDXF[:, 1, :],
                                          op0=ALU.is_ge, op1=ALU.mult).then_inc(
                    sem("vector_step"), n["vector_step"].up())
                v.wait_ge(sem("vector_step"), n["vector_step"].now())
                v.scalar_tensor_tensor(out=LMASK[:, l, :], in0=IDXF[:, 0, :], scalar=2 * s, in1=LMASK[:, l, :],
                                          op0=ALU.is_lt, op1=ALU.mult).then_inc(
                    sem("vector_step"), n["vector_step"].up())
                v.wait_ge(sem("vector_step"), n["vector_step"].now())
            for q in range(2):
                v.wait_ge(sem(full("dve", 5 + q)), n[full("dve", 5 + q)].next())
                p = psum[:, 5 + q, :].rearrange("p (m t) -> p m t", m=2)
                g = GG3[:, 2 * q:2 * q + 2, :]
                for m in range(2):
                    v.tensor_scalar(g[:, m, :], p[:, m, :], col("gla_b_gate_2", 2 * q + m), None, ALU.add).then_inc(
                        sem("vector_step"), n["vector_step"].up())
                    v.wait_ge(sem("vector_step"), n["vector_step"].now())
                v.scalar_tensor_tensor(out=GTMP3[:, 2 * q:2 * q + 2, :], in0=g, scalar=-1.0, in1=g, op0=ALU.mult,
                                       op1=ALU.max)
                v.tensor_scalar(g, g, -1.0, 0.0, ALU.mult, ALU.max).then_inc(
                    sem(free("dve", 5 + q)), n[free("dve", 5 + q)].up())
                v.wait_ge(sem(free("dve", 5 + q)), n[free("dve", 5 + q)].now())
            v.sem_inc(sem("decay_in"), n["decay_in"].up())
            v.wait_ge(sem("decay_ln"), n["decay_ln"].next())
            v.tensor_tensor(GG3, GG3, GTMP3, ALU.add).then_inc(sem("decay_in"), n["decay_in"].up())
            v.wait_ge(sem("decay_in"), n["decay_in"].now())
            v.wait_ge(sem("ab_ready"), n["ab_ready"].next())

            def dil_stage(i):
                v.tensor_copy(DQ, QA[:, ds(i, 1), :])
                v.tensor_copy(DK, KA[:, ds(i, 1), :])
                v.tensor_copy(DV, VA[:, :, ds(i * P, P)]).then_inc(sem("heads_staged"), n["heads_staged"].up())
                v.wait_ge(sem("heads_staged"), n["heads_staged"].now())

            def dil_mask(i, u, b):
                v.tensor_tensor(psum[:, b, 0:T], psum[:, b, 0:T], MASK[:, u, :], ALU.add).then_inc(
                    sem("vector_step"), n["vector_step"].up())
                v.wait_ge(sem("vector_step"), n["vector_step"].now())

            def dil_weigh(u):
                v.tensor_tensor(DP[u], DP[u], CNT[:, u, :], ALU.mult).then_inc(
                    sem("vector_step"), n["vector_step"].up())
                v.wait_ge(sem("vector_step"), n["vector_step"].now())
                v.tensor_reduce(small[:, 4 + u:5 + u], DP[u], AX_X, ALU.add).then_inc(
                    sem("vector_step"), n["vector_step"].up())
                v.wait_ge(sem("vector_step"), n["vector_step"].now())

            softmax_rounds(HT, 2, dil_stage, dil_mask, dil_weigh, DP, Y, 0, 8, 256)

            def linear_attention(turns, nv, f, q_of, g_of, k_of, v_of, dst, steps):
                per = {n["vector_step"]: steps, n["levels_ready"]: 1, n["head_scores"]: 2}
                for b in (4, 5, 6):
                    for fn in (full, free):
                        per[n[fn("dve", b)]] = 4 if b < 6 else 2
                for b in range(nv):
                    for fn in (full, free):
                        per[n[fn("dve", b)]] = 1
                Dd, Ff, QL, KL = f["D"], f["F"], f["QL"], f["KL"]
                with rounds(v, turns, per) as i:
                    q, k = QL[:, 0, :], KL[:, 0, :]
                    q_of(i, q)
                    k_of(i, k)
                    g_of(i, Dd)
                    v_of(i, f["V"])
                    v.memset(Ff, 1.0).then_inc(sem("vector_step"), n["vector_step"].up())
                    v.wait_ge(sem("vector_step"), n["vector_step"].now())
                    for l in range(1, LEVELS + 1):
                        s = 2 ** (l - 1)
                        v.tensor_tensor(KL[:, l, :], k, Ff, ALU.mult).then_inc(
                            sem("vector_step"), n["vector_step"].up())
                        ins = v.tensor_tensor(QL[:, l, :], q, Dd, ALU.mult)
                        if l == LEVELS:
                            ins.then_inc(sem("levels_ready"), n["levels_ready"].up())
                            v.wait_ge(sem("levels_ready"), n["levels_ready"].now())
                            break
                        ins.then_inc(sem("vector_step"), n["vector_step"].up())
                        v.wait_ge(sem("vector_step"), n["vector_step"].now(-1))
                        dv = Dd.rearrange("p (n w s) -> p n w s", w=2, s=s)
                        fv = Ff.rearrange("p (n w s) -> p n w s", w=2, s=s)
                        shape = [P, 512 // (2 * s), s]
                        v.tensor_tensor(fv[:, :, 0, :], fv[:, :, 0, :], dv[:, :, 1, s - 1:s].broadcast_to(shape),
                                        ALU.mult).then_inc(sem("vector_step"), n["vector_step"].up())
                        v.wait_ge(sem("vector_step"), n["vector_step"].now())
                        v.tensor_tensor(dv[:, :, 1, :], dv[:, :, 1, :], dv[:, :, 0, s - 1:s].broadcast_to(shape),
                                        ALU.mult).then_inc(sem("vector_step"), n["vector_step"].up())
                        v.wait_ge(sem("vector_step"), n["vector_step"].now())
                    for h in range(2):
                        for b in range(2):
                            for half in range(2):
                                v.wait_ge(sem(full("dve", 4 + half)), n[full("dve", 4 + half)].next())
                                v.tensor_tensor(f["A"][:, 4 * half:4 * half + 4, :],
                                                        psum[:, 4 + half, :].rearrange("p (l i) -> p l i", l=4),
                                                        LMASK[:, 4 * half:4 * half + 4, :], ALU.mult).then_inc(
                                    sem(free("dve", 4 + half)), n[free("dve", 4 + half)].up())
                                v.wait_ge(sem(free("dve", 4 + half)), n[free("dve", 4 + half)].now())
                            v.tensor_reduce(f["SC"][:, h, b, :], f["A"].rearrange("p l i -> p i l"), AX_X, ALU.add).then_inc(
                                sem("vector_step"), n["vector_step"].up())
                            v.wait_ge(sem("vector_step"), n["vector_step"].now())
                        v.wait_ge(sem(full("dve", 6)), n[full("dve", 6)].next())
                        v.tensor_copy(f["SC"][:, h, 2, :], psum[:, 6, 0:P]).then_inc(
                            sem(free("dve", 6)), n[free("dve", 6)].up())
                        v.wait_ge(sem(free("dve", 6)), n[free("dve", 6)].now())
                        v.sem_inc(sem("head_scores"), n["head_scores"].up())
                    for b in range(nv):
                        v.wait_ge(sem(full("dve", b)), n[full("dve", b)].next())
                        v.tensor_copy(dst[:, ds(i * (2 * nv) + 2 * b, 2), :],
                                              psum[:, b, :].rearrange("p (m t) -> p m t", m=2)).then_inc(
                            sem(free("dve", b)), n[free("dve", b)].up())
                        v.wait_ge(sem(free("dve", b)), n[free("dve", b)].now())

            def flat(t):
                return t.rearrange("p (a b) -> p a b", a=2)

            v.wait_ge(sem("decay_exp"), n["decay_exp"].next())
            linear_attention(2, 2, GLA,
                             lambda i, o: v.tensor_scalar(flat(o), QB[:, ds(2 * i, 2), :], float(P) ** -0.5, None,
                                                          ALU.mult),
                             lambda i, o: v.tensor_copy(flat(o), GG[:, ds(2 * i, 2), :]),
                             lambda i, o: v.tensor_copy(flat(o), KB[:, ds(2 * i, 2), :]),
                             lambda i, o: v.tensor_copy(o, VB[:, :, ds(i * 512, 512)]),
                             Y[:, HT:KT, :], 34)

            def head_norm(y, heads, each, sq, name):
                v.tensor_tensor(sq, y, y, ALU.mult).then_inc(sem("squares_ready"), n["squares_ready"].up())
                v.wait_ge(sem("squares_ready"), n["squares_ready"].now())
                for h in range(0, heads, 2):
                    b = (h // 2) % 4
                    v.wait_ge(sem(full("dve", b)), n[full("dve", b)].next())
                    v.tensor_scalar(sq[:, h:h + 2, :], psum[:, b, :].rearrange("p (m t) -> p m t", m=2),
                                            1.0 / (each * P), EPS, ALU.mult, ALU.add).then_inc(
                        sem(free("dve", b)), n[free("dve", b)].up())
                    v.wait_ge(sem(free("dve", b)), n[free("dve", b)].now())
                v.sem_inc(sem("norm_var"), n["norm_var"].up())
                v.wait_ge(sem("norm_std"), n["norm_std"].next())
                v.reciprocal(sq[:, 0:heads, :], sq[:, 0:heads, :]).then_inc(sem("vector_step"), n["vector_step"].up())
                v.wait_ge(sem("vector_step"), n["vector_step"].now())
                for h in range(heads):
                    for e in range(each):
                        k = h * each + e
                        ins = v.scalar_tensor_tensor(out=y[:, k, :], in0=y[:, k, :], scalar=col(name, k),
                                                     in1=sq[:, h, :], op0=ALU.mult, op1=ALU.mult)
                ins.then_inc(sem("vector_step"), n["vector_step"].up())
                v.wait_ge(sem("vector_step"), n["vector_step"].now())

            head_norm(Y[:, HT:KT, :], 4, 2, GLA["SQ"], "gla_norm_g_2")
            v.tensor_tensor(Y, Y, GATE2, ALU.mult).then_inc(sem("vector_step"), n["vector_step"].up())
            v.wait_ge(sem("vector_step"), n["vector_step"].now())
            v.sem_inc(sem("y_ready"), n["y_ready"].up())

            def add_in(i, s):
                x = one(X, i * 4 + s)
                v.tensor_tensor(x, psum[:, s, 0:T], x, ALU.add).then_inc(sem(free("dve", s)), n[free("dve", s)].up())
                v.wait_ge(sem(free("dve", s)), n[free("dve", s)].now())
                square(x)

            no_squares()
            evac("ab_out", add_in, steps=8)

            rms_norm(X, H2, 4, lambda k: col("norm_g_2", KT + k), None)
            v.sem_inc(sem("y_used"), n["y_used"].up())
            n["load_s5"].n += 3
            v.wait_ge(sem("load_s5"), n["load_s5"].now())
            v.tensor_copy(S5N[0:32, 2 * P:3 * P].rearrange("p (a b) -> p a b", a=2),
                             over(S5DT[0:32, :], 64, 2)).then_inc(sem("dt_spread"), n["dt_spread"].up())
            v.wait_ge(sem("dt_spread"), n["dt_spread"].now())
            v.wait_ge(sem(full("dve", 4)), n[full("dve", 4)].next())
            v.tensor_copy(s5p[:, 0:3, :], psum[:, 4, 0:96].rearrange("p (a b) -> p a b", a=3)).then_inc(
                sem(free("dve", 4)), n[free("dve", 4)].up())
            v.wait_ge(sem(free("dve", 4)), n[free("dve", 4)].now())
            v.sem_inc(sem("s5_dt"), n["s5_dt"].up())
            v.wait_ge(sem("s5_act"), n["s5_act"].next())
            col5 = lambda k: s5p[:, k, :]
            def TT(o, a, b, op):
                v.tensor_tensor(o, a, b, op).then_inc(sem("vector_step"), n["vector_step"].up())
                v.wait_ge(sem("vector_step"), n["vector_step"].now())

            TT(col5(3), col5(0), col5(2), ALU.mult)
            TT(col5(4), col5(1), col5(2), ALU.mult)
            v.tensor_scalar(col5(10), col5(4), 1.0 / TWO_PI, ROUND, ALU.mult, ALU.add).then_inc(
                sem("vector_step"), n["vector_step"].up())
            v.wait_ge(sem("vector_step"), n["vector_step"].now())
            v.tensor_scalar(col5(10), col5(10), ROUND, None, ALU.subtract).then_inc(
                sem("vector_step"), n["vector_step"].up())
            v.wait_ge(sem("vector_step"), n["vector_step"].now())
            for part in (6.28125, 0.0019350051879882812, 3.019916050561823e-07):
                v.scalar_tensor_tensor(out=col5(4), in0=col5(10), scalar=-part, in1=col5(4), op0=ALU.mult,
                                          op1=ALU.add).then_inc(sem("vector_step"), n["vector_step"].up())
                v.wait_ge(sem("vector_step"), n["vector_step"].now())
            v.tensor_scalar(col5(5), col5(4), 3.1415925, -3.1415925, ALU.min, ALU.max).then_inc(
                sem("vector_step"), n["vector_step"].up())
            v.wait_ge(sem("vector_step"), n["vector_step"].now())
            v.scalar_tensor_tensor(out=col5(4), in0=col5(5), scalar=-1.0, in1=col5(5), op0=ALU.mult, op1=ALU.max).then_inc(
                sem("vector_step"), n["vector_step"].up())
            v.wait_ge(sem("vector_step"), n["vector_step"].now())
            v.tensor_scalar(col5(4), col5(4), -1.0, TWO_PI / 4, ALU.mult, ALU.add).then_inc(
                sem("vector_step"), n["vector_step"].up())
            v.wait_ge(sem("vector_step"), n["vector_step"].now())
            v.sem_inc(sem("s5_dt"), n["s5_dt"].up())
            v.wait_ge(sem("s5_act"), n["s5_act"].next())
            TT(col5(6), col5(3), col5(4), ALU.mult)
            TT(col5(7), col5(3), col5(5), ALU.mult)
            TT(col5(10), col5(0), col5(0), ALU.mult)
            TT(col5(11), col5(1), col5(1), ALU.mult)
            TT(col5(10), col5(10), col5(11), ALU.add)
            v.reciprocal(col5(10), col5(10)).then_inc(sem("vector_step"), n["vector_step"].up())
            v.wait_ge(sem("vector_step"), n["vector_step"].now())
            v.tensor_scalar(col5(11), col5(6), 1.0, None, ALU.subtract).then_inc(
                sem("vector_step"), n["vector_step"].up())
            v.wait_ge(sem("vector_step"), n["vector_step"].now())
            TT(col5(8), col5(11), col5(0), ALU.mult)
            TT(col5(9), col5(7), col5(1), ALU.mult)
            TT(col5(8), col5(8), col5(9), ALU.add)
            TT(col5(8), col5(8), col5(10), ALU.mult)
            TT(col5(11), col5(11), col5(1), ALU.mult)
            TT(col5(9), col5(7), col5(0), ALU.mult)
            TT(col5(9), col5(9), col5(11), ALU.subtract)
            TT(col5(9), col5(9), col5(10), ALU.mult)
            n["load_s5b"].n += 2
            v.wait_ge(sem("load_s5b"), n["load_s5b"].now())
            bb = S5B.rearrange("p (j a h) -> p j a h", a=2, h=16)
            v.memset(S5B, 0.0).then_inc(sem("vector_step"), n["vector_step"].up())
            v.wait_ge(sem("vector_step"), n["vector_step"].now())
            for c in range(2):
                for a in range(2):
                    r = slice(64 * a, 64 * a + 64)
                    o = bb[r, :, a, :]
                    t = S5T[r, :, :]
                    re, im = over(s5p[r, 8, :], 16, 2), over(s5p[r, 9, :], 16, 2)
                    v.tensor_tensor(o, S5BN[r, c, :, :], re, ALU.mult).then_inc(
                        sem("vector_step"), n["vector_step"].up())
                    v.wait_ge(sem("vector_step"), n["vector_step"].now())
                    v.tensor_tensor(t, S5BN[r, 1 - c, :, :], im, ALU.mult).then_inc(
                        sem("vector_step"), n["vector_step"].up())
                    v.wait_ge(sem("vector_step"), n["vector_step"].now())
                    v.tensor_tensor(o, o, t, ALU.subtract if c == 0 else ALU.add).then_inc(
                        sem("vector_step"), n["vector_step"].up())
                    v.wait_ge(sem("vector_step"), n["vector_step"].now())
                v.sem_inc(sem("b_ready"), n["b_ready"].up())
                for q in range(2):
                    v.wait_ge(sem(full("dve", 6 + q)), n[full("dve", 6 + q)].next())
                    v.tensor_copy(BT[:, c, 4 * q:4 * q + 4, :],
                                          psum[:, 6 + q, :].rearrange("p (g s) -> p g s", g=4)).then_inc(
                        sem(free("dve", 6 + q)), n[free("dve", 6 + q)].up())
                    v.wait_ge(sem(free("dve", 6 + q)), n[free("dve", 6 + q)].now())
            v.memset(CMASK, 0.0).then_inc(sem("vector_step"), n["vector_step"].up())
            v.wait_ge(sem("vector_step"), n["vector_step"].now())
            for a in range(2):
                v.memset(CMASK[64 * a:64 * a + 64, :].rearrange("p (n a h) -> p n a h", a=2, h=16)[:, :, a, :], 1.0).then_inc(
                    sem("vector_step"), n["vector_step"].up())
                v.wait_ge(sem("vector_step"), n["vector_step"].now())
            for c in range(2):
                for q in range(2):
                    v.wait_ge(sem(full("dve", 6 + q)), n[full("dve", 6 + q)].next())
                    v.scalar_tensor_tensor(out=CT[:, c, 4 * q:4 * q + 4, :],
                                                   in0=psum[:, 6 + q, :].rearrange("p (g s) -> p g s", g=4),
                                                   scalar=1.0 if c == 0 else -1.0, in1=over(CMASK, 4), op0=ALU.mult,
                                                   op1=ALU.mult).then_inc(
                        sem(free("dve", 6 + q)), n[free("dve", 6 + q)].up())
                    v.wait_ge(sem(free("dve", 6 + q)), n[free("dve", 6 + q)].now())

            def times(o_re, o_im, a_re, a_im, b_re, b_im, t):
                v.tensor_tensor(t, a_im, b_im, ALU.mult).then_inc(sem("vector_step"), n["vector_step"].up())
                v.wait_ge(sem("vector_step"), n["vector_step"].now())
                v.tensor_tensor(o_re, a_re, b_re, ALU.mult).then_inc(sem("vector_step"), n["vector_step"].up())
                v.wait_ge(sem("vector_step"), n["vector_step"].now())
                v.tensor_tensor(o_re, o_re, t, ALU.subtract).then_inc(sem("vector_step"), n["vector_step"].up())
                v.wait_ge(sem("vector_step"), n["vector_step"].now())
                v.tensor_tensor(t, a_im, b_re, ALU.mult).then_inc(sem("vector_step"), n["vector_step"].up())
                v.wait_ge(sem("vector_step"), n["vector_step"].now())
                v.tensor_tensor(o_im, a_re, b_im, ALU.mult).then_inc(sem("vector_step"), n["vector_step"].up())
                v.wait_ge(sem("vector_step"), n["vector_step"].now())
                v.tensor_tensor(o_im, o_im, t, ALU.add).then_inc(sem("vector_step"), n["vector_step"].up())
                v.wait_ge(sem("vector_step"), n["vector_step"].now())

            v.tensor_copy(PW[:, 0, :, 0:1], s5p[:, 6, :].unsqueeze(2)).then_inc(
                sem("vector_step"), n["vector_step"].up())
            v.wait_ge(sem("vector_step"), n["vector_step"].now())
            v.tensor_copy(PW[:, 1, :, 0:1], s5p[:, 7, :].unsqueeze(2)).then_inc(
                sem("vector_step"), n["vector_step"].up())
            v.wait_ge(sem("vector_step"), n["vector_step"].now())
            w = 1
            while w < 16:
                sh = [P, 32, w]
                times(PW[:, 0, :, w:2 * w], PW[:, 1, :, w:2 * w], PW[:, 0, :, 0:w], PW[:, 1, :, 0:w],
                      PW[:, 0, :, w - 1:w].broadcast_to(sh), PW[:, 1, :, w - 1:w].broadcast_to(sh),
                      ST[:, 0:32 * w].rearrange("p (a b) -> p a b", a=32))
                w *= 2
            v.sem_inc(sem("s5_tables"), n["s5_tables"].up())

            def advance(dst, src, a_re, a_im, ta, tb):
                v.tensor_tensor(ta, src, a_re, ALU.mult).then_inc(sem("vector_step"), n["vector_step"].up())
                v.tensor_tensor(tb, src, a_im, ALU.mult).then_inc(sem("vector_step"), n["vector_step"].up())
                v.wait_ge(sem("vector_step"), n["vector_step"].now(-1))
                v.tensor_tensor(dst, dst, ta, ALU.add).then_inc(sem("vector_step"), n["vector_step"].up())
                v.wait_ge(sem("vector_step"), n["vector_step"].now())
                v.tensor_tensor(dst[:, 0], dst[:, 0], tb[:, 1], ALU.subtract).then_inc(
                    sem("vector_step"), n["vector_step"].up())
                v.tensor_tensor(dst[:, 1], dst[:, 1], tb[:, 0], ALU.add).then_inc(
                    sem("vector_step"), n["vector_step"].up())
                v.wait_ge(sem("vector_step"), n["vector_step"].now())

            v.wait_ge(sem("u_ready"), n["u_ready"].next())
            for half in range(2):
                v.wait_ge(sem("inputs_ready"), n["inputs_ready"].next())
                j0 = 16 * half
                xs = SX.rearrange("p c j (m r) -> p c j m r", r=16)
                with rounds(v, 15, {n["vector_step"]: 5}) as r:
                    t = ST.rearrange("p (q c j m) -> p q c j m", q=2, c=2, j=16)
                    sh = [P, 2, 16, 16]
                    run = lambda k: xs[:, :, :, :, ds(k, 1)].rearrange("p c j m r -> p c j (m r)")
                    advance(run(r + 1), run(r), PW[:, 0, j0:j0 + 16, 0:1].unsqueeze(1).broadcast_to(sh),
                            PW[:, 1, j0:j0 + 16, 0:1].unsqueeze(1).broadcast_to(sh), t[:, 0], t[:, 1])
                with rounds(v, 15, {n["vector_step"]: 5}) as m:
                    t = ST[:, 0:64].rearrange("p (q c j) -> p q c j", q=2, c=2)
                    last = xs[:, :, :, :, 15:16].rearrange("p c j m r -> p c j (m r)")
                    end = lambda k: last[:, :, :, ds(k, 1)].rearrange("p c j m -> p c (j m)")
                    advance(end(m + 1), end(m), over(PW[:, 0, j0:j0 + 16, 15], 2), over(PW[:, 1, j0:j0 + 16, 15], 2),
                            t[:, 0], t[:, 1])
                with rounds(v, 16, {n["vector_step"]: 5}) as j:
                    t = ST[:, 0:900].rearrange("p (q c m r) -> p q c m r", q=2, c=2, m=15)
                    sh = [P, 2, 15, 15]
                    sx = lambda m0, r0, r1: xs[:, :, ds(j, 1), m0:m0 + 15, r0:r1].rearrange("p c j m r -> p c (j m) r")
                    pw = lambda c: PW[:, c, ds(j + j0, 1), 0:15].unsqueeze(1).broadcast_to(sh)
                    advance(sx(1, 0, 15), sx(0, 15, 16).broadcast_to(sh), pw(0), pw(1), t[:, 0], t[:, 1])
                v.sem_inc(sem("states_ready"), n["states_ready"].up())
                for q in range(4):
                    ut = 4 * half + q
                    v.wait_ge(sem(full("dve", 4 + q % 2)), n[full("dve", 4 + q % 2)].next())
                    v.scalar_tensor_tensor(out=Y5[:, ut, :], in0=SU5[:, ut, :], scalar=col("s5_d_2", ut),
                                                   in1=psum[:, 4 + q % 2, 0:T], op0=ALU.mult, op1=ALU.add).then_inc(
                        sem(free("dve", 4 + q % 2)), n[free("dve", 4 + q % 2)].up())
                    v.wait_ge(sem(free("dve", 4 + q % 2)), n[free("dve", 4 + q % 2)].now())
            v.sem_inc(sem("s5_sum"), n["s5_sum"].up())
            v.wait_ge(sem("s5_gelu"), n["s5_gelu"].next())
            v.wait_ge(sem("cd_ready"), n["cd_ready"].next())
            v.sem_inc(sem("glu_in"), n["glu_in"].up())
            g0, g1 = col("hgrn_gamma_2", 0, HT), col("hgrn_gamma_2", HT, HT)
            v.tensor_tensor(s5p[:, 0, 0:HT], g0, g1, ALU.max).then_inc(sem("vector_step"), n["vector_step"].up())
            v.wait_ge(sem("vector_step"), n["vector_step"].now())
            v.tensor_tensor(small[:, 0:HT], g0, s5p[:, 0, 0:HT], ALU.subtract).then_inc(
                sem("vector_step"), n["vector_step"].up())
            v.wait_ge(sem("vector_step"), n["vector_step"].now())
            v.tensor_tensor(small[:, HT:16], g1, s5p[:, 0, 0:HT], ALU.subtract).then_inc(
                sem("gamma_in"), n["gamma_in"].up())
            v.wait_ge(sem("gamma_in"), n["gamma_in"].now())
            v.wait_ge(sem("gamma_exp"), n["gamma_exp"].next())
            v.tensor_tensor(s5p[:, 0, 0:HT], small[:, 0:HT], small[:, HT:16], ALU.add).then_inc(
                sem("vector_step"), n["vector_step"].up())
            v.wait_ge(sem("vector_step"), n["vector_step"].now())
            v.reciprocal(s5p[:, 0, 0:HT], s5p[:, 0, 0:HT]).then_inc(sem("vector_step"), n["vector_step"].up())
            v.wait_ge(sem("vector_step"), n["vector_step"].now())
            v.tensor_tensor(s5p[:, 1, 0:16].rearrange("p (a b) -> p a b", a=2),
                               small[:, 0:16].rearrange("p (a b) -> p a b", a=2), over(s5p[:, 0, 0:HT], 2), ALU.mult).then_inc(
                sem("vector_step"), n["vector_step"].up())
            v.wait_ge(sem("vector_step"), n["vector_step"].now())
            v.tensor_tensor(s5p[:, 2, 0:HT], s5p[:, 1, 0:HT], s5p[:, 1, HT:16], ALU.add).then_inc(
                sem("vector_step"), n["vector_step"].up())
            v.wait_ge(sem("vector_step"), n["vector_step"].now())
            v.tensor_tensor(s5p[:, 2, 0:HT], s5p[:, 2, 0:HT], s5p[:, 1, 0:HT], ALU.subtract).then_inc(
                sem("vector_step"), n["vector_step"].up())
            v.wait_ge(sem("vector_step"), n["vector_step"].now())
            v.tensor_scalar(s5p[:, 3, 0:HT], s5p[:, 2, 0:HT], -1.0, 1.0, ALU.mult, ALU.add).then_inc(
                sem("vector_step"), n["vector_step"].up())
            v.wait_ge(sem("vector_step"), n["vector_step"].now())
            for k in range(HT):
                ins = v.tensor_scalar(FD[:, k, :], FD[:, k, :], s5p[:, 3, k:k + 1], s5p[:, 2, k:k + 1], ALU.mult,
                                      ALU.add)
            ins.then_inc(sem("vector_step"), n["vector_step"].up())
            v.wait_ge(sem("vector_step"), n["vector_step"].now())
            v.wait_ge(sem("glu_ready"), n["glu_ready"].next())
            v.tensor_tensor(Y5, Y5, SIG, ALU.mult).then_inc(sem("vector_step"), n["vector_step"].up())
            v.wait_ge(sem("vector_step"), n["vector_step"].now())
            linear_attention(4, 1, HG,
                             lambda i, o: v.tensor_copy(flat(o), QD[:, ds(2 * i, 2), :]),
                             lambda i, o: v.tensor_copy(flat(o), FD[:, ds(2 * i, 2), :]),
                             lambda i, o: v.tensor_scalar(flat(o), FD[:, ds(2 * i, 2), :], -1.0, 1.0, ALU.mult, ALU.add),
                             lambda i, o: v.tensor_copy(o, ID[:, :, ds(i * 256, 256)]),
                             YD, 34)
            head_norm(YD, 8, 1, HG["SQ"], "hgrn_norm_g_2")
            v.tensor_tensor(Y5P[:, 0:HT, :], Y5, GATE3[:, 0:HT, :], ALU.mult).then_inc(
                sem("vector_step"), n["vector_step"].up())
            v.wait_ge(sem("vector_step"), n["vector_step"].now())
            v.tensor_tensor(Y5P[:, HT:KT, :], YD, GATE3[:, HT:KT, :], ALU.mult).then_inc(
                sem("y_ready"), n["y_ready"].up())
            v.wait_ge(sem("y_ready"), n["y_ready"].now())
            no_squares()
            evac("cd_out", add_in, steps=8)
            rms_norm(X, FIN, 4, lambda k: col("final_g_2", k), None)
            v.sem_inc(sem("y_used"), n["y_used"].up())


NAMES = ("x", "c", "ctx", "c_ctx", "w_mod", "b_mod", "norm1_g", "norm2_g", "w_in", "b_in", "conv_w", "conv_b",
         "conv_ln_g", "conv_ln_b", "w_conv_out", "sgu_ln_g", "sgu_ln_b", "sgu_w", "sgu_b", "w_sgu_out", "na_rpb",
         "w_na_out", "w_o", "b_o", "w_ff1", "b_ff1", "w_ff2", "b_ff2", "final_g", "norm_g_2", "final_g_2", "ab_w_in_2",
         "gla_w_gate_2", "gla_b_gate_2", "gla_norm_g_2", "ab_w_out_2", "cd_w_in_2", "s5_lam_re_2", "s5_lam_im_2",
         "s5_log_dt_2", "s5_b_re_2", "s5_b_im_2", "s5_c_re_2", "s5_c_im_2", "s5_d_2", "s5_w_glu_2", "s5_b_glu_2",
         "hgrn_gamma_2", "hgrn_norm_g_2", "cd_w_out_2")
FLAT = ("norm_g_2", "hgrn_gamma_2", "s5_d_2")


def layout(inputs):
    arrays = {}
    for name in NAMES:
        a = np.ascontiguousarray(inputs[name])
        if a.ndim > 1 and a.shape[0] == 1:
            a = a.reshape(a.shape[1:])
        if name in FLAT:
            a = a.reshape(-1)
        arrays[name] = a
    return arrays


def kernel(**inputs):
    import concourse.bacc as bacc
    from concourse.bass_utils import run_bass_kernel_spmd

    nc = bacc.Bacc("TRN2", target_bir_lowering=False, num_devices=1)
    arrays = layout(inputs)
    dram = {n: nc.dram_tensor(n, a.shape, F32, kind="ExternalInput").ap() for n, a in arrays.items()}
    out = nc.dram_tensor("out", (T, D), F32, kind="ExternalOutput").ap()
    program(nc, dram, out)
    r = run_bass_kernel_spmd(nc, [arrays], core_ids=[0])
    return r.results[0]["out"].reshape(1, T, D)
```
